# Optimizing a Trainium2 kernel written in Bass

```python
import math
import jax, jax.numpy as jnp
from jax import lax
import numpy as np

D_MODEL = 1024
BATCH = 1
SEQ = 256
DEPTH = 1

HG_HEADS = 4
HG_KDIM = 128
HG_VDIM = 128
HG_F = HG_HEADS * HG_KDIM
HG_V = HG_HEADS * HG_VDIM
HG_CHUNK = 64
MLA_HEADS = 8
MLA_NOPE = 64
MLA_ROPE = 32
MLA_VDIM = 64
MLA_QK = MLA_NOPE + MLA_ROPE
MLA_Q_RANK = 256
MLA_KV_RANK = 128
ATTN_BLOCK = 128
ROPE_THETA = 10000.0
N_GROUPS = 8
EXPERTS_PER_GROUP = 8
N_EXPERTS = N_GROUPS * EXPERTS_PER_GROUP
TOP_K = 2
D_EXPERT = 256
MOE_BLOCK = 128
PLE_DIM = 256
EPS = 1e-6
IN_WIDTHS = (HG_F, HG_F, HG_F, HG_V, HG_V, MLA_Q_RANK, MLA_KV_RANK, MLA_ROPE, D_MODEL, D_MODEL)
D_IN = HG_F * 3 + HG_V * 2 + MLA_Q_RANK + MLA_KV_RANK + MLA_ROPE + 2 * D_MODEL


def rmsnorm(x, g):
    xf = x.astype(jnp.float32)
    y = xf * lax.rsqrt(jnp.mean(xf * xf, axis=-1, keepdims=True) + EPS)
    return (y * g.astype(jnp.float32)).astype(x.dtype)

def rope(x, positions):
    half = MLA_ROPE // 2
    inv_freq = ROPE_THETA ** (-jnp.arange(half, dtype=jnp.float32) / half)
    ang = positions.astype(jnp.float32)[..., None] * inv_freq
    cos = jnp.cos(ang)[:, :, None, :]
    sin = jnp.sin(ang)[:, :, None, :]
    x1 = x[..., :half].astype(jnp.float32)
    x2 = x[..., half:].astype(jnp.float32)
    out = jnp.concatenate([x1 * cos - x2 * sin, x2 * cos + x1 * sin], axis=-1)
    return out.astype(x.dtype)

def gla_chunkwise(q, k, v, log_f):
    B, H, S, K = q.shape
    V = v.shape[-1]
    n = S // HG_CHUNK

    def to_chunks(a):
        return jnp.moveaxis(a.reshape(B, H, n, HG_CHUNK, a.shape[-1]), 2, 0)

    qc, kc, vc, gc = to_chunks(q), to_chunks(k), to_chunks(v), to_chunks(log_f)
    lower = jnp.tril(jnp.ones((HG_CHUNK, HG_CHUNK), dtype=bool))

    def step(state, inp):
        qb, kb, vb, gb = inp
        g = jnp.cumsum(gb, axis=2)
        o_inter = jnp.einsum('bhtk,bhkv->bhtv', qb * jnp.exp(g), state)
        diff = g[:, :, :, None, :] - g[:, :, None, :, :]
        decay = jnp.exp(jnp.where(lower[:, :, None], diff, -jnp.inf))
        scores = jnp.einsum('bhtk,bhsk,bhtsk->bhts', qb, kb, decay)
        o_intra = jnp.einsum('bhts,bhsv->bhtv', scores, vb)
        g_last = g[:, :, -1]
        k_dec = kb * jnp.exp(g_last[:, :, None, :] - g)
        new_state = jnp.exp(g_last)[..., None] * state + jnp.einsum('bhck,bhcv->bhkv', k_dec, vb)
        return new_state, o_inter + o_intra

    s0 = jnp.zeros((B, H, K, V), jnp.float32)
    _, o = lax.scan(step, s0, (qc, kc, vc, gc))
    return jnp.moveaxis(o, 0, 2).reshape(B, H, S, V)

def block_dense_attention(q, k, v):
    B, H, S, Dq = q.shape
    nb = S // ATTN_BLOCK
    qb = jnp.moveaxis(q.reshape(B, H, nb, ATTN_BLOCK, Dq), 2, 0)
    scale = MLA_QK ** -0.5

    def one_block(qblk):
        s = jnp.einsum('bhqd,bhkd->bhqk', qblk, k).astype(jnp.float32) * scale
        pr = jax.nn.softmax(s, axis=-1).astype(v.dtype)
        return jnp.einsum('bhqk,bhkd->bhqd', pr, v)

    o = lax.map(one_block, qb)
    return jnp.moveaxis(o, 0, 2).reshape(B, H, S, v.shape[-1])

def hierarchical_moe(h, w_rg, b_rg, w_re, b_re, w1, w3, w2):
    T, D = h.shape
    g_logits = (h @ w_rg).astype(jnp.float32) + b_rg.astype(jnp.float32)
    g_prob = jax.nn.softmax(g_logits, axis=-1)
    g_sel = jnp.argmax(g_prob, axis=-1).astype(jnp.int32)
    p_group = jnp.max(g_prob, axis=-1)
    e_logits = ((h @ w_re).astype(jnp.float32) + b_re.astype(jnp.float32)).reshape(T, N_GROUPS, EXPERTS_PER_GROUP)
    e_in_group = jnp.take_along_axis(e_logits, g_sel[:, None, None], axis=1)[:, 0]
    top_v, top_i = lax.top_k(e_in_group, TOP_K)
    w_local = jax.nn.softmax(top_v, axis=-1)
    expert = (g_sel[:, None] * EXPERTS_PER_GROUP + top_i.astype(jnp.int32)).reshape(-1)
    weight = (p_group[:, None] * w_local).reshape(-1)
    token = jnp.repeat(jnp.arange(T, dtype=jnp.int32), TOP_K)
    A = T * TOP_K

    counts = jnp.zeros((N_EXPERTS,), jnp.int32).at[expert].add(1)
    starts = jnp.cumsum(counts) - counts
    pcounts = (counts + MOE_BLOCK - 1) // MOE_BLOCK * MOE_BLOCK
    pends = jnp.cumsum(pcounts)
    pstarts = pends - pcounts
    order = jnp.argsort(expert)
    e_sorted = expert[order]
    rank = jnp.arange(A, dtype=jnp.int32) - starts[e_sorted]
    dest = pstarts[e_sorted] + rank
    n_blocks = (A + N_EXPERTS * (MOE_BLOCK - 1) + MOE_BLOCK - 1) // MOE_BLOCK
    P = n_blocks * MOE_BLOCK
    buf_tok = jnp.full((P,), T, jnp.int32).at[dest].set(token[order])
    buf_w = jnp.zeros((P,), h.dtype).at[dest].set(weight[order].astype(h.dtype))
    block_expert = jnp.minimum(
        jnp.searchsorted(pends, jnp.arange(n_blocks, dtype=jnp.int32) * MOE_BLOCK, side='right'),
        N_EXPERTS - 1)
    h_pad = jnp.concatenate([h, jnp.zeros((1, D), h.dtype)], axis=0)
    xb = h_pad[buf_tok].reshape(n_blocks, MOE_BLOCK, D)

    def expert_block(args):
        xblk, e = args
        return (jax.nn.silu(xblk @ w1[e]) * (xblk @ w3[e])) @ w2[e]

    yb = lax.map(expert_block, (xb, block_expert)).reshape(P, D)
    out = jax.ops.segment_sum(yb * buf_w[:, None], buf_tok, num_segments=T + 1)
    return out[:T]

def first_inputs(seed: int = 0) -> dict:
    key = jax.random.key(seed)
    ks = jax.random.split(key, 32)
    f32 = jnp.float32

    def w(k, shape, fan_in):
        return jax.random.normal(k, shape, f32) * (fan_in ** -0.5)

    def gain(k, shape):
        return 1.0 + 0.1 * jax.random.normal(k, shape, f32)

    L = DEPTH
    offsets = jax.random.randint(ks[2], (BATCH, 1), 0, SEQ, dtype=jnp.int32)
    positions = jnp.arange(SEQ, dtype=jnp.int32)[None, :] + offsets
    return {
        "x": jax.random.normal(ks[0], (BATCH, SEQ, D_MODEL), f32),
        "p": jax.random.normal(ks[1], (DEPTH, BATCH, SEQ, PLE_DIM), f32),
        "positions": positions,
        "ln_mix": gain(ks[3], (L, D_MODEL)),
        "w_in": w(ks[4], (L, D_MODEL, D_IN), D_MODEL),
        "hg_lb": 0.5 * jax.random.normal(ks[5], (2, DEPTH + 1, HG_F), f32),
        "hg_onorm": gain(ks[6], (L, HG_VDIM)),
        "w_oA": w(ks[7], (L, HG_V, D_MODEL), HG_V),
        "mla_qa_norm": gain(ks[8], (L, MLA_Q_RANK)),
        "mla_kva_norm": gain(ks[9], (L, MLA_KV_RANK)),
        "w_uq": w(ks[10], (L, MLA_Q_RANK, MLA_HEADS * MLA_QK), MLA_Q_RANK),
        "w_ukv": w(ks[11], (L, MLA_KV_RANK, MLA_HEADS * (MLA_NOPE + MLA_VDIM)), MLA_KV_RANK),
        "q_norm": gain(ks[12], (L, MLA_QK)),
        "k_norm": gain(ks[13], (L, MLA_QK)),
        "w_oB": w(ks[14], (L, MLA_HEADS * MLA_VDIM, D_MODEL), MLA_HEADS * MLA_VDIM),
        "w_out": w(ks[15], (L, D_MODEL, D_MODEL), D_MODEL),
        "ln_moe": gain(ks[16], (L, D_MODEL)),
        "w_rg": w(ks[17], (L, D_MODEL, N_GROUPS), D_MODEL),
        "b_rg": 0.01 * jax.random.normal(ks[18], (L, N_GROUPS), f32),
        "w_re": w(ks[19], (L, D_MODEL, N_EXPERTS), D_MODEL),
        "b_re": 0.01 * jax.random.normal(ks[20], (L, N_EXPERTS), f32),
        "w1": w(ks[21], (L, N_EXPERTS, D_MODEL, D_EXPERT), D_MODEL),
        "w3": w(ks[22], (L, N_EXPERTS, D_MODEL, D_EXPERT), D_MODEL),
        "w2": w(ks[23], (L, N_EXPERTS, D_EXPERT, D_MODEL), D_EXPERT),
        "ln_ple": gain(ks[24], (L, D_MODEL)),
        "w_ple_gate": w(ks[25], (L, D_MODEL, D_MODEL), D_MODEL),
        "w_ple_proj": w(ks[26], (L, PLE_DIM, D_MODEL), PLE_DIM),
    }

def first_block(x, p, positions, ln_mix, w_in, hg_lb, hg_onorm, w_oA,
              mla_qa_norm, mla_kva_norm, w_uq, w_ukv, q_norm, k_norm, w_oB,
              w_out, ln_moe, w_rg, b_rg, w_re, b_re, w1, w3, w2,
              ln_ple, w_ple_gate, w_ple_proj):
    B, S, D = x.shape
    f32 = jnp.float32
    split_points = [int(v) for v in np.cumsum(IN_WIDTHS)[:-1]]
    lb_all = jnp.cumsum(jax.nn.softmax(hg_lb.astype(f32), axis=1), axis=1)

    def heads(a, hd):
        return a.reshape(B, S, -1, hd).transpose(0, 2, 1, 3)

    for layer in range(DEPTH):
        h = rmsnorm(x, ln_mix[layer])
        z = h @ w_in[layer]
        q_a, f_fw, f_bw, i_a, og_a, c_q, c_kv, k_rope, gate_a, gate_b = jnp.split(z, split_points, axis=-1)

        qh = heads(jax.nn.silu(q_a.astype(f32)), HG_KDIM)
        vh = heads(i_a.astype(f32), HG_VDIM)

        def hgrn_direction(f_logit, lb, reverse):
            f = lb + (1.0 - lb) * jax.nn.sigmoid(f_logit.astype(f32))
            log_f = heads(jnp.log(f), HG_KDIM)
            kh = heads(1.0 - f, HG_KDIM)
            if reverse:
                o = gla_chunkwise(jnp.flip(qh, 2), jnp.flip(kh, 2), jnp.flip(vh, 2), jnp.flip(log_f, 2))
                return jnp.flip(o, 2)
            return gla_chunkwise(qh, kh, vh, log_f)

        o_hg = hgrn_direction(f_fw, lb_all[0, layer], False) + hgrn_direction(f_bw, lb_all[1, layer], True)
        o_hg = o_hg.transpose(0, 2, 1, 3)
        o_hg = rmsnorm(o_hg, hg_onorm[layer]) * jax.nn.silu(og_a.astype(f32).reshape(B, S, HG_HEADS, HG_VDIM))
        y_a = o_hg.reshape(B, S, HG_V).astype(x.dtype) @ w_oA[layer]

        cq = rmsnorm(c_q, mla_qa_norm[layer])
        qm = (cq @ w_uq[layer]).reshape(B, S, MLA_HEADS, MLA_QK)
        ckv = rmsnorm(c_kv, mla_kva_norm[layer])
        kv = (ckv @ w_ukv[layer]).reshape(B, S, MLA_HEADS, MLA_NOPE + MLA_VDIM)
        k_nope, vm = kv[..., :MLA_NOPE], kv[..., MLA_NOPE:]
        km = jnp.concatenate(
            [k_nope, jnp.broadcast_to(k_rope[:, :, None, :], (B, S, MLA_HEADS, MLA_ROPE))], axis=-1)
        qm = rmsnorm(qm, q_norm[layer])
        km = rmsnorm(km, k_norm[layer])
        qm = jnp.concatenate([qm[..., :MLA_NOPE], rope(qm[..., MLA_NOPE:], positions)], axis=-1)
        km = jnp.concatenate([km[..., :MLA_NOPE], rope(km[..., MLA_NOPE:], positions)], axis=-1)
        o_mla = block_dense_attention(qm.transpose(0, 2, 1, 3), km.transpose(0, 2, 1, 3), vm.transpose(0, 2, 1, 3))
        y_b = o_mla.transpose(0, 2, 1, 3).reshape(B, S, MLA_HEADS * MLA_VDIM) @ w_oB[layer]

        merged = jax.nn.sigmoid(gate_a) * y_a + jax.nn.sigmoid(gate_b) * y_b
        x = x + merged @ w_out[layer]

        hm = rmsnorm(x, ln_moe[layer]).reshape(B * S, D)
        x = x + hierarchical_moe(hm, w_rg[layer], b_rg[layer], w_re[layer], b_re[layer],
                                 w1[layer], w3[layer], w2[layer]).reshape(B, S, D)

        ple_gate = jax.nn.sigmoid(rmsnorm(x, ln_ple[layer]) @ w_ple_gate[layer])
        x = x + (p[layer] @ w_ple_proj[layer]) * ple_gate
    return x


GRID_W = 64
CTX_LEN = 256
CONV_W = 1024
CONV_K = 3
N_HEADS = 16
HEAD_DIM = 64
ATTN_W = N_HEADS * HEAD_DIM
WIN_ROWS_MAX = 8
WIN_COLS = 16
ROPE_BASE = 10000.0
N_BRANCH = 2
IN_SIZES = [CONV_W] * 4 + [ATTN_W] * 4 + [D_MODEL] * N_BRANCH
IN_COLS = sum(IN_SIZES)
K_OFF = 4 * CONV_W + ATTN_W
V_END = 4 * CONV_W + 3 * ATTN_W


def _rmsnorm(u, g):
    u32 = u.astype(jnp.float32)
    return (u32 * lax.rsqrt(jnp.mean(u32 * u32, axis=-1, keepdims=True) + EPS)).astype(u.dtype) * g

def _modulation(cond, w_mod, b_mod):
    m = jax.nn.silu(cond) @ w_mod + b_mod
    return jnp.split(m, 3, axis=-1)

def _split_in(p):
    idx = np.cumsum(IN_SIZES)[:-1].tolist()
    return jnp.split(p, idx, axis=-1)

def _dwconv3(u, w, b):
    L = u.shape[1]
    up = jnp.pad(u, ((0, 0), (1, 1), (0, 0)))
    return up[:, :L] * w[0] + up[:, 1:L + 1] * w[1] + up[:, 2:] * w[2] + b

def _rope_2d_tables(L, dtype):
    t = jnp.arange(L, dtype=jnp.int32)
    row = (t // GRID_W).astype(jnp.float32)
    col = (t % GRID_W).astype(jnp.float32)
    half = HEAD_DIM // 2
    inv = ROPE_BASE ** (-jnp.arange(0, half, 2, dtype=jnp.float32) / half)
    ang_r = row[:, None] * inv
    ang_c = col[:, None] * inv
    ang = jnp.concatenate([ang_r, ang_r, ang_c, ang_c], axis=-1)
    return jnp.cos(ang).astype(dtype), jnp.sin(ang).astype(dtype)

def _rot_half_axial(u):
    u1, u2, u3, u4 = jnp.split(u, 4, axis=-1)
    return jnp.concatenate([-u2, u1, -u4, u3], axis=-1)

def _apply_rope(u, cos, sin):
    return u * cos[None, :, None, :] + _rot_half_axial(u) * sin[None, :, None, :]

def _heads(u):
    return u.reshape(u.shape[0], u.shape[1], N_HEADS, HEAD_DIM)

def _neighbourhood_attention(q, k, v, k_ctx, v_ctx, rpb):
    bsz, L, H, Dh = q.shape
    rows = L // GRID_W
    wr = min(WIN_ROWS_MAX, rows)
    n_nb = wr * WIN_COLS
    scale = HEAD_DIM ** -0.5
    qg = q.reshape(bsz, rows, GRID_W, H, Dh)
    kg = k.reshape(bsz, rows, GRID_W, H, Dh)
    vg = v.reshape(bsz, rows, GRID_W, H, Dh)
    col = jnp.arange(GRID_W, dtype=jnp.int32)
    col_start = jnp.clip(col - WIN_COLS // 2, 0, GRID_W - WIN_COLS)
    col_idx = col_start[:, None] + jnp.arange(WIN_COLS, dtype=jnp.int32)
    dc_idx = col_idx - col[:, None] + (WIN_COLS - 1)

    def row_block(r):
        rs = jnp.clip(r - wr // 2, 0, rows - wr)
        q_r = lax.dynamic_index_in_dim(qg, r, axis=1, keepdims=False)
        k_slab = lax.dynamic_slice_in_dim(kg, rs, wr, axis=1)
        v_slab = lax.dynamic_slice_in_dim(vg, rs, wr, axis=1)
        k_win = k_slab[:, :, col_idx]
        v_win = v_slab[:, :, col_idx]
        dr_idx = rs + jnp.arange(wr, dtype=jnp.int32) - r + (WIN_ROWS_MAX - 1)
        bias = rpb[:, dr_idx[None, :, None], dc_idx[:, None, :]]
        s_nb = (jnp.einsum('bqhd,bpqjhd->bqhpj', q_r, k_win).astype(jnp.float32) * scale
                + jnp.transpose(bias, (1, 0, 2, 3))[None].astype(jnp.float32))
        s_nb = s_nb.reshape(bsz, GRID_W, H, n_nb)
        s_ctx = jnp.einsum('bqhd,bchd->bqhc', q_r, k_ctx).astype(jnp.float32) * scale
        p = jax.nn.softmax(jnp.concatenate([s_nb, s_ctx], axis=-1), axis=-1).astype(v.dtype)
        p_nb = p[..., :n_nb].reshape(bsz, GRID_W, H, wr, WIN_COLS)
        p_ctx = p[..., n_nb:]
        return (jnp.einsum('bqhpj,bpqjhd->bqhd', p_nb, v_win)
                + jnp.einsum('bqhc,bchd->bqhd', p_ctx, v_ctx))

    out = lax.map(row_block, jnp.arange(rows, dtype=jnp.int32))
    return jnp.transpose(out, (1, 0, 2, 3, 4)).reshape(bsz, L, H * Dh)

def _ctx_attention(q, k, v):
    scale = HEAD_DIM ** -0.5
    s = jnp.einsum('bqhd,bkhd->bhqk', q, k).astype(jnp.float32) * scale
    p = jax.nn.softmax(s, axis=-1).astype(v.dtype)
    o = jnp.einsum('bhqk,bkhd->bqhd', p, v)
    return o.reshape(o.shape[0], o.shape[1], ATTN_W)

def _mixer_out(parts, attn_o, conv_w, conv_b, w_out_conv, w_out_attn, w_o):
    b_gate, c_gate, x_in, z_a, _, _, _, z_b, g_a, g_b = parts
    y_a = (jax.nn.silu(z_a) * b_gate * _dwconv3(c_gate * x_in, conv_w, conv_b)) @ w_out_conv
    y_b = (jax.nn.silu(z_b) * attn_o) @ w_out_attn
    merged = jax.nn.sigmoid(g_a) * y_a + jax.nn.sigmoid(g_b) * y_b
    return merged @ w_o

def second_inputs(seed: int = 0) -> dict:
    key = jax.random.key(seed)
    ks = jax.random.split(key, 16)
    f32 = jnp.float32
    nrm = lambda k, shape, s: jax.random.normal(k, shape, f32) * s
    return {
        "x": nrm(ks[0], (BATCH, SEQ, D_MODEL), 1.0),
        "c": nrm(ks[1], (BATCH, D_MODEL), 1.0),
        "ctx": nrm(ks[2], (BATCH, CTX_LEN, D_MODEL), 1.0),
        "c_ctx": nrm(ks[3], (D_MODEL,), 1.0),
        "w_mod": nrm(ks[4], (DEPTH, D_MODEL, 3 * D_MODEL), D_MODEL ** -0.5),
        "b_mod": nrm(ks[5], (DEPTH, 3 * D_MODEL), 0.02),
        "pre_g": 1.0 + nrm(ks[6], (DEPTH, D_MODEL), 0.05),
        "post_g": 1.0 + nrm(ks[7], (DEPTH, D_MODEL), 0.05),
        "w_in": nrm(ks[8], (DEPTH, D_MODEL, IN_COLS), D_MODEL ** -0.5),
        "conv_w": nrm(ks[9], (DEPTH, CONV_K, CONV_W), CONV_K ** -0.5),
        "conv_b": nrm(ks[10], (DEPTH, CONV_W), 0.02),
        "rpb": nrm(ks[11], (DEPTH, N_HEADS, 2 * WIN_ROWS_MAX - 1, 2 * WIN_COLS - 1), 0.1),
        "w_out_conv": nrm(ks[12], (DEPTH, CONV_W, D_MODEL), CONV_W ** -0.5),
        "w_out_attn": nrm(ks[13], (DEPTH, ATTN_W, D_MODEL), ATTN_W ** -0.5),
        "w_o": nrm(ks[14], (DEPTH, D_MODEL, D_MODEL), D_MODEL ** -0.5),
    }

def second_block(x, c, ctx, c_ctx, w_mod, b_mod, pre_g, post_g, w_in, conv_w, conv_b, rpb,
              w_out_conv, w_out_attn, w_o):
    L = x.shape[1]
    cos, sin = _rope_2d_tables(L, x.dtype)
    for i in range(DEPTH):
        last = i == DEPTH - 1
        sh, sc, gt = _modulation(c, w_mod[i], b_mod[i])
        sh_c, sc_c, gt_c = _modulation(c_ctx, w_mod[i], b_mod[i])
        h = _rmsnorm(x, pre_g[i]) * (1.0 + sc[:, None, :]) + sh[:, None, :]
        hc = _rmsnorm(ctx, pre_g[i]) * (1.0 + sc_c) + sh_c
        parts = _split_in(h @ w_in[i])
        q = _apply_rope(_heads(parts[4]), cos, sin)
        k = _apply_rope(_heads(parts[5]), cos, sin)
        v = _heads(parts[6])
        if last:
            kv_c = hc @ w_in[i][:, K_OFF:V_END]
            k_c, v_c = jnp.split(kv_c, 2, axis=-1)
            k_c, v_c = _heads(k_c), _heads(v_c)
        else:
            parts_c = _split_in(hc @ w_in[i])
            k_c, v_c = _heads(parts_c[5]), _heads(parts_c[6])
        attn = _neighbourhood_attention(q, k, v, k_c, v_c, rpb[i])
        y = _mixer_out(parts, attn, conv_w[i], conv_b[i], w_out_conv[i], w_out_attn[i], w_o[i])
        if not last:
            attn_c = _ctx_attention(_heads(parts_c[4]), k_c, v_c)
            y_c = _mixer_out(parts_c, attn_c, conv_w[i], conv_b[i], w_out_conv[i], w_out_attn[i], w_o[i])
            ctx = ctx + gt_c * _rmsnorm(y_c, post_g[i])
        x = x + gt[:, None, :] * _rmsnorm(y, post_g[i])
    return x


def setup_inputs(seed=0):
    out = dict(first_inputs(seed))
    for name, value in second_inputs(seed + 1).items():
        if name != "x":
            out[name + "_2"] = value
    return out


def reference(
    x, p, positions, ln_mix, w_in, hg_lb, hg_onorm, w_oA, mla_qa_norm, mla_kva_norm, w_uq,
    w_ukv, q_norm, k_norm, w_oB, w_out, ln_moe, w_rg, b_rg, w_re, b_re, w1, w3, w2, ln_ple,
    w_ple_gate, w_ple_proj, c_2, ctx_2, c_ctx_2, w_mod_2, b_mod_2, pre_g_2, post_g_2, w_in_2,
    conv_w_2, conv_b_2, rpb_2, w_out_conv_2, w_out_attn_2, w_o_2,
):
    x = first_block(
        x, p, positions, ln_mix, w_in, hg_lb, hg_onorm, w_oA, mla_qa_norm, mla_kva_norm, w_uq,
        w_ukv, q_norm, k_norm, w_oB, w_out, ln_moe, w_rg, b_rg, w_re, b_re, w1, w3, w2, ln_ple,
        w_ple_gate, w_ple_proj,
    )
    return second_block(
        x, c_2, ctx_2, c_ctx_2, w_mod_2, b_mod_2, pre_g_2, post_g_2, w_in_2, conv_w_2, conv_b_2,
        rpb_2, w_out_conv_2, w_out_attn_2, w_o_2,
    )


_drawn_inputs = setup_inputs


def setup_inputs(seed=0):
    import zlib

    import numpy as np

    out = dict(_drawn_inputs(seed))
    spreads = {}
    factors = {'mla_qa_norm': 3.095,
     'mla_kva_norm': 3.132,
     'q_norm': 4.651,
     'k_norm': 4.314,
     'b_rg': 13.382,
     'b_re': 24.449,
     'conv_b_2': 8.0,
     'rpb_2': 31.596,
     'hg_lb': 3.985,
     'ln_ple': 4.85,
     'b_mod_2': 3.412,
     'post_g_2': 3.894}
    for name, (base, spread) in spreads.items():
        noise = np.random.default_rng([zlib.crc32(name.encode()), seed]).standard_normal(out[name].shape)
        drawn = base * np.exp(spread * noise) if base else spread * noise
        out[name] = __import__('jax').numpy.asarray(drawn.astype(out[name].dtype))
    for name, factor in factors.items():
        out[name] = (out[name] * factor).astype(out[name].dtype)
    return out
```

```python
from contextlib import ExitStack

import numpy as np

import concourse.bass as bass
from concourse import mybir

F32 = mybir.dt.float32
I32 = mybir.dt.int32
U8 = mybir.dt.uint8
ALU = mybir.AluOpType
ACT = mybir.ActivationFunctionType
AX_X = mybir.AxisListType.X

P = 128
T = 256
TT = T // P
D = 1024
DK = D // P
EPS = 1e-6

GH, GK = 4, 128
F_FLOOR = float(np.exp(-20.0))
MH, NOPE, ROPE, VD = 8, 64, 32, 64
QK = NOPE + ROPE
QR, KVR = 256, 128
NG, EPG = 8, 8
FE = 256
SLOT = 64
ROUNDS = (T - NG) // SLOT + NG
COL_Q, COL_FF, COL_FB, COL_V, COL_OG = 0, 512, 1024, 1536, 2048
COL_CQ, COL_CKV, COL_GA, COL_GB = 2560, 2816, 2976, 4000

H2, HD = 16, 64
GW, ROWS, WIN = 64, 4, 16
C_B, C_C, C_X, C_ZA, C_Q, C_K, C_V, C_ZB, C_GA, C_GB = [1024 * i for i in range(10)]
TOEP = (2 * GW - 1) * ROWS

RING = 8
LEVELS = [128, 64, 32, 16, 8, "base_fwd", "base_bwd", "diag"]
MASK_OF = {32: 0, 16: 1, 8: 2, "base_fwd": 3, "base_bwd": 4, "diag": 5}

VEC_ROWS, _at = {}, 0
for _name, _n in (("pre_g_2", 8), ("b_mod_2", 16), ("conv_w_2", 24), ("conv_b_2", 8), ("c_2", 8), ("c_ctx_2", 8),
                  ("ln_mix", 8), ("ln_ple", 8), ("mla_qa_norm", 2), ("mla_kva_norm", 1), ("hg_lb", 16)):
    VEC_ROWS[_name] = (_at, _n)
    _at += _n
NVEC = _at

CONST_COLS, _at = {}, 0
for _name, _n in (("ident", 128), ("ustrict", 128), ("ones", 256), ("rot", 128), ("cosT", 256), ("sinT", 256),
                  ("winmask", 256), ("flip", 128), ("invfreq", 16), ("iota_slot", SLOT), ("rev8", 8), ("round_id", ROUNDS)):
    CONST_COLS[_name] = (_at, _n)
    _at += _n
NCONST = _at


def constants():
    c = np.zeros((P, NCONST), np.float32)

    def put(name, value):
        a, n = CONST_COLS[name]
        c[:, a:a + n] = value

    i = np.arange(P)
    put("ident", np.eye(P))
    put("ustrict", i[:, None] < i[None, :])
    put("ones", 1.0)
    rot = np.zeros((P, P))
    for r in range(P):
        if (r % 32) < 16:
            rot[r + 16, r] = -1.0
        else:
            rot[r - 16, r] = 1.0
    put("rot", rot)
    half = HD // 2
    inv = 10000.0 ** (-np.arange(0, half, 2, dtype=np.float32) / np.float32(half))
    t = np.arange(T)
    d = np.arange(P) % HD
    where = np.where(d[:, None] < 32, (t // GW)[None, :], (t % GW)[None, :]).astype(np.float32)
    ang = where * inv.astype(np.float32)[d % 16][:, None]
    put("cosT", np.cos(ang.astype(np.float64)))
    put("sinT", np.sin(ang.astype(np.float64)))
    qc = GW - 1 - i % GW
    put("flip", (i[:, None] // GW == i[None, :] // GW) & (i[:, None] % GW == GW - 1 - i[None, :] % GW))
    start = np.clip(qc - WIN // 2, 0, GW - WIN)
    kc = np.arange(T) // ROWS
    inside = (kc[None, :] >= start[:, None]) & (kc[None, :] < start[:, None] + WIN)
    put("winmask", np.where(inside, 0.0, -1e30))
    put("invfreq", 10000.0 ** (-np.arange(16, dtype=np.float32) / np.float32(16)))
    put("iota_slot", np.arange(SLOT))
    put("rev8", 8 - np.arange(8))
    put("round_id", np.arange(ROUNDS))
    m = np.zeros((P, 6, P), np.float32)
    s, t2 = i[:, None], i[None, :]
    m[:, 0] = s // 64 == t2 // 64
    m[:, 1] = s // 32 == t2 // 32
    m[:, 2] = s // 16 == t2 // 16
    m[:, 3] = s // 8 == t2 // 8
    m[:, 4] = (s // 8 == t2 // 8) & (s > t2)
    m[:, 5] = s == t2
    return c, m


def build(nc, a, out):
    with ExitStack() as ctx:
        sems = {}

        def S(name):
            if name not in sems:
                sems[name] = ctx.enter_context(nc.semaphore(name))
            return sems[name]

        def sb(name, shape, dt=F32):
            return ctx.enter_context(nc.sbuf_tensor(name, shape, dt))

        ring = sb("ring", [P, RING, 2048])
        X = sb("X", [P, TT, D])
        HN = sb("HN", [P, TT, D])
        HT = sb("HT", [P, DK, T])
        CST = sb("CST", [P, NCONST])
        MSK = sb("MSK", [P, 6, P], U8)
        VROW = sb("VROW", [P, P])
        VEC = sb("VEC", [P, NVEC])
        QKN = sb("QKN", [P, 2, QK])
        ONB = sb("ONB", [P, GK])
        RB = sb("RB", [P, 72])
        RW = sb("RW", [P, DK, 72])
        LNM = sb("LNM", [P, DK])
        PG = sb("PG", [P, D])
        POSI = sb("POSI", [P, TT], I32)
        SM = sb("SM", [P, 1200])
        RT = sb("RT", [P, 16], I32)
        sm_at = [0]

        def small(*shape):
            n = int(np.prod(shape))
            v = SM[:, sm_at[0]:sm_at[0] + n]
            sm_at[0] += n
            if len(shape) == 2:
                v = v.rearrange("p (a b) -> p a b", a=shape[0])
            if len(shape) == 3:
                v = v.rearrange("p (a b c) -> p a b c", a=shape[0], b=shape[1])
            return v

        AR = sb("AR", [P, 25200])

        def area(at, *shape):
            n = int(np.prod(shape))
            assert at + n <= 25200, (at, shape)
            v = AR[:, at:at + n]
            if len(shape) == 2:
                v = v.rearrange("p (a b) -> p a b", a=shape[0])
            if len(shape) == 3:
                v = v.rearrange("p (a b c) -> p a b c", a=shape[0], b=shape[1])
            if len(shape) == 4:
                v = v.rearrange("p (a b c d) -> p a b c d", a=shape[0], b=shape[1], c=shape[2])
            return v

        def const(name):
            at, n = CONST_COLS[name]
            return CST[:, at:at + n]

        def vec(name, k=0, n=1):
            at = VEC_ROWS[name][0] + k
            return VEC[:, at:at + n]

        def over(ap, *shape):
            return ap.to_broadcast([P] + list(shape))

        ident = const("ident")
        QT = area(0, GH, T)
        SF = area(1024, 2 * GH, T)
        KF = area(3072, 2 * GH, T)
        V = area(5120, TT, 512)
        OG = area(6144, TT, 512)
        GATE = area(7168, 16, T)
        OM = area(11264, TT, 512)
        M0 = 12288
        CQ = area(M0, TT, QR)
        CK = area(M0 + 512, TT, 160)
        CQT = area(M0 + 832, 2, T)
        CKT = area(M0 + 1344, T)
        KV = area(M0 + 1600, TT, D)
        QKM = area(M0 + 3648, 2, TT, MH * QK)
        QKT = area(M0 + 6720, MH, 512)
        SQ = area(M0 + 6720, 2, TT * MH, QK)
        PR = area(M0 + 10816, 2, TT, T)
        PT = area(M0 + 11840, 2, TT, T)
        FC = area(M0, GH, T)
        BX = area(M0 + 1024, GH, T)
        DEC = area(M0 + 2048, 2, 2, GH * T)
        AD = area(M0 + 6144, 2, GH, P)
        AXX = area(M0 + 7168, 2, GH, P)
        OO = area(M0 + 8192, TT, GH, GK)
        OSQ = area(M0, TT * GH, GK)
        OTG = area(M0 + 2048, GH, T)
        OTM = area(M0 + 3072, GH, T)
        KC = area(0, DK, T)
        VC = area(2048, TT, D)
        PP = area(4096, TT, D)
        CSQ = area(4096, TT, D)
        E0 = 6144
        SCB = area(E0, DK, P)
        PRAW = area(E0 + 1024, TT, T)
        PTR = area(E0 + 1536, 2, T)
        BGT = area(E0 + 2048, D)
        WTB = area(E0, TT * EPG, P)
        SEL = area(E0 + 2048, TT, SLOT)
        XG = area(E0 + 2176, DK, SLOT)
        WB = area(E0 + 2688, EPG, SLOT)
        STR = area(E0 + 3200, T)
        SGM = area(E0 + 3456, 2, 2, SLOT)
        H3W = area(E0 + 3712, 2, 2, SLOT)
        HH = area(E0 + 3968, 2, 2, SLOT)
        YT = area(E0 + 4224, DK, SLOT)
        YY = area(E0 + 4736, D)
        LGT = area(E0 + 5760, TT, 72)
        GEX = area(E0 + 5904, NG, EPG)
        SG = area(E0, 2, TT, T)
        GA = area(E0, DK, T)
        GB = area(E0 + 2048, DK, T)
        ZB = area(E0 + 4096, TT, D)
        YA = area(E0 + 6144, DK, T)
        UC = area(E0 + 8192, DK, T + 2)
        BT = area(E0 + 8192, 2, TT, T)
        BM = area(E0 + 9216, 2, T)
        QT2 = area(E0 + 10256, DK, T)
        KT2 = area(E0 + 12304, DK, T)
        V2 = area(E0 + 14352, TT, D)
        RAW = area(E0 + 16400, 2, 512)
        RTM = area(E0 + 17424, 2, 512)
        PR2 = area(E0 + 16400, 2, 512)
        PT2 = area(E0 + 17424, 2, 512)
        YF = area(E0 + 10256, TT, D)

        MODT = small(16, 2)
        CC = small(DK, 2)
        ACOL = small(2, DK)
        LBF = small(8)
        LBR = small(8)
        NHALF = small(32)
        ss = {n: small(2) for n in ("x", "hm", "ctx", "ple", "two", "y")}
        rs = {n: small(2) for n in ss}
        SSL, RSL = small(4), small(4)
        SSH, RSH = small(32), small(32)
        SSO, RSO = small(8), small(8)
        ANG, CS, SN = small(TT, 16), small(TT, 16), small(TT, 16)
        POSF, KQ, RED = small(2), small(TT, 16), small(TT, 16)
        MX, NMX, SUM, RSM = small(2, 2), small(2, 2), small(2, 2), small(2, 2)
        MX2, NMX2, SUM2, RSM2 = small(2), small(2), small(2), small(2)
        GMX, GEXP, GSM, PGR = small(2), small(TT, 8), small(2), small(2)
        VAL, VMX, GOH = small(TT, 8), small(2), small(TT, 8)
        EL, EL2, M1, M2, O1, O2 = small(TT, 8), small(TT, 8), small(2), small(2), small(TT, 8), small(TT, 8)
        DLT, E2W, DEN, W1, W2 = small(2), small(2), small(2), small(2), small(2)
        WT = small(TT, 8)
        CNT, NR, ENDS, STA = small(8), small(8), small(8), small(8)
        RK, POS = small(TT, 8), small(2)
        TAB = small(ROUNDS, 8)
        TABR = small(ROUNDS)

        B = [ctx.enter_context(nc.psum_tensor(f"bank{i}", [P, 512], F32)) for i in range(8)]

        def wcols(w, c0, n, k=DK):
            return w[0].rearrange("(k p) n -> p k n", p=P)[:, :, c0:c0 + n], k, n

        w_in, w_in2 = a["w_in"], a["w_in_2"]
        fills = []
        results = []

        def fill(src, name, feature=True, ncols=256):
            fills.append(src)
            k, n = src[1], src[2]
            for c0 in range(0, n, ncols):
                results.append((name, len(fills) - 1, c0, feature, min(ncols, n - c0)))

        fill(wcols(w_in, COL_CQ, 256), name="cq", feature=False)
        fill(wcols(w_in, COL_CKV, 160), name="ckv", feature=False)
        for c in range(2):
            fill(wcols(w_in, COL_FF + 256 * c, 256), name="f")
        for c in range(2):
            fill(wcols(w_in, COL_FB + 256 * c, 256), name="f")
        for c in range(2):
            fill(wcols(w_in, COL_Q + 256 * c, 256), name="q")
        for c in range(2):
            fill(wcols(w_in, COL_V + 256 * c, 256), name="v", feature=False)
        for c in range(2):
            fill(wcols(w_in, COL_OG + 256 * c, 256), name="og", feature=False)
        fill(wcols(a["w_uq"], 0, 768, 2), name="uq", feature=False)
        fill(wcols(a["w_ukv"], 0, 1024, 1), name="ukv", feature=False)
        for c in range(8):
            fill(wcols(w_in, COL_GA + 256 * c, 256), name="gate")
        for c in range(2):
            fill(wcols(a["w_oB"], 512 * c, 512, 4), name="yb")
        for c in range(2):
            fill(wcols(a["w_oA"], 512 * c, 512, 4), name="ya")
        for c in range(4):
            fill(wcols(a["w_out"], 256 * c, 256), name="out", feature=False)
        for c in range(8):
            fill(wcols(a["w_mod_2"], 256 * c, 256), name="mod")
        for c in range(4):
            fill(wcols(a["w_mod_2"], 2048 + 256 * c, 256), name="gt", feature=False)
        for c in range(4):
            fill(wcols(w_in2, C_K + 256 * c, 256), name="kc")
        for c in range(4):
            fill(wcols(w_in2, C_V + 256 * c, 256), name="vc", feature=False)
        fill(wcols(a["w_ple_proj"], 0, 1024, 2), name="pp", feature=False)
        NA = len(fills)
        NRA = len(results)
        for c in range(4):
            fill(wcols(a["w_ple_gate"], 256 * c, 256), name="ple", feature=False)
        for name, col, feature in (("zb", C_ZB, False), ("ga", C_GA, True), ("gb", C_GB, True), ("za", C_ZA, True),
                                   ("b", C_B, True), ("c", C_C, True), ("xin", C_X, True), ("q2", C_Q, True),
                                   ("k2", C_K, True), ("v2", C_V, False)):
            for c in range(4):
                fill(wcols(w_in2, col + 256 * c, 256), name=name, feature=feature)
        for c in range(4):
            fill(wcols(a["w_out_conv_2"], 256 * c, 256), name="yconv")
        for c in range(4):
            fill(wcols(a["w_out_attn_2"], 256 * c, 256), name="yattn")
        for c in range(4):
            fill(wcols(a["w_o_2"], 256 * c, 256), name="wo", feature=False)
        NC_ = len(fills) - NA
        last_result = {f: i for i, (_, f, _, _, _) in enumerate(results)}
        of = {}
        for i, r in enumerate(results):
            of.setdefault(r[0], []).append(i)

        EMPTIER = {"cq": "dve", "ckv": "dve", "f": "act", "q": "dve", "v": "act", "og": "dve", "uq": "dve",
                   "ukv": "act", "gate": "act", "yb": "dve", "ya": "dve", "out": "dve", "mod": "dve", "gt": "dve",
                   "kc": "act", "vc": "act", "pp": "act", "ple": "act", "zb": "dve", "ga": "act", "gb": "act",
                   "za": "dve", "b": "dve", "c": "act", "xin": "dve", "q2": "act", "k2": "act", "v2": "act",
                   "yconv": "dve", "yattn": "dve", "wo": "dve"}
        emptied, _n = {}, {"dve": 0, "act": 0}
        for i, r in enumerate(results):
            e = EMPTIER[r[0]]
            _n[e] += 1
            emptied[i] = (e, _n[e])

        def ready_sem(i):
            return ("res_a", i + 1) if i < NRA else ("res_c", i - NRA + 1)

        def wait_result(eng, i):
            n, v = ready_sem(i)
            eng.wait_ge(S(n), v)

        def bank_of(i):
            return B[i % 4]

        moe_order = [("w1", 0), ("w3", 0)]
        for e in range(EPG):
            if e + 1 < EPG:
                moe_order += [("w1", e + 1), ("w3", e + 1)]
            moe_order.append(("w2", e))
        moe_index = {ke: j for j, ke in enumerate(moe_order)}
        NM = len(moe_order)
        M_BASE = NA % RING

        def moe_slot(j):
            return (M_BASE + j) % RING

        def c_slot(f):
            return (M_BASE + f - NA) % RING

        def slot_of(f):
            return f % RING if f < NA else c_slot(f)

        def slot_view(f):
            _, k, n = fills[f]
            return ring[:, slot_of(f), 0:k * n].rearrange("p (k n) -> p k n", k=k)

        EARLY, SMALL = 16 * 13, 16 * 9
        NORMS = ["x", "lat", "qk", "o", "ctx", "hm", "ple", "two", "y"]
        TURNS = ["x", "ctx", "hm", "ple", "two", "o"]

        def nth(tag, seq=NORMS):
            return seq.index(tag) + 1

        block = ctx.enter_context(nc.Block())

        @block.sync
        def _(sp):
            sp.dma_start(X[:], a["x"][0].rearrange("(t p) d -> p t d", p=P)).then_inc(S("x_in"), 16)

            def stream_a():
                for f in range(NA):
                    if f >= RING:
                        sp.wait_ge(S("res_a"), last_result[f - RING] + 1)
                    sp.dma_start(slot_view(f), fills[f][0]).then_inc(S(f"arr_a{slot_of(f)}"), 16)

            stream_a()

            def expert_dma(j, g):
                kind, e = moe_order[j]
                dst = ring[:, moe_slot(j), :]
                if kind == "w2":
                    src = a["w2"][0, bass.ds(g * EPG + e, 1), :, :].rearrange("o (c p) n -> p (o c) n", p=P)
                    dst = dst.rearrange("p (c n) -> p c n", c=2)
                else:
                    src = a[kind][0, bass.ds(g * EPG + e, 1), :, :].rearrange("o (p k) n -> p (o k) n", p=P)
                    dst = dst.rearrange("p (k n) -> p k n", k=DK)
                sp.dma_start(dst, src).then_inc(S(f"arr_m{moe_slot(j)}"), 16)

            for j in range(NM):
                if j < RING:
                    sp.wait_ge(S("res_a"), last_result[NA - RING + j] + 1)
                else:
                    sp.wait_ge(S("moe_used"), j - RING + 1)
                expert_dma(j, 0)
            sp.wait_ge(S("table"), 1)
            rounds = sp.value_load(RT[0:1, 0:1], min_val=4, max_val=ROUNDS)
            with sp.Fori(0, rounds - 1) as r:
                g = sp.value_load(RT[0:1, bass.ds(r + 2, 1)], min_val=0, max_val=NG - 1)
                for j in range(NM):
                    sp.wait_ge(S("moe_used"), r * NM + (NM + j - RING + 1))
                    expert_dma(j, g)

            used = sp.value_load(RT[0:1, 14:15], min_val=4 * NM - RING, max_val=ROUNDS * NM)
            for f in range(NA, NA + NC_):
                if f - NA < RING:
                    sp.wait_ge(S("moe_used"), used + (f - NA + 1))
                else:
                    sp.wait_ge(S("res_c"), last_result[f - RING] - NRA + 1)
                sp.dma_start(slot_view(f), fills[f][0]).then_inc(S(f"arr_c{slot_of(f)}"), 16)
            sp.wait_ge(S("final"), 2)
            sp.dma_start(out[0].rearrange("(t p) d -> p t d", p=P), HN[:]).then_inc(S("stored"), 16)
            sp.wait_ge(S("stored"), 16)

        def wait_slot(pe, f):
            if f < NA:
                pe.wait_ge(S(f"arr_a{slot_of(f)}"), 16 * (f // RING + 1))
            else:
                pe.wait_ge(S(f"arr_c{slot_of(f)}"), 16 * ((f - NA) // RING + 1))

        @block.tensor
        def _(pe):
            def wait_bank(i):
                if i >= 4:
                    e, n = emptied[i - 4]
                    pe.wait_ge(S("emptied_" + e), n)

            def product(i, act, first=None):
                name, f, c0, feature, n = results[i]
                if first is None:
                    wait_bank(i)
                if c0 == 0:
                    wait_slot(pe, f)
                w, bank = slot_view(f), bank_of(i)
                k_n = fills[f][1]
                for part in range(2):
                    for k in range(k_n):
                        if feature:
                            mm = pe.matmul(bank[:, part * T:part * T + T], w[:, k, c0 + part * P:c0 + part * P + P],
                                           act[:, k, :], start=(k == 0), stop=(k == k_n - 1))
                        else:
                            mm = pe.matmul(bank[:, part * 256:part * 256 + n], act[:, k, part * P:part * P + P],
                                           w[:, k, c0:c0 + n], start=(k == 0), stop=(k == k_n - 1))
                mm.then_inc(S(ready_sem(i)[0]), 1)

            def products(name, act):
                for i in of[name]:
                    product(i, act)

            def turn_rows(src):
                for k in range(DK):
                    for t in range(TT):
                        mm = pe.transpose(B[4 + k // 2][:, (k % 2) * T + t * P:(k % 2) * T + t * P + P], src(k, t), ident)
                    if k % 2 == 1:
                        mm.then_inc(S("turned"), 1)

            def cols(tile):
                return lambda k, t: tile[:, t, k * P:k * P + P]

            pe.wait_ge(S("early_in"), EARLY)
            pe.wait_ge(S("early_in"), EARLY)
            pe.transpose(B[4][:, 0:NVEC], VROW[0:NVEC, :], ident[0:NVEC, 0:NVEC]).then_inc(S("vec_ps"), 1)
            pe.wait_ge(S("vec"), 1)
            pe.wait_ge(S("normed"), nth("x"))
            turn_rows(cols(HN))
            pe.wait_ge(S("hT_dve"), 4)
            pe.wait_ge(S("hT_act"), 4)
            products("cq", HT)
            products("ckv", HT)
            for name in ("f", "q", "v", "og"):
                products(name, HT)
            pe.wait_ge(S("normed"), nth("lat"))
            for c in range(2):
                for t in range(TT):
                    pe.transpose(B[4][:, c * T + t * P:c * T + t * P + P], CQ[:, t, c * P:c * P + P], ident)
            for t in range(TT):
                mm = pe.transpose(B[5][:, t * P:t * P + P], CK[:, t, 0:P], ident)
            mm.then_inc(S("lat_ps"), 1)
            pe.wait_ge(S("latT"), 1)
            products("uq", CQT)
            products("ukv", CKT.unsqueeze(1))
            products("gate", HT)
            pe.wait_ge(S("normed"), nth("qk"))
            pe.wait_ge(S("qk_pool"), 1)
            for h in range(MH):
                if h >= 4:
                    pe.wait_ge(S("qkT_even" if h % 2 == 0 else "qkT_odd"), h // 2 - 1)
                for s in range(2):
                    for t in range(TT):
                        mm = pe.transpose(B[4 + h % 4][0:QK, s * T + t * P:s * T + t * P + P],
                                          QKM[:, s, t, h * QK:h * QK + QK], ident)
                mm.then_inc(S("qkT_ps"), 1)
            pe.wait_ge(S("qkT_even"), 4)
            pe.wait_ge(S("qkT_odd"), 4)
            for i in of["gate"][-4:]:
                pe.wait_ge(S("emptied_" + emptied[i][0]), emptied[i][1])

            def mla_scores(h):
                if h >= 2:
                    pe.wait_ge(S("mla_p"), 2 * (h - 1))
                for t in range(TT):
                    mm = pe.matmul(B[4 + h % 2][:, t * T:t * T + T], QKT[0:QK, h, t * P:t * P + P],
                                   QKT[0:QK, h, T:2 * T], start=True, stop=True)
                mm.then_inc(S("mla_s"), 1)

            mla_scores(0)
            for h in range(MH):
                if h + 1 < MH:
                    mla_scores(h + 1)
                pe.wait_ge(S("mla_p"), 2 * h + 2)
                if h >= 2:
                    pe.wait_ge(S("mla_pt"), h - 1)
                for kt in range(TT):
                    for t in range(TT):
                        mm = pe.transpose(B[6 + h % 2][:, kt * T + t * P:kt * T + t * P + P],
                                          PR[:, h % 2, t, kt * P:kt * P + P], ident)
                mm.then_inc(S("mla_pT"), 1)
                pe.wait_ge(S("mla_pt"), h + 1)
                if h >= 2:
                    pe.wait_ge(S("mla_o"), h - 1)
                for t in range(TT):
                    for kt in range(TT):
                        mm = pe.matmul(B[h % 2][:, t * VD:t * VD + VD], PT[:, h % 2, kt, t * P:t * P + P],
                                       KV[:, kt, h * P + NOPE:h * P + P], start=(kt == 0), stop=(kt == TT - 1))
                mm.then_inc(S("mla_pv"), 1)
            for n, lv in enumerate(LEVELS):
                pe.wait_ge(S("gla_qk"), n + 1)
                if n == 0:
                    pe.wait_ge(S("mla_o"), MH)
                if n >= 4:
                    pe.wait_ge(S("gla_a"), n - 3)
                for st in range(TT):
                    bank = B[2 * (n % 4) + st]
                    for h in range(GH):
                        tt = 1 - st if lv == 128 else st
                        q = QT if lv == "diag" else DEC[:, n % 2, 0].rearrange("p (h t) -> p h t", h=GH)
                        k = DEC[:, n % 2, 1].rearrange("p (h t) -> p h t", h=GH)
                        mm = pe.matmul(bank[:, h * P:h * P + P], k[:, h, st * P:st * P + P],
                                       q[:, h, tt * P:tt * P + P], start=True, stop=True)
                mm.then_inc(S("gla_s"), 1)
            pe.wait_ge(S("gla_a"), len(LEVELS))
            for tt in range(TT):
                for h in range(GH):
                    for st in range(TT):
                        sc = AD[:, st, h, :] if st == tt else AXX[:, st, h, :]
                        mm = pe.matmul(B[tt][:, h * P:h * P + P], sc, V[:, st, h * P:h * P + P],
                                       start=(st == 0), stop=(st == TT - 1))
            mm.then_inc(S("gla_o_ps"), 1)
            for c in range(GH):
                for t in range(TT):
                    mm = pe.transpose(B[4 + c // 2][:, (c % 2) * T + t * P:(c % 2) * T + t * P + P],
                                      OM[:, t, c * P:c * P + P], ident)
            mm.then_inc(S("omT_ps"), 1)
            pe.wait_ge(S("normed"), nth("o"))
            for c in range(GH):
                for t in range(TT):
                    mm = pe.transpose(B[6 + c // 2][:, (c % 2) * T + t * P:(c % 2) * T + t * P + P],
                                      OO[:, t, c, :], ident)
            mm.then_inc(S("ogT_ps"), 1)
            pe.wait_ge(S("omT"), 1)
            pe.wait_ge(S("gla_o"), 1)
            products("yb", OTM)
            pe.wait_ge(S("ogT"), 1)
            products("ya", OTG)
            pe.wait_ge(S("merged"), 4)
            products("out", GATE[:, 0:8, :])

            pe.wait_ge(S("silu_c"), 1)
            for n, i in enumerate(of["mod"]):
                name, f, c0, feature, _n256 = results[i]
                wait_bank(i)
                wait_slot(pe, f)
                w = slot_view(f)
                for part in range(2):
                    for k in range(DK):
                        mm = pe.matmul(bank_of(i)[:, 2 * part:2 * part + 2], w[:, k, part * P:part * P + P],
                                       CC[:, k, :], start=(k == 0), stop=(k == DK - 1))
                mm.then_inc(S("res_a"), 1)
            pe.wait_ge(S("silu_cb"), 1)
            for i in of["gt"]:
                name, f, c0, feature, _n256 = results[i]
                wait_bank(i)
                wait_slot(pe, f)
                w = slot_view(f)
                for k in range(DK):
                    mm = pe.matmul(bank_of(i)[:, 0:256], SCB[:, k, :], w[:, k, :], start=(k == 0), stop=(k == DK - 1))
                mm.then_inc(S("res_a"), 1)
            pe.wait_ge(S("normed"), nth("ctx"))
            turn_rows(cols(HN))
            pe.wait_ge(S("cT_dve"), 8)
            products("kc", HT)
            products("vc", HT)
            pe.wait_ge(S("p_in"), 16)
            for c in range(2):
                for t in range(TT):
                    mm = pe.transpose(B[4][:, c * T + t * P:c * T + t * P + P], PRAW[:, t, c * P:c * P + P], ident)
            mm.then_inc(S("pT_ps"), 1)
            pe.wait_ge(S("pT"), 1)
            products("pp", PTR)

            pe.wait_ge(S("normed"), nth("hm"))
            turn_rows(cols(HN))
            pe.wait_ge(S("rT_dve"), 4)
            pe.wait_ge(S("rT_act"), 4)
            pe.wait_ge(S("small_in"), SMALL)
            for t in range(TT):
                for k in range(DK):
                    mm = pe.matmul(B[4][:, t * 72:t * 72 + 72], HT[:, k, t * P:t * P + P], RW[:, k, :],
                                   start=(k == 0), stop=(k == DK - 1))
            mm.then_inc(S("logits_ps"), 1)
            pe.wait_ge(S("group"), 1)
            U, ONE = const("ustrict"), const("ones")[:, 0:P]
            pe.matmul(B[5][:, 0:8], U, GOH[:, 0, :], start=True, stop=True)
            pe.matmul(B[5][:, 8:16], ONE, GOH[:, 0, :], start=True, stop=False)
            pe.matmul(B[5][:, 8:16], U, GOH[:, 1, :], start=False, stop=True)
            pe.matmul(B[5][:, 16:24], ONE, GOH[:, 0, :], start=True, stop=False)
            pe.matmul(B[5][:, 16:24], ONE, GOH[:, 1, :], start=False, stop=True).then_inc(S("rank_ps"), 1)

            def slot_in(j, r):
                if isinstance(r, int):
                    pe.wait_ge(S(f"arr_m{moe_slot(j)}"), 16 * (3 * r + j // RING + 1))
                else:
                    pe.wait_ge(S(f"arr_m{moe_slot(j)}"), r * 48 + 16 * (j // RING + 1))

            def moe_round(r):
                def at(n, k):
                    return r * n + k

                pe.wait_ge(S("sel"), at(1, 1))
                for k in range(DK):
                    for t in range(TT):
                        mm = pe.matmul(B[0][:, k * SLOT:k * SLOT + SLOT], HN[:, t, k * P:k * P + P], SEL[:, t, :],
                                       start=(t == 0), stop=(t == TT - 1))
                mm.then_inc(S("gath_ps"), 1)
                for e in range(EPG):
                    for t in range(TT):
                        mm = pe.matmul(B[1][:, e * SLOT:e * SLOT + SLOT], WTB[:, t * EPG + e, :], SEL[:, t, :],
                                       start=(t == 0), stop=(t == TT - 1))
                for t in range(TT):
                    mm = pe.transpose(B[2][0:SLOT, t * P:t * P + P], SEL[:, t, :], ident)
                mm.then_inc(S("wb_ps"), 1)
                pe.wait_ge(S("gath"), at(1, 1))

                def up(e):
                    bank = B[3 + e % 2]
                    if e >= 2:
                        pe.wait_ge(S("hh"), at(EPG, e - 1))
                    for half, kind in ((0, "w1"), (1, "w3")):
                        j = moe_index[(kind, e)]
                        slot_in(j, r)
                        w = ring[:, moe_slot(j), :].rearrange("p (k n) -> p k n", k=DK)
                        for c in range(2):
                            for k in range(DK):
                                o = (2 * half + c) * SLOT
                                mm = pe.matmul(bank[:, o:o + SLOT], w[:, k, c * P:c * P + P], XG[:, k, :],
                                               start=(k == 0), stop=(k == DK - 1))
                        mm.then_inc(S("moe_used"), 1)

                def down(e):
                    j = moe_index[("w2", e)]
                    slot_in(j, r)
                    w = ring[:, moe_slot(j), :].rearrange("p (c n) -> p c n", c=2)
                    pe.wait_ge(S("hh"), at(EPG, e + 1))
                    for c2 in range(DK):
                        for c in range(2):
                            mm = pe.matmul(B[5][:, c2 * SLOT:c2 * SLOT + SLOT], w[:, c, c2 * P:c2 * P + P],
                                           HH[:, e % 2, c, :], start=(e == 0 and c2 == 0 and c == 0),
                                           stop=(e == EPG - 1 and c == 1), skip_group_check=True)
                    mm.then_inc(S("moe_used"), 1)

                up(0)
                for e in range(EPG):
                    if e + 1 < EPG:
                        up(e + 1)
                    down(e)
                pe.wait_ge(S("group"), 1)
                pe.wait_ge(S("yt"), at(1, 1))
                for c in range(DK):
                    mm = pe.transpose(B[6 + c // 4][0:SLOT, (c % 4) * P:(c % 4) * P + P], YT[:, c, :], ident)
                mm.then_inc(S("yrow_ps"), 1)
                pe.wait_ge(S("yrow"), at(1, 1))
                for t in range(TT):
                    for half in range(2):
                        mm = pe.matmul(B[2 * t + half][:, :], STR[0:SLOT, t * P:t * P + P],
                                       YY[0:SLOT, half * 512:half * 512 + 512], start=True, stop=True)
                mm.then_inc(S("scat_ps"), 1)

            for i in range(NRA - 4, NRA):
                pe.wait_ge(S("emptied_" + emptied[i][0]), emptied[i][1])
            moe_round(0)
            pe.wait_ge(S("table"), 1)
            rounds = pe.value_load(RT[0:1, 0:1], min_val=4, max_val=ROUNDS)
            with pe.Fori(1, rounds) as r:
                moe_round(r)

            pe.wait_ge(S("normed"), nth("ple"))
            turn_rows(cols(HN))
            pe.wait_ge(S("pleT_dve"), 4)
            pe.wait_ge(S("pleT_act"), 4)
            for i in of["ple"]:
                product(i, HT, first=True)

            pe.wait_ge(S("normed"), nth("two"))
            turn_rows(cols(HN))
            pe.wait_ge(S("twoT"), 8)
            for name in ("zb", "ga", "gb", "za", "b", "c", "xin"):
                products(name, HT)
            for name in ("q2", "k2"):
                for n, i in enumerate(of[name]):
                    product(i, HT)
                    m = n + (4 if name == "k2" else 0)
                    pe.wait_ge(S("emptied_act"), emptied[i][1])
                    if m >= 2:
                        pe.wait_ge(S("roped"), m - 1)
                    pe.matmul(B[4 + m % 2][:, :], const("rot"), RAW[:, m % 2, :], start=True, stop=True)\
                      .then_inc(S("rot_ps"), 1)
            products("v2", HT)
            pe.wait_ge(S("roped"), 8)
            for i in of["v2"]:
                pe.wait_ge(S("emptied_" + emptied[i][0]), emptied[i][1])

            N2 = H2 * TT

            def scores2(n):
                h, t = divmod(n, TT)
                c, p0 = h // 2, (h % 2) * HD
                if n >= 2:
                    pe.wait_ge(S("na_p"), n - 1)
                bank = B[4 + n % 2]
                pe.matmul(bank[:, 0:T], QT2[p0:p0 + HD, c, t * P:t * P + P], KT2[p0:p0 + HD, c, :], start=True, stop=False)
                pe.wait_ge(S("bm"), n + 1)
                pe.matmul(bank[:, 0:T], const("flip"), BM[:, n % 2, :], start=False, stop=True)
                pe.matmul(bank[:, T:2 * T], QT2[p0:p0 + HD, c, t * P:t * P + P], KC[p0:p0 + HD, c, :],
                          start=True, stop=True).then_inc(S("na_s"), 1)

            scores2(0)
            for n in range(N2):
                h, t = divmod(n, TT)
                if n + 1 < N2:
                    scores2(n + 1)
                pe.wait_ge(S("na_p"), n + 1)
                if n >= 2:
                    pe.wait_ge(S("na_pt"), n - 1)
                for kt in range(4):
                    mm = pe.transpose(B[6 + n % 2][:, kt * P:kt * P + P], PR2[:, n % 2, kt * P:kt * P + P], ident)
                mm.then_inc(S("na_pT"), 1)
                pe.wait_ge(S("na_pt"), n + 1)
                if n >= 2:
                    pe.wait_ge(S("na_o"), n - 1)
                for kt in range(4):
                    v = V2 if kt < 2 else VC
                    mm = pe.matmul(B[n % 2][:, 0:HD], PT2[:, n % 2, kt * P:kt * P + P],
                                   v[:, kt % 2, h * HD:h * HD + HD], start=(kt == 0), stop=(kt == 3))
                mm.then_inc(S("na_pv"), 1)
            pe.wait_ge(S("na_o"), N2)
            turn_rows(cols(HN))
            products("yconv", YA)
            pe.wait_ge(S("oT"), 8)
            products("yattn", HT)
            pe.wait_ge(S("merged2"), 4)
            products("wo", GA)

        @block.scalar
        def _(act):
            act.dma_start(CST[:], a["consts"]).then_inc(S("early_in"), 16)
            for name, (row, n) in VEC_ROWS.items():
                v = a[name]
                if name == "b_mod_2":
                    src = v[0, 0:2048].rearrange("(r p) -> r p", p=P)
                elif name == "conv_w_2":
                    src = v[0].rearrange("k (r p) -> (k r) p", p=P)
                elif name == "hg_lb":
                    src = v.rearrange("d j (r p) -> (d j r) p", p=P)
                elif name == "c_ctx_2":
                    src = v.rearrange("(r p) -> r p", p=P)
                else:
                    src = v[0].rearrange("(r p) -> r p", p=P)
                act.dma_start(VROW[row:row + n, :], src).then_inc(S("early_in"), 16)
            act.dma_start(POSI[:], a["positions"].rearrange("o (t p) -> p (o t)", p=P),
                          allow_slow_non_contiguous=True).then_inc(S("early_in"), 16)
            act.dma_start(QKN[:, 0, :], a["q_norm"][0].partition_broadcast(P)).then_inc(S("small_in"), 16)
            act.dma_start(QKN[:, 1, :], a["k_norm"][0].partition_broadcast(P)).then_inc(S("small_in"), 16)
            act.dma_start(ONB[:], a["hg_onorm"][0].partition_broadcast(P)).then_inc(S("small_in"), 16)
            act.dma_start(HT[:, 0:3, :].rearrange("p a b -> p (a b)"), a["masks"].rearrange("p a b -> p (a b)"))\
               .then_inc(S("masks_in"), 16)
            act.dma_start(RB[:, 0:8], a["b_rg"][0].partition_broadcast(P)).then_inc(S("small_in"), 16)
            act.dma_start(RB[:, 8:72], a["b_re"][0].partition_broadcast(P)).then_inc(S("small_in"), 16)
            act.dma_start(RW[:, :, 0:8], a["w_rg"][0].rearrange("(p k) n -> p k n", p=P)).then_inc(S("small_in"), 16)
            act.dma_start(RW[:, :, 8:72], a["w_re"][0].rearrange("(p k) n -> p k n", p=P)).then_inc(S("small_in"), 16)
            act.dma_start(LNM[:], a["ln_moe"][0].rearrange("(p k) -> p k", p=P)).then_inc(S("small_in"), 16)
            act.dma_start(PG[:], a["post_g_2"][0].partition_broadcast(P)).then_inc(S("small_in"), 16)

            def sumsq(src, tag):
                for t in range(TT):
                    ins = nc.scalar.activation(HN[:, t, :], src[:, t, :], ACT.Square, accum_out=ss[tag][:, t:t + 1])
                ins.then_inc(S("sumsq"), 1)

            def turned(tag, done, gain):
                for k in range(4, 8):
                    if k % 2 == 0:
                        act.wait_ge(S("turned"), 4 * nth(tag, TURNS) - 3 + k // 2)
                    nc.scalar.activation(HT[:, k, :], B[4 + k // 2][:, (k % 2) * T:(k % 2) * T + T], ACT.Copy,
                                         scale=gain(k)).then_inc(S(done), 1)

            act.wait_ge(S("x_in"), 16)
            sumsq(X, "x")
            act.wait_ge(S("ang"), 1)
            nc.scalar.activation(SN, RED, ACT.Sin)
            nc.scalar.activation(CS, KQ, ACT.Sin).then_inc(S("sincos"), 1)
            act.wait_ge(S("vec"), 1)
            turned("x", "hT_act", lambda k: vec("ln_mix", k))
            act.wait_ge(S("lbd"), 2)
            nc.scalar.activation(LBF, LBF, ACT.Sigmoid)
            nc.scalar.activation(LBR, LBR, ACT.Sigmoid).then_inc(S("lb"), 1)
            for n, i in enumerate(of["f"]):
                wait_result(act, i)
                nc.scalar.activation(SF[:, 2 * n:2 * n + 2, :].rearrange("p a t -> p (a t)"), bank_of(i)[:, :],
                                     ACT.Sigmoid).then_inc(S("emptied_act"), 1)
            for n, i in enumerate(of["q"]):
                wait_result(act, i)
                nc.scalar.activation(QT[:, 2 * n:2 * n + 2, :].rearrange("p a t -> p (a t)"), bank_of(i)[:, :],
                                     ACT.Sigmoid).then_inc(S("sig"), 1)
            for n, i in enumerate(of["v"]):
                wait_result(act, i)
                nc.scalar.activation(V[:, :, 256 * n:256 * n + 256], bank_of(i)[:, :].rearrange("p (t c) -> p t c", t=TT),
                                     ACT.Copy).then_inc(S("emptied_act"), 1)
            for n, i in enumerate(of["og"]):
                wait_result(act, i)
                nc.scalar.activation(OG[:, :, 256 * n:256 * n + 256], bank_of(i)[:, :].rearrange("p (t c) -> p t c", t=TT),
                                     ACT.Sigmoid).then_inc(S("sig"), 1)
            act.wait_ge(S("emptied_dve"), emptied[of["ckv"][0]][1])
            for t in range(TT):
                nc.scalar.activation(CQT[:, t, :], CQ[:, t, :], ACT.Square, accum_out=SSL[:, t:t + 1])
            for t in range(TT):
                ins = nc.scalar.activation(CKT[:, t * P:t * P + P], CK[:, t, 0:P], ACT.Square, accum_out=SSL[:, 2 + t:3 + t])
            ins.then_inc(S("sumsq"), 1)
            for n, i in enumerate(of["ukv"]):
                wait_result(act, i)
                nc.scalar.activation(KV[:, :, 256 * n:256 * n + 256], bank_of(i)[:, :].rearrange("p (t c) -> p t c", t=TT),
                                     ACT.Copy).then_inc(S("emptied_act"), 1)
            act.wait_ge(S("emptied_dve"), emptied[of["uq"][-1]][1])
            nc.scalar.activation(SQ[:, 0], QKM[:, 0].rearrange("p t (h d) -> p (t h) d", h=MH), ACT.Square)
            act.wait_ge(S("km"), 1)
            nc.scalar.activation(SQ[:, 1], QKM[:, 1].rearrange("p t (h d) -> p (t h) d", h=MH), ACT.Square)\
              .then_inc(S("sumsq"), 1)
            for n, i in enumerate(of["gate"]):
                wait_result(act, i)
                nc.scalar.activation(GATE[:, 2 * n:2 * n + 2, :].rearrange("p a t -> p (a t)"), bank_of(i)[:, :],
                                     ACT.Sigmoid).then_inc(S("emptied_act"), 1)
            act.wait_ge(S("fgate"), 1)
            nc.scalar.activation(SF[:, :, :], SF[:, :, :], ACT.Ln).then_inc(S("logf"), 1)
            for h in range(0, MH, 2):
                act.wait_ge(S("qkT_ps"), h + 1)
                nc.scalar.activation(QKT[0:QK, h, :], B[4 + h % 4][0:QK, :], ACT.Copy).then_inc(S("qkT_even"), 1)
            scale = QK ** -0.5
            for h in range(MH):
                act.wait_ge(S("mla_nmax"), h + 1)
                if h >= 2:
                    act.wait_ge(S("mla_pT"), h - 1)
                for t in range(TT):
                    nc.scalar.activation(PR[:, h % 2, t, :], B[4 + h % 2][:, t * T:t * T + T], ACT.Exp, scale=scale,
                                         bias=NMX[:, h % 2, t:t + 1], accum_out=SUM[:, h % 2, t:t + 1])\
                      .then_inc(S("mla_p"), 1)
                act.wait_ge(S("mla_pT"), h + 1)
                if h >= 2:
                    act.wait_ge(S("mla_pv"), h - 1)
                nc.scalar.activation(PT[:, h % 2, :, :].rearrange("p a t -> p (a t)"), B[6 + h % 2][:, :], ACT.Copy)\
                  .then_inc(S("mla_pt"), 1)
            for n, lv in enumerate(LEVELS):
                if lv != "diag":
                    act.wait_ge(S("gla_dec"), n + 1)
                    nc.scalar.activation(DEC[:, n % 2, :, :], DEC[:, n % 2, :, :], ACT.Exp).then_inc(S("gla_exp"), 1)
            act.wait_ge(S("omT_ps"), 1)
            for c in range(2):
                ins = nc.scalar.activation(OTM[:, 2 * c:2 * c + 2, :].rearrange("p a t -> p (a t)"), B[4 + c][:, :], ACT.Copy)
            ins.then_inc(S("omT"), 1)
            act.wait_ge(S("gla_o"), 1)
            nc.scalar.activation(OSQ, OO.rearrange("p t h v -> p (t h) v"), ACT.Square).then_inc(S("sumsq"), 1)
            act.wait_ge(S("ogT_ps"), 1)
            for c in range(2):
                ins = nc.scalar.activation(OTG[:, 2 * c:2 * c + 2, :].rearrange("p a t -> p (a t)"), B[6 + c][:, :], ACT.Copy)
            ins.then_inc(S("ogT"), 1)

            act.wait_ge(S("merged"), 4)
            act.wait_ge(S("emptied_dve"), emptied[of["out"][-1]][1])
            act.dma_start(HN[:], a["ctx_2"][0].rearrange("(t p) d -> p t d", p=P)).then_inc(S("ctx_in"), 16)
            act.dma_start(PRAW[:], a["p"][0, 0].rearrange("(t p) d -> p t d", p=P)).then_inc(S("p_in"), 16)
            act.dma_start(BGT[:], a["b_mod_2"][0, 2048:3072].partition_broadcast(P)).then_inc(S("bgt_in"), 16)
            act.wait_ge(S("cc"), 1)
            nc.scalar.activation(CC[:, :, :], CC[:, :, :], ACT.Sigmoid).then_inc(S("sig_c"), 1)
            act.wait_ge(S("ctx_in"), 16)
            for t in range(TT):
                ins = nc.scalar.activation(CSQ[:, t, :], HN[:, t, :], ACT.Square, accum_out=ss["ctx"][:, t:t + 1])
            ins.then_inc(S("sumsq"), 1)
            for n, i in enumerate(of["kc"]):
                wait_result(act, i)
                nc.scalar.activation(KC[:, 2 * n:2 * n + 2, :].rearrange("p a t -> p (a t)"), bank_of(i)[:, :],
                                     ACT.Copy).then_inc(S("emptied_act"), 1)
            for n, i in enumerate(of["vc"]):
                wait_result(act, i)
                nc.scalar.activation(VC[:, :, 256 * n:256 * n + 256], bank_of(i)[:, :].rearrange("p (t c) -> p t c", t=TT),
                                     ACT.Copy).then_inc(S("emptied_act"), 1)
            for n, i in enumerate(of["pp"]):
                wait_result(act, i)
                nc.scalar.activation(PP[:, :, 256 * n:256 * n + 256], bank_of(i)[:, :].rearrange("p (t c) -> p t c", t=TT),
                                     ACT.Copy).then_inc(S("emptied_act"), 1)
            act.wait_ge(S("turned"), 4 * nth("ctx", TURNS))
            sumsq(X, "hm")
            act.wait_ge(S("small_in"), SMALL)
            turned("hm", "rT_act", lambda k: LNM[:, k:k + 1])
            act.wait_ge(S("gdiff"), 1)
            nc.scalar.activation(GEXP, GEXP, ACT.Exp).then_inc(S("gexp"), 1)
            act.wait_ge(S("ediff"), 1)
            nc.scalar.activation(E2W, DLT, ACT.Exp).then_inc(S("eexp"), 1)

            def moe_round(r):
                def at(n, k):
                    return r * n + k

                act.wait_ge(S("wb_ps"), at(1, 1))
                nc.scalar.activation(WB.rearrange("p e s -> p (e s)"), B[1][:, :], ACT.Copy)
                nc.scalar.activation(STR[0:SLOT, :], B[2][0:SLOT, 0:T], ACT.Copy).then_inc(S("wb"), 1)
                for e in range(EPG):
                    act.wait_ge(S("moe_used"), at(NM, moe_index[("w3", e)] + 1))
                    nc.scalar.activation(SGM[:, e % 2].rearrange("p c s -> p (c s)"), B[3 + e % 2][:, 0:2 * SLOT],
                                         ACT.Sigmoid).then_inc(S("moe_sig"), 1)
                act.wait_ge(S("moe_used"), at(NM, NM))
                nc.scalar.activation(YT.rearrange("p c s -> p (c s)"), B[5][:, :], ACT.Copy).then_inc(S("yt"), 1)
                act.wait_ge(S("yrow_ps"), at(1, 1))
                for half in range(2):
                    ins = nc.scalar.activation(YY[0:SLOT, half * 512:half * 512 + 512], B[6 + half][0:SLOT, :], ACT.Copy)
                ins.then_inc(S("yrow"), 1)

            moe_round(0)
            act.wait_ge(S("table"), 1)
            rounds = act.value_load(RT[0:1, 0:1], min_val=4, max_val=ROUNDS)
            with act.Fori(1, rounds) as r:
                moe_round(r)

            act.wait_ge(S("moe_x"), rounds + 0)
            sumsq(X, "ple")
            turned("ple", "pleT_act", lambda k: vec("ln_ple", k))
            for n, i in enumerate(of["ple"]):
                wait_result(act, i)
                if n >= 2:
                    act.wait_ge(S("ple_x"), n - 1)
                nc.scalar.activation(SG[:, n % 2].rearrange("p t c -> p (t c)"), bank_of(i)[:, :], ACT.Sigmoid)\
                  .then_inc(S("emptied_act"), 1)
            act.wait_ge(S("ple_x"), 4)
            act.wait_ge(S("turned"), 4 * nth("ple", TURNS))
            sumsq(X, "two")
            for n, i in enumerate(of["zb"]):
                wait_result(act, i)
                nc.scalar.activation(ZB[:, :, 256 * n:256 * n + 256], bank_of(i)[:, :].rearrange("p (t c) -> p t c", t=TT),
                                     ACT.Sigmoid).then_inc(S("sig2"), 1)
            for name, dst in (("ga", GA), ("gb", GB)):
                for n, i in enumerate(of[name]):
                    wait_result(act, i)
                    nc.scalar.activation(dst[:, 2 * n:2 * n + 2, :].rearrange("p a t -> p (a t)"), bank_of(i)[:, :],
                                         ACT.Sigmoid).then_inc(S("emptied_act"), 1)
            for n, i in enumerate(of["za"]):
                wait_result(act, i)
                nc.scalar.activation(YA[:, 2 * n:2 * n + 2, :].rearrange("p a t -> p (a t)"), bank_of(i)[:, :],
                                     ACT.Sigmoid).then_inc(S("sig2"), 1)
            for n, i in enumerate(of["c"]):
                wait_result(act, i)
                nc.scalar.activation(UC[:, 2 * n:2 * n + 2, 1:T + 1], bank_of(i)[:, :].rearrange("p (a t) -> p a t", a=2),
                                     ACT.Copy).then_inc(S("emptied_act"), 1)
            for m, i in enumerate(of["q2"] + of["k2"]):
                wait_result(act, i)
                if m >= 2:
                    act.wait_ge(S("roped"), m - 1)
                nc.scalar.activation(RAW[:, m % 2, :], bank_of(i)[:, :], ACT.Copy).then_inc(S("emptied_act"), 1)
            act.wait_ge(S("conv"), 8)
            for n, i in enumerate(of["v2"]):
                wait_result(act, i)
                nc.scalar.activation(V2[:, :, 256 * n:256 * n + 256], bank_of(i)[:, :].rearrange("p (t c) -> p t c", t=TT),
                                     ACT.Copy).then_inc(S("emptied_act"), 1)
            act.wait_ge(S("roped"), 8)
            for n in range(H2 * TT):
                act.wait_ge(S("na_nmax"), n + 1)
                if n >= 2:
                    act.wait_ge(S("na_pT"), n - 1)
                nc.scalar.activation(PR2[:, n % 2, :], B[4 + n % 2][:, :], ACT.Exp, bias=NMX2[:, n % 2:n % 2 + 1],
                                     accum_out=SUM2[:, n % 2:n % 2 + 1]).then_inc(S("na_p"), 1)
                act.wait_ge(S("na_pT"), n + 1)
                if n >= 2:
                    act.wait_ge(S("na_pv"), n - 1)
                nc.scalar.activation(PT2[:, n % 2, :], B[6 + n % 2][:, :], ACT.Copy).then_inc(S("na_pt"), 1)
            for k in range(DK):
                if k % 2 == 0:
                    act.wait_ge(S("turned"), 4 * nth("o", TURNS) - 3 + k // 2)
                nc.scalar.activation(HT[:, k, :], B[4 + k // 2][:, (k % 2) * T:(k % 2) * T + T], ACT.Copy)\
                  .then_inc(S("oT"), 1)
            act.wait_ge(S("emptied_dve"), emptied[of["wo"][-1]][1])
            sumsq(YF, "y")

        M_TMP_K = area(M0, 4, TT, MH * 16)
        M_TMP_Q = area(M0 + 6720, 4, TT, MH * 16)

        def norm_rope(ve, link, s, tmp):
            x = QKM[:, s].rearrange("p t (h d) -> p (t h) d", h=MH)
            link(ve.tensor_tensor(x, x, over(RSH[:, 16 * s:16 * s + 16].unsqueeze(2), 16, QK), ALU.mult))
            link(ve.tensor_tensor(x, x, over(QKN[:, s:s + 1, :], 16, QK), ALU.mult))
            xr = QKM[:, s].rearrange("p t (h d) -> p t h d", h=MH)
            x1, x2 = xr[:, :, :, NOPE:NOPE + 16], xr[:, :, :, NOPE + 16:QK]
            tm = [tmp[:, j].rearrange("p t (h d) -> p t h d", h=MH) for j in range(4)]
            cs = over(CS.unsqueeze(2), TT, MH, 16)
            sn = over(SN.unsqueeze(2), TT, MH, 16)
            ve.tensor_tensor(tm[0], x1, cs, ALU.mult)
            ve.tensor_tensor(tm[1], x2, sn, ALU.mult)
            ve.tensor_tensor(tm[2], x2, cs, ALU.mult)
            link(ve.tensor_tensor(tm[3], x1, sn, ALU.mult))
            ve.tensor_tensor(x1, tm[0], tm[1], ALU.subtract)
            return ve.tensor_tensor(x2, tm[2], tm[3], ALU.add)

        @block.gpsimd
        def _(pool):
            def power(dst, src, n, tag):
                pool.wait_ge(S("mean_sq"), nth(tag))
                nc.gpsimd.tensor_tensor(dst, src, NHALF[:, 0:n], ALU.pow).then_inc(S("rms"), 1)

            nc.gpsimd.memset(NHALF, -0.5).then_inc(S("nhalf"), 1)
            pool.wait_ge(S("nhalf"), 1)
            power(rs["x"], ss["x"], 2, "x")
            power(RSL, SSL, 4, "lat")
            for t in range(TT):
                dst = QKM[:, 1, t].rearrange("p (h d) -> p h d", h=MH)
                if t == 0:
                    pool.wait_ge(S("emptied_act"), emptied[of["ukv"][-1]][1])
                    pool.wait_ge(S("emptied_dve"), emptied[of["ckv"][0]][1])
                nc.gpsimd.tensor_copy(dst[:, :, 0:NOPE], KV[:, t].rearrange("p (h d) -> p h d", h=MH)[:, :, 0:NOPE])
                ins = nc.gpsimd.tensor_copy(dst[:, :, NOPE:QK], over(CK[:, t, P:160].unsqueeze(1), MH, ROPE))
            ins.then_inc(S("km"), 1)
            power(RSH, SSH, 32, "qk")

            def chain(ins, name, n=[0]):
                n[0] += 1
                ins.then_inc(S(name), 1)
                pool.wait_ge(S(name), n[0])

            pool.wait_ge(S("km"), 1)
            pool.wait_ge(S("sumsq"), nth("qk"))
            pool.wait_ge(S("rms"), nth("qk"))
            pool.wait_ge(S("small_in"), SMALL)
            pool.wait_ge(S("sincos"), 1)
            norm_rope(nc.gpsimd, lambda ins: chain(ins, "pool_chain"), 1, M_TMP_K).then_inc(S("qk_pool"), 1)

            pool.wait_ge(S("mla_pv"), MH)
            pool.wait_ge(S("mla_o"), MH)
            pool.wait_ge(S("cum"), 1)
            for n, lv in enumerate(LEVELS[:-1]):
                if n >= 2:
                    pool.wait_ge(S("gla_s"), n - 1)
                dq, dk = DEC[:, n % 2, 0], DEC[:, n % 2, 1]
                fc = FC.rearrange("p h t -> p (h t)")
                bx = BX.rearrange("p h t -> p (h t)")
                if isinstance(lv, int):
                    m = lv

                    def halves(v):
                        v = v.rearrange("p (b two m) -> p b two m", two=2, m=m)
                        return v[:, :, 0, :], v[:, :, 1, :]

                    blocks = GH * T // (2 * m)
                    fl, fr = halves(fc)
                    bl, br = halves(bx)
                    qs = halves(dq)
                    ks = halves(dk)
                    f_edge = over(fl[:, :, m - 1:m], blocks, m)
                    b_edge = over(br[:, :, 0:1], blocks, m)
                    nc.gpsimd.tensor_tensor(qs[0], b_edge, bl, ALU.subtract)
                    nc.gpsimd.tensor_tensor(qs[1], fr, f_edge, ALU.subtract)
                    nc.gpsimd.tensor_tensor(ks[0], f_edge, fl, ALU.subtract)
                    nc.gpsimd.tensor_tensor(ks[1], br, b_edge, ALU.subtract).then_inc(S("gla_dec"), 1)
                else:
                    def blk(v):
                        return v.rearrange("p (b m) -> p b m", m=8)

                    if lv == "base_fwd":
                        ref = over(blk(fc)[:, :, 3:4], GH * T // 8, 8)
                        nc.gpsimd.tensor_tensor(blk(dq), blk(fc), ref, ALU.subtract)
                        nc.gpsimd.tensor_tensor(blk(dk), ref, blk(fc), ALU.subtract).then_inc(S("gla_dec"), 1)
                    else:
                        ref = over(blk(bx)[:, :, 4:5], GH * T // 8, 8)
                        nc.gpsimd.tensor_tensor(blk(dq), ref, blk(bx), ALU.subtract)
                        nc.gpsimd.tensor_tensor(blk(dk), blk(bx), ref, ALU.subtract).then_inc(S("gla_dec"), 1)
            power(RSO, SSO, 8, "o")
            power(rs["ctx"], ss["ctx"], 2, "ctx")
            power(rs["hm"], ss["hm"], 2, "hm")
            power(rs["ple"], ss["ple"], 2, "ple")
            power(rs["two"], ss["two"], 2, "two")
            pool.wait_ge(S("conv"), 8)

            def bias_dma(h):
                for t in range(TT):
                    for q in range(2):
                        at = (h * ROWS + 2 * t + q) * TOEP
                        src = bass.AP(a["toeplitz"].tensor, at, [[ROWS, GW], [1, T]])
                        pool.dma_start(BT[q * GW:q * GW + GW, h % 2, t, :], src).then_inc(S(f"bt{h % 2}"), 16)

            bias_dma(0)
            for h in range(H2):
                if h + 1 < H2:
                    bias_dma(h + 1)
                pool.wait_ge(S(f"bt{h % 2}"), 64 * (h // 2 + 1))
                for t in range(TT):
                    n = h * TT + t
                    if n >= 2:
                        pool.wait_ge(S("na_s"), n - 1)
                    nc.gpsimd.tensor_tensor(BM[:, n % 2, :].rearrange("p (r c) -> p c r", r=ROWS),
                                            BT[:, h % 2, t, :].rearrange("p (c r) -> p c r", r=ROWS),
                                            const("winmask").rearrange("p (c r) -> p c r", r=ROWS), ALU.add)\
                      .then_inc(S("bm"), 1)
                    pool.wait_ge(S("bm"), n + 1)
            power(rs["y"], ss["y"], 2, "y")

        @block.vector
        def _(dve):
            V_ = nc.vector
            links = [0]

            def link(ins):
                links[0] += 1
                ins.then_inc(S("dve_chain"), 1)
                dve.wait_ge(S("dve_chain"), links[0])

            def mean_sq(tag, n):
                v = ss[tag]
                dve.wait_ge(S("sumsq"), nth(tag))
                V_.tensor_scalar(v, v, 1.0 / n, EPS, ALU.mult, ALU.add).then_inc(S("mean_sq"), 1)

            def normalize(src, tag, dst=None):
                mean_sq(tag, D)
                dve.wait_ge(S("rms"), nth(tag))
                for t in range(TT):
                    o = HN[:, t, :] if dst is None else dst(t)
                    i_ = src[:, t, :] if dst is None else src[:, t, :].rearrange("p (q k) -> p k q", k=DK)
                    ins = V_.tensor_scalar(o, i_, rs[tag][:, t:t + 1], None, ALU.mult)
                ins.then_inc(S("normed"), 1)

            def turned(tag, done, gain, ks=range(4), bias=None):
                for k in ks:
                    if k % 2 == 0:
                        dve.wait_ge(S("turned"), 4 * nth(tag, TURNS) - 3 + k // 2)
                    src = B[4 + k // 2][:, (k % 2) * T:(k % 2) * T + T]
                    if bias is None:
                        V_.tensor_scalar(HT[:, k, :], src, gain(k), None, ALU.mult).then_inc(S(done), 1)
                    else:
                        V_.tensor_scalar(HT[:, k, :], src, gain(k), bias(k), ALU.mult, ALU.add).then_inc(S(done), 1)

            def tiles(i):
                return bank_of(i)[:, :].rearrange("p (t c) -> p t c", t=TT)

            dve.wait_ge(S("early_in"), EARLY)
            dve.wait_ge(S("early_in"), EARLY)
            link(V_.tensor_copy(POSF, POSI[:]))
            for t in range(TT):
                ins = V_.tensor_scalar(ANG[:, t, :], const("invfreq"), POSF[:, t:t + 1], None, ALU.mult)
            link(ins)
            magic = 1.5 * 2 ** 23
            link(V_.tensor_scalar(KQ, ANG, 1.0 / (2 * np.pi), magic, ALU.mult, ALU.add))
            link(V_.tensor_scalar(KQ, KQ, magic, None, ALU.subtract))
            c1 = 6.28125
            c2 = float(np.float32(2 * np.pi - c1))
            c3 = float(2 * np.pi - c1 - np.float64(np.float32(c2)))
            link(V_.scalar_tensor_tensor(out=RED, in0=KQ, scalar=-c1, in1=ANG, op0=ALU.mult, op1=ALU.add))
            link(V_.scalar_tensor_tensor(out=RED, in0=KQ, scalar=-c2, in1=RED, op0=ALU.mult, op1=ALU.add))
            link(V_.scalar_tensor_tensor(out=RED, in0=KQ, scalar=-c3, in1=RED, op0=ALU.mult, op1=ALU.add))
            link(V_.tensor_scalar(RED, RED, float(np.float32(3.1415925)), -float(np.float32(3.1415925)), ALU.min, ALU.max))
            link(V_.tensor_scalar(KQ, RED, -1.0, None, ALU.mult))
            link(V_.tensor_tensor(KQ, KQ, RED, ALU.max))
            V_.tensor_scalar(KQ, KQ, -1.0, float(np.pi / 2), ALU.mult, ALU.add).then_inc(S("ang"), 1)

            dve.wait_ge(S("masks_in"), 16)
            V_.tensor_copy(MSK[:].rearrange("p a b -> p (a b)"), HT[:, 0:3, :].rearrange("p a b -> p (a b)"))
            dve.wait_ge(S("vec_ps"), 1)
            V_.tensor_copy(VEC[:], B[4][:, 0:NVEC]).then_inc(S("vec"), 1)
            normalize(X, "x")
            dve.wait_ge(S("vec"), 1)
            at = VEC_ROWS["hg_lb"][0]
            lbv = VEC[:, at:at + 16].rearrange("p (d j r) -> p d j r", d=2, j=2)
            l0, l1 = lbv[:, :, 0, :], lbv[:, :, 1, :]
            V_.tensor_tensor(LBF.rearrange("p (d r) -> p d r", d=2), l0, l1, ALU.subtract).then_inc(S("lbd"), 1)
            V_.tensor_tensor(LBR.rearrange("p (d r) -> p d r", d=2), l1, l0, ALU.subtract).then_inc(S("lbd"), 1)
            V_.tensor_copy(CC[:, :, 0], vec("c_2", 0, 8))
            V_.tensor_copy(CC[:, :, 1], vec("c_ctx_2", 0, 8)).then_inc(S("cc"), 1)
            turned("x", "hT_dve", lambda k: vec("ln_mix", k))
            i = of["cq"][0]
            wait_result(dve, i)
            V_.tensor_copy(CQ[:, :, :], tiles(i)).then_inc(S("emptied_dve"), 1)
            i = of["ckv"][0]
            wait_result(dve, i)
            V_.tensor_copy(CK[:, :, :], tiles(i)[:, :, 0:160]).then_inc(S("emptied_dve"), 1)

            def silu_result(dst, i, sem, n):
                wait_result(dve, i)
                dve.wait_ge(S(sem), n)
                V_.tensor_tensor(dst, dst, bank_of(i)[:, :] if len(dst.shape) == 2 else tiles(i), ALU.mult)\
                  .then_inc(S("emptied_dve"), 1)

            for n, i in enumerate(of["q"]):
                silu_result(QT[:, 2 * n:2 * n + 2, :].rearrange("p a t -> p (a t)"), i, "sig", n + 1)
            dve.wait_ge(S("lb"), 1)
            dve.wait_ge(S("emptied_act"), emptied[of["f"][-1]][1])
            for c in range(8):
                ins = V_.tensor_scalar(SF[:, c, :], SF[:, c, :], LBR[:, c:c + 1], LBF[:, c:c + 1], ALU.mult, ALU.add)
            link(ins)
            link(V_.tensor_scalar(KF[:, :, :], SF[:, :, :], -1.0, 1.0, ALU.mult, ALU.add))
            V_.tensor_scalar(SF[:, :, :], SF[:, :, :], F_FLOOR, None, ALU.max).then_inc(S("fgate"), 1)
            for n, i in enumerate(of["og"]):
                silu_result(OG[:, :, 256 * n:256 * n + 256], i, "sig", n + 3)
            dve.wait_ge(S("sumsq"), nth("lat"))
            V_.tensor_scalar(SSL[:, 0:2], SSL[:, 0:2], 1.0 / QR, EPS, ALU.mult, ALU.add)
            V_.tensor_scalar(SSL[:, 2:4], SSL[:, 2:4], 1.0 / KVR, EPS, ALU.mult, ALU.add).then_inc(S("mean_sq"), 1)
            dve.wait_ge(S("rms"), nth("lat"))
            for t in range(TT):
                V_.tensor_scalar(CQ[:, t, :], CQ[:, t, :], RSL[:, t:t + 1], None, ALU.mult)
                ins = V_.tensor_scalar(CK[:, t, 0:P], CK[:, t, 0:P], RSL[:, 2 + t:3 + t], None, ALU.mult)
            ins.then_inc(S("normed"), 1)
            dve.wait_ge(S("lat_ps"), 1)
            for c in range(2):
                V_.tensor_scalar(CQT[:, c, :], B[4][:, c * T:c * T + T], vec("mla_qa_norm", c), None, ALU.mult)
            V_.tensor_scalar(CKT, B[5][:, 0:T], vec("mla_kva_norm"), None, ALU.mult).then_inc(S("latT"), 1)
            for n, i in enumerate(of["uq"]):
                wait_result(dve, i)
                V_.tensor_copy(QKM[:, 0, :, 256 * n:256 * n + 256], tiles(i)).then_inc(S("emptied_dve"), 1)
            dve.wait_ge(S("sumsq"), nth("qk"))
            link(V_.tensor_reduce(SSH, SQ.rearrange("p s a d -> p (s a) d"), AX_X, ALU.add))
            V_.tensor_scalar(SSH, SSH, 1.0 / QK, EPS, ALU.mult, ALU.add).then_inc(S("mean_sq"), 1)
            dve.wait_ge(S("rms"), nth("qk"))
            dve.wait_ge(S("small_in"), SMALL)
            dve.wait_ge(S("sincos"), 1)
            norm_rope(V_, link, 0, M_TMP_Q).then_inc(S("normed"), 1)
            dve.wait_ge(S("normed"), nth("qk"))
            for h in range(1, MH, 2):
                dve.wait_ge(S("qkT_ps"), h + 1)
                V_.tensor_copy(QKT[0:QK, h, :], B[4 + h % 4][0:QK, :]).then_inc(S("qkT_odd"), 1)
            scale = QK ** -0.5

            def mla_max(h):
                dve.wait_ge(S("mla_s"), h + 1)
                link(V_.tensor_reduce(MX[:, h % 2, :], B[4 + h % 2][:, :].rearrange("p (t k) -> p t k", t=TT), AX_X, ALU.max))
                if h >= 2:
                    dve.wait_ge(S("mla_p"), 2 * (h - 1))
                V_.tensor_scalar(NMX[:, h % 2, :], MX[:, h % 2, :], -scale, None, ALU.mult).then_inc(S("mla_nmax"), 1)

            mla_max(0)
            for h in range(MH):
                if h + 1 < MH:
                    mla_max(h + 1)
                dve.wait_ge(S("mla_p"), 2 * h + 2)
                link(V_.reciprocal(RSM[:, h % 2, :], SUM[:, h % 2, :]))
                dve.wait_ge(S("mla_pv"), h + 1)
                V_.tensor_tensor(OM[:, :, h * VD:h * VD + VD], B[h % 2][:, 0:TT * VD].rearrange("p (t v) -> p t v", t=TT),
                                 over(RSM[:, h % 2, :].unsqueeze(2), TT, VD), ALU.mult).then_inc(S("mla_o"), 1)
            dve.wait_ge(S("logf"), 1)
            for h in range(GH):
                V_.memset(BX[:, h, 0:1], 0.0)
                V_.tensor_tensor_scan(FC[:, h, :], const("ones"), SF[:, h, :], 0.0, ALU.mult, ALU.add)
                ins = V_.tensor_tensor_scan(BX[:, h, 1:T], const("ones")[:, 0:T - 1], SF[:, GH + h, 0:T - 1], 0.0,
                                            ALU.mult, ALU.add)
            ins.then_inc(S("cum"), 1)
            kfl = KF[:, 0:GH, :].rearrange("p h t -> p (h t)")
            kbl = KF[:, GH:2 * GH, :].rearrange("p h t -> p (h t)")
            qfl = QT.rearrange("p h t -> p (h t)")

            def gla_operands(n):
                lv = LEVELS[n]
                dq, dk = DEC[:, n % 2, 0], DEC[:, n % 2, 1]
                if lv == "diag":
                    dve.wait_ge(S("gla_s"), n - 1)
                    V_.tensor_tensor(dk, kfl, kbl, ALU.add).then_inc(S("gla_qk"), 1)
                    return
                dve.wait_ge(S("gla_exp"), n + 1)
                V_.tensor_tensor(dq, dq, qfl, ALU.mult)
                if isinstance(lv, int):
                    def halves(v):
                        v = v.rearrange("p (b two m) -> p b two m", two=2, m=lv)
                        return v[:, :, 0, :], v[:, :, 1, :]
                    (dl, dr), (kl, _), (_, kr) = halves(dk), halves(kfl), halves(kbl)
                    V_.tensor_tensor(dl, dl, kl, ALU.mult)
                    ins = V_.tensor_tensor(dr, dr, kr, ALU.mult)
                else:
                    ins = V_.tensor_tensor(dk, dk, kfl if lv == "base_fwd" else kbl, ALU.mult)
                ins.then_inc(S("gla_qk"), 1)

            def gla_scores(n):
                lv = LEVELS[n]
                dve.wait_ge(S("gla_s"), n + 1)
                if n:
                    dve.wait_ge(S("gla_a"), n)
                for st in range(TT):
                    bank = B[2 * (n % 4) + st][:, :].rearrange("p (h t) -> p h t", h=GH)
                    if lv == 128:
                        ins = V_.tensor_copy(AXX[:, st], bank)
                    elif lv == 64:
                        ins = V_.tensor_copy(AD[:, st], bank)
                    else:
                        ins = V_.copy_predicated(AD[:, st], over(MSK[:, MASK_OF[lv]:MASK_OF[lv] + 1, :], GH, P), bank)
                ins.then_inc(S("gla_a"), 1)

            gla_operands(0)
            for n in range(len(LEVELS)):
                if n + 1 < len(LEVELS):
                    gla_operands(n + 1)
                gla_scores(n)
            dve.wait_ge(S("gla_o_ps"), 1)
            for tt in range(TT):
                ins = V_.tensor_copy(OO[:, tt], B[tt][:, :].rearrange("p (h v) -> p h v", h=GH))
            ins.then_inc(S("gla_o"), 1)
            dve.wait_ge(S("sumsq"), nth("o"))
            link(V_.tensor_reduce(SSO, OSQ, AX_X, ALU.add))
            V_.tensor_scalar(SSO, SSO, 1.0 / GK, EPS, ALU.mult, ALU.add).then_inc(S("mean_sq"), 1)
            dve.wait_ge(S("rms"), nth("o"))
            dve.wait_ge(S("small_in"), SMALL)
            oo = OO.rearrange("p t h v -> p (t h) v")
            link(V_.tensor_tensor(oo, oo, over(RSO.unsqueeze(2), 8, GK), ALU.mult))
            link(V_.tensor_tensor(oo, oo, over(ONB[:].unsqueeze(1), 8, GK), ALU.mult))
            oo2 = OO.rearrange("p t h v -> p (t h v)")
            V_.tensor_tensor(oo2, oo2, OG.rearrange("p t c -> p (t c)"), ALU.mult).then_inc(S("normed"), 1)
            def pair(base, n):
                return GATE[:, base + 2 * n:base + 2 * n + 2, :].rearrange("p a t -> p (a t)")
            dve.wait_ge(S("emptied_act"), emptied[of["gate"][-1]][1])
            for n, i in enumerate(of["yb"]):
                wait_result(dve, i)
                V_.tensor_tensor(pair(8, n), pair(8, n), bank_of(i)[:, :], ALU.mult).then_inc(S("emptied_dve"), 1)
            for n, i in enumerate(of["ya"]):
                wait_result(dve, i)
                V_.tensor_tensor(pair(0, n), pair(0, n), bank_of(i)[:, :], ALU.mult).then_inc(S("emptied_dve"), 1)
                dve.wait_ge(S("emptied_dve"), emptied[i][1])
                V_.tensor_tensor(pair(0, n), pair(0, n), pair(8, n), ALU.add).then_inc(S("merged"), 1)
            for n, i in enumerate(of["out"]):
                wait_result(dve, i)
                xs = X[:, :, 256 * n:256 * n + 256]
                V_.tensor_tensor(xs, xs, tiles(i), ALU.add).then_inc(S("emptied_dve"), 1)
            dve.wait_ge(S("sig_c"), 1)
            V_.tensor_tensor(CC[:, :, 0], CC[:, :, 0], vec("c_2", 0, 8), ALU.mult)
            V_.tensor_tensor(CC[:, :, 1], CC[:, :, 1], vec("c_ctx_2", 0, 8), ALU.mult).then_inc(S("silu_c"), 1)
            dve.wait_ge(S("silu_c"), 1)
            V_.tensor_copy(SCB[:, :, :], over(CC[:, :, 0:1], DK, P)).then_inc(S("silu_cb"), 1)
            for n, i in enumerate(of["mod"]):
                wait_result(dve, i)
                V_.tensor_tensor(MODT[:, 2 * n:2 * n + 2, :], bank_of(i)[:, 0:4].rearrange("p (a b) -> p a b", a=2),
                                 over(vec("b_mod_2", 2 * n, 2).unsqueeze(2), 2, 2), ALU.add).then_inc(S("emptied_dve"), 1)
            dve.wait_ge(S("emptied_dve"), emptied[of["mod"][-1]][1])
            for s in range(2):
                ins = V_.tensor_scalar(ACOL[:, s, :], MODT[:, 8:16, s], 1.0, None, ALU.add)
            link(ins)
            for s in range(2):
                ins = V_.tensor_tensor(ACOL[:, s, :], ACOL[:, s, :], vec("pre_g_2", 0, 8), ALU.mult)
            link(ins)
            dve.wait_ge(S("bgt_in"), 16)
            for n, i in enumerate(of["gt"]):
                wait_result(dve, i)
                bs = BGT[:, 256 * n:256 * n + 256]
                V_.tensor_tensor(bs, bs, bank_of(i)[:, 0:256], ALU.add).then_inc(S("emptied_dve"), 1)
            dve.wait_ge(S("emptied_dve"), emptied[of["gt"][-1]][1])
            dve.wait_ge(S("small_in"), SMALL)
            link(V_.tensor_tensor(PG[:], PG[:], BGT, ALU.mult))
            mean_sq("ctx", D)
            dve.wait_ge(S("rms"), nth("ctx"))
            for t in range(TT):
                ins = V_.tensor_scalar(HN[:, t, :], HN[:, t, :], rs["ctx"][:, t:t + 1], None, ALU.mult)
            ins.then_inc(S("normed"), 1)
            dve.wait_ge(S("emptied_dve"), emptied[of["out"][-1]][1])
            turned("ctx", "cT_dve", lambda k: ACOL[:, 1, k:k + 1], range(DK), lambda k: MODT[:, k, 1:2])
            dve.wait_ge(S("pT_ps"), 1)
            V_.tensor_copy(PTR.rearrange("p a t -> p (a t)"), B[4][:, :]).then_inc(S("pT"), 1)

            normalize(X, "hm", lambda t: HN[:, t, :].rearrange("p (k q) -> p k q", k=DK))
            dve.wait_ge(S("small_in"), SMALL)
            turned("hm", "rT_dve", lambda k: LNM[:, k:k + 1])
            dve.wait_ge(S("logits_ps"), 1)
            dve.wait_ge(S("small_in"), SMALL)
            link(V_.tensor_tensor(LGT, B[4][:, 0:144].rearrange("p (t c) -> p t c", t=TT), over(RB[:].unsqueeze(1), TT, 72),
                                  ALU.add))
            g = LGT[:, :, 0:8]
            rev = over(const("rev8").unsqueeze(1), TT, 8)

            def first_max(v, mx, onehot):
                link(V_.tensor_reduce(mx, v, AX_X, ALU.max))
                link(V_.tensor_tensor(VAL, v, over(mx.unsqueeze(2), TT, 8), ALU.is_equal))
                link(V_.tensor_tensor(VAL, VAL, rev, ALU.mult))
                link(V_.tensor_reduce(VMX, VAL, AX_X, ALU.max))
                return V_.tensor_tensor(onehot, VAL, over(VMX.unsqueeze(2), TT, 8), ALU.is_equal)

            first_max(g, GMX, GOH).then_inc(S("group"), 1)
            V_.tensor_tensor(GEXP, g, over(GMX.unsqueeze(2), TT, 8), ALU.subtract).then_inc(S("gdiff"), 1)
            dve.wait_ge(S("group"), 1)
            for t in range(TT):
                link(V_.tensor_tensor(GEX, LGT[:, t, 8:72].rearrange("p (g e) -> p g e", g=NG),
                                      over(GOH[:, t, :].unsqueeze(2), NG, EPG), ALU.mult))
                link(V_.tensor_reduce(EL[:, t, :], GEX.rearrange("p g e -> p e g"), AX_X, ALU.add))
            link(first_max(EL, M1, O1))
            link(V_.scalar_tensor_tensor(out=EL2, in0=O1, scalar=-1e30, in1=EL, op0=ALU.mult, op1=ALU.add))
            link(first_max(EL2, M2, O2))
            V_.tensor_tensor(DLT, M2, M1, ALU.subtract).then_inc(S("ediff"), 1)
            dve.wait_ge(S("gexp"), 1)
            link(V_.tensor_reduce(GSM, GEXP, AX_X, ALU.add))
            link(V_.reciprocal(PGR, GSM))
            dve.wait_ge(S("eexp"), 1)
            link(V_.tensor_scalar(DEN, E2W, 1.0, None, ALU.add))
            link(V_.reciprocal(W1, DEN))
            link(V_.tensor_tensor(W1, W1, PGR, ALU.mult))
            link(V_.tensor_tensor(W2, W1, E2W, ALU.mult))
            link(V_.tensor_tensor(O1, O1, over(W1.unsqueeze(2), TT, 8), ALU.mult))
            link(V_.tensor_tensor(O2, O2, over(W2.unsqueeze(2), TT, 8), ALU.mult))
            link(V_.tensor_tensor(WT, O1, O2, ALU.add))
            V_.tensor_copy(WTB, over(WT.rearrange("p t e -> p (t e)").unsqueeze(2), 16, P))
            dve.wait_ge(S("rank_ps"), 1)
            V_.tensor_copy(RK, B[5][:, 0:16].rearrange("p (t g) -> p t g", t=TT))
            link(V_.tensor_copy(CNT, B[5][:, 16:24]))
            link(V_.tensor_scalar(NR, CNT, 0.5, None, ALU.is_gt))
            for lot in range(1, T // SLOT):
                link(V_.scalar_tensor_tensor(out=NR, in0=CNT, scalar=SLOT * lot + 0.5, in1=NR, op0=ALU.is_gt, op1=ALU.add))
            link(V_.tensor_scalar(NR[:, 0:1], NR[:, 0:1], 1.0, None, ALU.max))
            link(V_.tensor_tensor_scan(ENDS, const("ones")[:, 0:8], NR, 0.0, ALU.mult, ALU.add))
            link(V_.tensor_tensor(STA, ENDS, NR, ALU.subtract))
            link(V_.scalar_tensor_tensor(out=RK, in0=over(STA.unsqueeze(1), TT, 8), scalar=float(SLOT), in1=RK,
                                         op0=ALU.mult, op1=ALU.add))
            link(V_.tensor_tensor(RK, RK, GOH, ALU.mult))
            link(V_.tensor_reduce(POS, RK, AX_X, ALU.add))
            link(V_.tensor_tensor(TAB, over(ENDS.unsqueeze(1), ROUNDS, 8), over(const("round_id").unsqueeze(2), ROUNDS, 8),
                                  ALU.is_le))
            link(V_.tensor_reduce(TABR, TAB, AX_X, ALU.add))
            link(V_.tensor_scalar(TABR, TABR, float(NG - 1), None, ALU.min))
            V_.tensor_copy(RT[:, 1:1 + ROUNDS], TABR)
            V_.tensor_scalar(RT[:, 14:15], ENDS[:, 7:8], float(NM), float(-RING), ALU.mult, ALU.add)
            V_.tensor_copy(RT[:, 0:1], ENDS[:, 7:8]).then_inc(S("table"), 1)
            dve.wait_ge(S("table"), 1)

            def moe_round(r):
                def at(n, k):
                    return r * n + k

                for t in range(TT):
                    ins = V_.tensor_scalar(SEL[:, t, :], const("iota_slot"), POS[:, t:t + 1], None, ALU.is_equal)
                ins.then_inc(S("sel"), 1)
                dve.wait_ge(S("sel"), at(1, 1))
                V_.tensor_scalar(POS, POS, float(SLOT), None, ALU.subtract).then_inc(S("pos_next"), 1)
                dve.wait_ge(S("gath_ps"), at(1, 1))
                V_.tensor_tensor(XG, B[0][:, :].rearrange("p (k s) -> p k s", k=DK), over(LNM[:].unsqueeze(2), DK, SLOT),
                                 ALU.mult).then_inc(S("gath"), 1)
                dve.wait_ge(S("wb"), at(1, 1))
                for e in range(EPG):
                    bank = B[3 + e % 2]
                    dve.wait_ge(S("moe_sig"), at(EPG, e + 1))
                    V_.tensor_tensor(SGM[:, e % 2].rearrange("p c s -> p (c s)"), SGM[:, e % 2].rearrange("p c s -> p (c s)"),
                                     bank[:, 0:2 * SLOT], ALU.mult)
                    V_.tensor_tensor(H3W[:, e % 2], bank[:, 2 * SLOT:4 * SLOT].rearrange("p (c s) -> p c s", c=2),
                                     over(WB[:, e:e + 1, :], 2, SLOT), ALU.mult).then_inc(S("moe_h3"), 1)
                    dve.wait_ge(S("moe_h3"), at(EPG, e + 1))
                    V_.tensor_tensor(HH[:, e % 2], SGM[:, e % 2], H3W[:, e % 2], ALU.mult).then_inc(S("hh"), 1)
                dve.wait_ge(S("scat_ps"), at(1, 1))
                for t in range(TT):
                    for half in range(2):
                        xs = X[:, t, half * 512:half * 512 + 512]
                        ins = V_.tensor_tensor(xs, xs, B[2 * t + half][:, :], ALU.add)
                ins.then_inc(S("moe_x"), 1)
                dve.wait_ge(S("moe_x"), at(1, 1))

            moe_round(0)
            rounds = dve.value_load(RT[0:1, 0:1], min_val=4, max_val=ROUNDS)
            with dve.Fori(1, rounds) as r:
                moe_round(r)

            normalize(X, "ple")
            turned("ple", "pleT_dve", lambda k: vec("ln_ple", k))
            for n, i in enumerate(of["ple"]):
                dve.wait_ge(S("emptied_act"), emptied[i][1])
                link(V_.tensor_tensor(SG[:, n % 2], SG[:, n % 2], PP[:, :, 256 * n:256 * n + 256], ALU.mult))
                xs = X[:, :, 256 * n:256 * n + 256]
                V_.tensor_tensor(xs, xs, SG[:, n % 2], ALU.add).then_inc(S("ple_x"), 1)
            normalize(X, "two")
            turned("two", "twoT", lambda k: ACOL[:, 0, k:k + 1], range(DK), lambda k: MODT[:, k, 0:1])
            for n, i in enumerate(of["zb"]):
                silu_result(ZB[:, :, 256 * n:256 * n + 256], i, "sig2", n + 1)
            V_.memset(UC[:, :, 0:1], 0.0)
            V_.memset(UC[:, :, T + 1:T + 2], 0.0)

            def two(tile, n):
                return tile[:, 2 * n:2 * n + 2, :].rearrange("p a t -> p (a t)")

            for n, i in enumerate(of["za"]):
                silu_result(two(YA, n), i, "sig2", n + 5)
            for n, i in enumerate(of["b"]):
                wait_result(dve, i)
                dve.wait_ge(S("emptied_dve"), emptied[of["za"][n]][1])
                V_.tensor_tensor(two(YA, n), two(YA, n), bank_of(i)[:, :], ALU.mult).then_inc(S("emptied_dve"), 1)
            for n, i in enumerate(of["xin"]):
                wait_result(dve, i)
                dve.wait_ge(S("emptied_act"), emptied[of["c"][n]][1])
                u = UC[:, 2 * n:2 * n + 2, 1:T + 1]
                V_.tensor_tensor(u, u, bank_of(i)[:, :].rearrange("p (a t) -> p a t", a=2), ALU.mult)\
                  .then_inc(S("emptied_dve"), 1)
            dve.wait_ge(S("emptied_dve"), emptied[of["xin"][-1]][1])

            def conv_chunk(k):
                cv = V2[:, k % 2, 0:T]
                link(V_.tensor_scalar(cv, UC[:, k, 0:T], vec("conv_w_2", k), vec("conv_b_2", k), ALU.mult, ALU.add))
                link(V_.scalar_tensor_tensor(out=cv, in0=UC[:, k, 1:T + 1], scalar=vec("conv_w_2", 8 + k), in1=cv,
                                             op0=ALU.mult, op1=ALU.add))
                link(V_.scalar_tensor_tensor(out=cv, in0=UC[:, k, 2:T + 2], scalar=vec("conv_w_2", 16 + k), in1=cv,
                                             op0=ALU.mult, op1=ALU.add))
                return V_.tensor_tensor(YA[:, k, :], YA[:, k, :], cv, ALU.mult)

            for m in range(8):
                conv_chunk(m).then_inc(S("conv"), 1)
                s = 1.0 if m >= 4 else HD ** -0.5
                dst = two(QT2 if m < 4 else KT2, m % 4)
                i = (of["q2"] + of["k2"])[m]
                dve.wait_ge(S("rot_ps"), m + 1)
                d3 = dst.rearrange("p (a t) -> p a t", a=2)
                V_.tensor_tensor(d3, B[4 + m % 2][:, :].rearrange("p (a t) -> p a t", a=2),
                                 over(const("sinT").unsqueeze(1), 2, T), ALU.mult)
                raw = RAW[:, m % 2, :].rearrange("p (a t) -> p a t", a=2)
                link(V_.tensor_tensor(RTM[:, m % 2, :].rearrange("p (a t) -> p a t", a=2), raw,
                                      over(const("cosT").unsqueeze(1), 2, T), ALU.mult))
                if m >= 4:
                    V_.tensor_tensor(dst, dst, RTM[:, m % 2, :], ALU.add).then_inc(S("roped"), 1)
                else:
                    link(V_.tensor_tensor(dst, dst, RTM[:, m % 2, :], ALU.add))
                    V_.tensor_scalar(dst, dst, s, None, ALU.mult).then_inc(S("roped"), 1)

            def na_max(n):
                dve.wait_ge(S("na_s"), n + 1)
                bank = B[4 + n % 2]
                link(V_.tensor_reduce(MX2[:, n % 2:n % 2 + 1], bank[:, :], AX_X, ALU.max))
                if n >= 2:
                    dve.wait_ge(S("na_p"), n - 1)
                V_.tensor_scalar(NMX2[:, n % 2:n % 2 + 1], MX2[:, n % 2:n % 2 + 1], -1.0, None, ALU.mult)\
                  .then_inc(S("na_nmax"), 1)

            na_max(0)
            for n in range(H2 * TT):
                h, t = divmod(n, TT)
                if n + 1 < H2 * TT:
                    na_max(n + 1)
                dve.wait_ge(S("na_p"), n + 1)
                link(V_.reciprocal(RSM2[:, n % 2:n % 2 + 1], SUM2[:, n % 2:n % 2 + 1]))
                dve.wait_ge(S("na_pv"), n + 1)
                V_.scalar_tensor_tensor(out=HN[:, t, h * HD:h * HD + HD], in0=B[n % 2][:, 0:HD],
                                        scalar=RSM2[:, n % 2:n % 2 + 1], in1=ZB[:, t, h * HD:h * HD + HD],
                                        op0=ALU.mult, op1=ALU.mult).then_inc(S("na_o"), 1)
            for n, i in enumerate(of["yconv"]):
                wait_result(dve, i)
                V_.tensor_tensor(two(GA, n), two(GA, n), bank_of(i)[:, :], ALU.mult).then_inc(S("emptied_dve"), 1)
            for n, i in enumerate(of["yattn"]):
                wait_result(dve, i)
                V_.tensor_tensor(two(GB, n), two(GB, n), bank_of(i)[:, :], ALU.mult).then_inc(S("emptied_dve"), 1)
                dve.wait_ge(S("emptied_dve"), emptied[i][1])
                V_.tensor_tensor(two(GA, n), two(GA, n), two(GB, n), ALU.add).then_inc(S("merged2"), 1)
            for n, i in enumerate(of["wo"]):
                wait_result(dve, i)
                V_.tensor_copy(YF[:, :, 256 * n:256 * n + 256], tiles(i)).then_inc(S("emptied_dve"), 1)
            mean_sq("y", D)
            dve.wait_ge(S("rms"), nth("y"))
            for t in range(TT):
                link(V_.scalar_tensor_tensor(out=YF[:, t, :], in0=YF[:, t, :], scalar=rs["y"][:, t:t + 1], in1=PG[:],
                                             op0=ALU.mult, op1=ALU.mult))
                V_.tensor_tensor(HN[:, t, :], YF[:, t, :], X[:, t, :], ALU.add).then_inc(S("final"), 1)


_NAMES = ["x", "p", "positions", "ln_mix", "w_in", "hg_lb", "hg_onorm", "w_oA", "mla_qa_norm", "mla_kva_norm", "w_uq",
          "w_ukv", "q_norm", "k_norm", "w_oB", "w_out", "ln_moe", "w_rg", "b_rg", "w_re", "b_re", "w1", "w3", "w2",
          "ln_ple", "w_ple_gate", "w_ple_proj", "c_2", "ctx_2", "c_ctx_2", "w_mod_2", "b_mod_2", "pre_g_2", "post_g_2",
          "w_in_2", "conv_w_2", "conv_b_2", "w_out_conv_2", "w_out_attn_2", "w_o_2"]


def kernel(**inputs):
    import concourse.bacc as bacc
    from concourse.bass_utils import run_bass_kernel_spmd

    nc = bacc.Bacc("TRN2", target_bir_lowering=False, num_devices=1)
    arrays = {n: np.ascontiguousarray(inputs[n]) for n in _NAMES}
    rpb = np.asarray(inputs["rpb_2"])[0]
    table = np.zeros((H2, ROWS, 2 * GW - 1, ROWS), rpb.dtype)
    for qr in range(ROWS):
        table[:, qr, GW - WIN:GW + WIN - 1, :] = rpb[:, 7 - qr:7 - qr + ROWS, :].transpose(0, 2, 1)
    arrays["toeplitz"] = table.reshape(-1)
    arrays["consts"], arrays["masks"] = constants()
    a, maps = {}, {}
    for n, v in arrays.items():
        maps["in_" + n] = v
        a[n] = nc.dram_tensor("in_" + n, v.shape, mybir.dt.from_np(v.dtype), kind="ExternalInput").ap()
    out = nc.dram_tensor("out", (1, T, D), F32, kind="ExternalOutput").ap()
    build(nc, a, out)
    r = run_bass_kernel_spmd(nc, [maps], core_ids=[0])
    return r.results[0]["out"]
```

```python
from contextlib import ExitStack

import numpy as np

import concourse.bass as bass
from concourse import mybir

F32 = mybir.dt.float32
I32 = mybir.dt.int32
U8 = mybir.dt.uint8
ALU = mybir.AluOpType
ACT = mybir.ActivationFunctionType
AX_X = mybir.AxisListType.X

P = 128
T = 256
TT = T // P
D = 1024
DK = D // P
EPS = 1e-6

GH, GK = 4, 128
F_FLOOR = float(np.exp(-20.0))
MH, NOPE, ROPE, VD = 8, 64, 32, 64
QK = NOPE + ROPE
QR, KVR = 256, 128
NG, EPG = 8, 8
FE = 256
SLOT = 64
ROUNDS = (T - NG) // SLOT + NG
COL_Q, COL_FF, COL_FB, COL_V, COL_OG = 0, 512, 1024, 1536, 2048
COL_CQ, COL_CKV, COL_GA, COL_GB = 2560, 2816, 2976, 4000

H2, HD = 16, 64
GW, ROWS, WIN = 64, 4, 16
C_B, C_C, C_X, C_ZA, C_Q, C_K, C_V, C_ZB, C_GA, C_GB = [1024 * i for i in range(10)]
TOEP = (2 * GW - 1) * ROWS

RING = 8
LEVELS = [128, 64, 32, 16, 8, "base_fwd", "base_bwd", "diag"]
GLA_BANKS = (0, 4, 6)
MASK_OF = {32: 0, 16: 1, 8: 2, "base_fwd": 3, "base_bwd": 4, "diag": 5}

VEC_ROWS, _at = {}, 0
for _name, _n in (("pre_g_2", 8), ("b_mod_2", 16), ("conv_w_2", 24), ("conv_b_2", 8), ("c_2", 8), ("c_ctx_2", 8),
                  ("ln_mix", 8), ("ln_ple", 8), ("mla_qa_norm", 2), ("mla_kva_norm", 1), ("hg_lb", 16)):
    VEC_ROWS[_name] = (_at, _n)
    _at += _n
NVEC = _at

CONST_COLS, _at = {}, 0
for _name, _n in (("ident", 128), ("ustrict", 128), ("ones", 256), ("rot", 128), ("cosT", 256), ("sinT", 256),
                  ("winmask", 256), ("flip", 128), ("invfreq", 16), ("iota_slot", 128), ("rev8", 8), ("pick2", 2), ("row0", 128), ("round_id", ROUNDS)):
    CONST_COLS[_name] = (_at, _n)
    _at += _n
NCONST = _at


def constants():
    c = np.zeros((P, NCONST), np.float32)

    def put(name, value):
        a, n = CONST_COLS[name]
        c[:, a:a + n] = value

    i = np.arange(P)
    put("ident", np.eye(P))
    put("ustrict", i[:, None] < i[None, :])
    put("ones", 1.0)
    rot = np.zeros((P, P))
    for r in range(P):
        if (r % 32) < 16:
            rot[r + 16, r] = -1.0
        else:
            rot[r - 16, r] = 1.0
    put("rot", rot)
    half = HD // 2
    inv = 10000.0 ** (-np.arange(0, half, 2, dtype=np.float32) / np.float32(half))
    t = np.arange(T)
    d = np.arange(P) % HD
    where = np.where(d[:, None] < 32, (t // GW)[None, :], (t % GW)[None, :]).astype(np.float32)
    ang = where * inv.astype(np.float32)[d % 16][:, None]
    put("cosT", np.cos(ang.astype(np.float64)))
    put("sinT", np.sin(ang.astype(np.float64)))
    qc = GW - 1 - i % GW
    put("flip", (i[:, None] // GW == i[None, :] // GW) & (i[:, None] % GW == GW - 1 - i[None, :] % GW))
    start = np.clip(qc - WIN // 2, 0, GW - WIN)
    kc = np.arange(T) // ROWS
    inside = (kc[None, :] >= start[:, None]) & (kc[None, :] < start[:, None] + WIN)
    put("winmask", np.where(inside, 0.0, -1e30))
    put("invfreq", 10000.0 ** (-np.arange(16, dtype=np.float32) / np.float32(16)))
    put("iota_slot", np.arange(P) % SLOT)
    put("rev8", 8 - np.arange(8))
    put("pick2", i[:, None] % 32 == np.arange(2)[None, :])
    put("row0", (i % 32 == 0)[:, None])
    put("round_id", np.arange(ROUNDS))
    m = np.zeros((P, 6, P), np.float32)
    s, t2 = i[:, None], i[None, :]
    m[:, 0] = s // 64 == t2 // 64
    m[:, 1] = s // 32 == t2 // 32
    m[:, 2] = s // 16 == t2 // 16
    m[:, 3] = s // 8 == t2 // 8
    m[:, 4] = (s // 8 == t2 // 8) & (s > t2)
    m[:, 5] = s == t2
    return c, m


def build(nc, a, out):
    with ExitStack() as ctx:
        sems = {}

        def S(name):
            if name not in sems:
                sems[name] = ctx.enter_context(nc.semaphore(name))
            return sems[name]

        def sb(name, shape, dt=F32):
            return ctx.enter_context(nc.sbuf_tensor(name, shape, dt))

        ring = sb("ring", [P, RING, 2048])
        X = sb("X", [P, TT, D])
        HN = sb("HN", [P, TT, D])
        HT = sb("HT", [P, DK, T])
        CST = sb("CST", [P, NCONST])
        MSK = sb("MSK", [P, 6, P], U8)
        VROW = sb("VROW", [P, P])
        VEC = sb("VEC", [P, NVEC])
        QKN = sb("QKN", [P, 2, QK])
        ONB = sb("ONB", [P, GK])
        RB = sb("RB", [P, 72])
        RW = sb("RW", [P, DK, 72])
        LNM = sb("LNM", [P, DK])
        PG = sb("PG", [P, D])
        POSI = sb("POSI", [P, TT], I32)
        SM = sb("SM", [P, 1200])
        RT = sb("RT", [P, 16], I32)
        sm_at = [0]

        def small(*shape):
            n = int(np.prod(shape))
            v = SM[:, sm_at[0]:sm_at[0] + n]
            sm_at[0] += n
            if len(shape) == 2:
                v = v.rearrange("p (a b) -> p a b", a=shape[0])
            if len(shape) == 3:
                v = v.rearrange("p (a b c) -> p a b c", a=shape[0], b=shape[1])
            return v

        AR = sb("AR", [P, 25152])

        def area(at, *shape):
            n = int(np.prod(shape))
            assert at + n <= 25152, (at, shape)
            v = AR[:, at:at + n]
            if len(shape) == 2:
                v = v.rearrange("p (a b) -> p a b", a=shape[0])
            if len(shape) == 3:
                v = v.rearrange("p (a b c) -> p a b c", a=shape[0], b=shape[1])
            if len(shape) == 4:
                v = v.rearrange("p (a b c d) -> p a b c d", a=shape[0], b=shape[1], c=shape[2])
            return v

        def const(name):
            at, n = CONST_COLS[name]
            return CST[:, at:at + n]

        def vec(name, k=0, n=1):
            at = VEC_ROWS[name][0] + k
            return VEC[:, at:at + n]

        def over(ap, *shape):
            return ap.to_broadcast([P] + list(shape))

        ident = const("ident")
        QT = area(0, GH, T)
        SF = area(1024, 2 * GH, T)
        KF = area(3072, 2 * GH, T)
        V = area(5120, TT, 512)
        OG = area(6144, TT, 512)
        GATE = area(7168, 16, T)
        OM = area(11264, TT, 512)
        M0 = 12288
        CQ = area(M0, TT, QR)
        CK = area(M0 + 512, TT, 160)
        CQT = area(M0 + 832, 2, T)
        CKT = area(M0 + 1344, T)
        KV = area(M0 + 1600, TT, D)
        QKM = area(M0 + 3648, 2, TT, MH * QK)
        QKT = area(M0 + 6720, MH, 512)
        SQ = area(M0 + 6720, 2, TT * MH, QK)
        PR = area(M0 + 10816, 2, TT, T)
        PT = area(M0 + 11840, 2, TT, T)
        FC = area(M0, GH, T)
        BX = area(M0 + 1024, GH, T)
        DEC = area(M0 + 2048, 2, 2, GH * T)
        AD = area(M0 + 6144, 2, GH, P)
        AXX = area(M0 + 7168, 2, GH, P)
        OO = area(M0 + 8192, TT, GH, GK)
        OSQ = area(M0, TT * GH, GK)
        OTG = area(M0 + 2048, GH, T)
        OTM = area(M0 + 3072, GH, T)
        KC = area(1024, DK, T)
        VC = area(M0 + 10816, TT, D)
        PP = area(3072, TT, D)
        PRAW = area(5120, TT, T)
        PTR = area(5632, 2, T)
        CSQ = area(M0 + 6720, TT, D)
        BGT = area(M0 + 10816, D)
        MRW = area(M0 + 11840, 2, 256)
        E0 = 6144
        SEL = area(E0, TT, P)
        XG = area(E0 + 256, DK, SLOT)
        STR = area(E0 + 768, T)
        SGM = area(E0 + 1024, 2, FE)
        HHR = area(E0 + 1536, 2, FE)
        HHT = area(E0 + 2048, 2, 2, P)
        YY = area(E0 + 2560, 512)
        LGT = area(E0 + 5760, TT, 72)
        GEX = area(E0 + 5904, NG, EPG)
        SG = area(E0, 2, TT, T)
        E0 = 3072
        GA = area(E0, DK, T)
        GB = area(E0 + 2048, DK, T)
        ZB = area(E0 + 4096, TT, D)
        YA = area(E0 + 6144, DK, T)
        UC = area(E0 + 8192, DK, T + 2)
        BT = area(E0 + 8192, 2, TT, T)
        BM = area(E0 + 9216, 2, T)
        QT2 = area(E0 + 10256, DK, T)
        KT2 = area(E0 + 12304, DK, T)
        V2 = area(E0 + 14352, TT, D)
        RAW = area(E0 + 16400, 2, 512)
        RTM = area(E0 + 17424, 2, 512)
        PR2 = area(E0 + 16400, 2, 512)
        PT2 = area(E0 + 17424, 2, 512)
        YF = area(E0 + 10256, TT, D)

        MODT = small(16, 2)
        CC = small(DK, 32)
        CSG = small(DK, 2)
        ACOL = small(2, DK)
        LBF = small(8)
        LBR = small(8)
        NHALF = small(32)
        ss = {n: small(2) for n in ("x", "hm", "ctx", "ple", "two", "y")}
        rs = {n: small(2) for n in ss}
        SSL, RSL = small(4), small(4)
        SSH, RSH = small(32), small(32)
        SSO, RSO = small(8), small(8)
        ANG, CS, SN = small(TT, 16), small(TT, 16), small(TT, 16)
        POSF, KQ, RED = small(2), small(TT, 16), small(TT, 16)
        MX, NMX, SUM, RSM = small(2, 2), small(2, 2), small(2, 2), small(2, 2)
        MX2, NMX2, SUM2, RSM2 = small(2), small(2), small(2), small(2)
        GMX, GEXP, GSM, PGR = small(2), small(TT, 8), small(2), small(2)
        VAL, VMX, GOH = small(TT, 8), small(2), small(TT, 8)
        EL, EL2, M1, M2, O1, O2 = small(TT, 8), small(TT, 8), small(2), small(2), small(TT, 8), small(TT, 8)
        DLT, E2W, DEN, W1, W2 = small(2), small(2), small(2), small(2), small(2)
        WT = small(TT, 8)
        WPR = small(EPG // 2)
        CNT, NR, ENDS, STA = small(8), small(8), small(8), small(8)
        RK, POS = small(TT, 8), small(2)
        TAB = small(ROUNDS, 8)
        TABR = small(ROUNDS)

        B = [ctx.enter_context(nc.psum_tensor(f"bank{i}", [P, 512], F32)) for i in range(8)]

        def wcols(w, c0, n, k=DK):
            return w[0].rearrange("(k p) n -> p k n", p=P)[:, :, c0:c0 + n], k, n

        w_in, w_in2 = a["w_in"], a["w_in_2"]
        fills = []
        results = []

        def fill(src, name, feature=True, ncols=256):
            fills.append(src)
            k, n = src[1], src[2]
            for c0 in range(0, n, ncols):
                results.append((name, len(fills) - 1, c0, feature, min(ncols, n - c0)))

        fill(wcols(w_in, COL_CQ, 256), name="cq", feature=False)
        fill(wcols(w_in, COL_CKV, 160), name="ckv", feature=False)
        for c in range(2):
            fill(wcols(w_in, COL_FF + 256 * c, 256), name="f")
        for c in range(2):
            fill(wcols(w_in, COL_FB + 256 * c, 256), name="f")
        for c in range(2):
            fill(wcols(w_in, COL_Q + 256 * c, 256), name="q")
        for c in range(2):
            fill(wcols(w_in, COL_V + 256 * c, 256), name="v", feature=False)
        for c in range(2):
            fill(wcols(w_in, COL_OG + 256 * c, 256), name="og", feature=False)
        fill(wcols(a["w_uq"], 0, 768, 2), name="uq", feature=False)
        fill(wcols(a["w_ukv"], 0, 1024, 1), name="ukv", feature=False)
        mods = 0
        for c in range(8):
            fill(wcols(w_in, COL_GA + 256 * c, 256), name="gate")
            for _ in range(2 - c % 2):
                fill(wcols(a["w_mod_2"], 256 * mods, 256), name="mod")
                mods += 1
        for c in range(4):
            fill(wcols(w_in2, C_K + 256 * c, 256), name="kc")
        for c in range(4):
            fill(wcols(w_in2, C_V + 256 * c, 256), name="vc", feature=False)
        for c in range(2):
            fill(wcols(a["w_oB"], 512 * c, 512, 4), name="yb")
        for c in range(2):
            fill(wcols(a["w_oA"], 512 * c, 512, 4), name="ya")
        for c in range(4):
            fill(wcols(a["w_out"], 256 * c, 256), name="out", feature=False)
        fill(wcols(a["w_ple_proj"], 0, 1024, 2), name="pp", feature=False)
        NA = len(fills)
        NRA = len(results)
        for c in range(4):
            fill(wcols(a["w_ple_gate"], 256 * c, 256), name="ple", feature=False)
        for name, col, feature in (("zb", C_ZB, False), ("ga", C_GA, True), ("gb", C_GB, True), ("za", C_ZA, True),
                                   ("b", C_B, True), ("c", C_C, True), ("xin", C_X, True), ("q2", C_Q, True),
                                   ("k2", C_K, True), ("v2", C_V, False)):
            for c in range(4):
                fill(wcols(w_in2, col + 256 * c, 256), name=name, feature=feature)
        for c in range(4):
            fill(wcols(a["w_out_conv_2"], 256 * c, 256), name="yconv")
        for c in range(4):
            fill(wcols(a["w_out_attn_2"], 256 * c, 256), name="yattn")
        for c in range(4):
            fill(wcols(a["w_o_2"], 256 * c, 256), name="wo", feature=False)
        NC_ = len(fills) - NA
        last_result = {f: i for i, (_, f, _, _, _) in enumerate(results)}
        of = {}
        for i, r in enumerate(results):
            of.setdefault(r[0], []).append(i)

        EMPTIER = {"cq": "dve", "ckv": "dve", "f": "act", "q": "dve", "v": "act", "og": "dve", "uq": "dve",
                   "ukv": "act", "gate": "act", "yb": "dve", "ya": "dve", "out": "dve", "mod": "act",
                   "kc": "act", "vc": "act", "pp": "act", "ple": "act", "zb": "dve", "ga": "act", "gb": "act",
                   "za": "dve", "b": "dve", "c": "act", "xin": "dve", "q2": "act", "k2": "act", "v2": "act",
                   "yconv": "dve", "yattn": "dve", "wo": "dve"}
        emptied, _n = {}, {"dve": 0, "act": 0}
        for i, r in enumerate(results):
            e = EMPTIER[r[0]]
            _n[e] += 1
            emptied[i] = (e, _n[e])

        def ready_sem(i):
            return ("res_a", i + 1) if i < NRA else ("res_c", i - NRA + 1)

        def wait_result(eng, i):
            n, v = ready_sem(i)
            eng.wait_ge(S(n), v)

        bank_no = [2 + n % 2 if r[0] in ("kc", "vc") else n % 4 for n, r in enumerate(results)]

        def bank_of(i):
            return B[bank_no[i]]

        def bank_before(i):
            return max((j for j in range(i) if bank_no[j] == bank_no[i]), default=None)

        PAIRS = EPG // 2

        def ups(p):
            return [("up", 2 * p + e, half) for half in range(2) for e in range(2)]

        def downs(p):
            return [("down", 2 * p + e, 0) for e in range(2)]

        moe_order = ups(0) + ups(1) + downs(0) + ups(2) + downs(1) + ups(3) + downs(2) + downs(3)
        moe_index = {key: j for j, key in enumerate(moe_order)}
        NM = len(moe_order)
        M_BASE = NA % RING

        def moe_slot(j):
            return (M_BASE + j) % RING

        slot_sum, slot_after = {}, []
        for _j, _key in enumerate(moe_order):
            _s = moe_slot(_j)
            slot_sum[_s] = slot_sum.get(_s, 0) + (32 if _key[0] == "up" else 16)
            slot_after.append(slot_sum[_s])

        def c_slot(f):
            return (M_BASE + f - NA) % RING

        def slot_of(f):
            return f % RING if f < NA else c_slot(f)

        def slot_view(f):
            _, k, n = fills[f]
            return ring[:, slot_of(f), 0:k * n].rearrange("p (k n) -> p k n", k=k)

        EARLY, SMALL = 16 * 13, 16 * 10
        NORMS = ["x", "ctx", "lat", "qk", "o", "hm", "ple", "two", "y"]
        TURNS = ["x", "ctx", "hm", "ple", "two", "o"]

        def nth(tag, seq=NORMS):
            return seq.index(tag) + 1

        block = ctx.enter_context(nc.Block())

        @block.sync
        def _(sp):
            sp.dma_start(X[:], a["x"][0].rearrange("(t p) d -> p t d", p=P)).then_inc(S("x_in"), 16)

            def stream_a():
                for f in range(NA):
                    if f >= RING:
                        sp.wait_ge(S("res_a"), last_result[f - RING] + 1)
                    sp.dma_start(slot_view(f), fills[f][0]).then_inc(S(f"arr_a{slot_of(f)}"), 16)

            stream_a()

            def expert_dma(j, g):
                kind, e, half = moe_order[j]
                dst, arrived = ring[:, moe_slot(j), :], S(f"arr_m{moe_slot(j)}")
                if kind == "down":
                    src = a["w2"][0, bass.ds(g * EPG + e, 1), :, :].rearrange("o (c p) n -> p (o c) n", p=P)
                    sp.dma_start(dst.rearrange("p (c n) -> p c n", c=2), src).then_inc(arrived, 16)
                else:
                    for w, name in enumerate(("w1", "w3")):
                        src = a[name][0, bass.ds(g * EPG + e, 1), :, :].rearrange("o (p k) n -> p (o k) n", p=P)
                        sp.dma_start(dst.rearrange("p (k n) -> p k n", k=DK // 2)[:, :, w * FE:w * FE + FE],
                                     src[:, half * DK // 2:(half + 1) * DK // 2, :]).then_inc(arrived, 16)

            for j in range(NM):
                if j < RING:
                    sp.wait_ge(S("res_a"), last_result[NA - RING + j] + 1)
                else:
                    sp.wait_ge(S("moe_used"), j - RING + 1)
                expert_dma(j, 0)
            sp.wait_ge(S("table"), 1)
            rounds = sp.value_load(RT[0:1, 0:1], min_val=4, max_val=ROUNDS)
            with sp.Fori(0, rounds - 1) as r:
                g = sp.value_load(RT[0:1, bass.ds(r + 2, 1)], min_val=0, max_val=NG - 1)
                for j in range(NM):
                    sp.wait_ge(S("moe_used"), r * NM + (NM + j - RING + 1))
                    expert_dma(j, g)

            used = sp.value_load(RT[0:1, 14:15], min_val=4 * NM - RING, max_val=ROUNDS * NM)
            for f in range(NA, NA + NC_):
                if f - NA < RING:
                    sp.wait_ge(S("moe_used"), used + (f - NA + 1))
                else:
                    sp.wait_ge(S("res_c"), last_result[f - RING] - NRA + 1)
                sp.dma_start(slot_view(f), fills[f][0]).then_inc(S(f"arr_c{slot_of(f)}"), 16)
            sp.wait_ge(S("final"), 2)
            sp.dma_start(out[0].rearrange("(t p) d -> p t d", p=P), HN[:]).then_inc(S("stored"), 16)
            sp.wait_ge(S("stored"), 16)

        def wait_slot(pe, f):
            if f < NA:
                pe.wait_ge(S(f"arr_a{slot_of(f)}"), 16 * (f // RING + 1))
            else:
                pe.wait_ge(S(f"arr_c{slot_of(f)}"), 16 * ((f - NA) // RING + 1))

        @block.tensor
        def _(pe):
            def wait_bank(i):
                if bank_before(i) is not None:
                    e, n = emptied[bank_before(i)]
                    pe.wait_ge(S("emptied_" + e), n)

            def product(i, act, first=None, parts=(0, 1)):
                name, f, c0, feature, n = results[i]
                if first is None and 0 in parts:
                    wait_bank(i)
                if c0 == 0 and 0 in parts:
                    wait_slot(pe, f)
                w, bank = slot_view(f), bank_of(i)
                k_n = fills[f][1]
                for part in parts:
                    for k in range(k_n):
                        if feature:
                            mm = pe.matmul(bank[:, part * T:part * T + T], w[:, k, c0 + part * P:c0 + part * P + P],
                                           act[:, k, :], start=(k == 0), stop=(k == k_n - 1))
                        else:
                            mm = pe.matmul(bank[:, part * 256:part * 256 + n], act[:, k, part * P:part * P + P],
                                           w[:, k, c0:c0 + n], start=(k == 0), stop=(k == k_n - 1))
                if 1 in parts:
                    mm.then_inc(S(ready_sem(i)[0]), 1)

            def products(name, act):
                for i in of[name]:
                    product(i, act)

            def turn_rows(src, first_bank=4):
                for k in range(DK):
                    for t in range(TT):
                        mm = pe.transpose(B[first_bank + k // 2][:, (k % 2) * T + t * P:(k % 2) * T + t * P + P], src(k, t), ident)
                    if k % 2 == 1:
                        mm.then_inc(S("turned"), 1)

            def cols(tile):
                return lambda k, t: tile[:, t, k * P:k * P + P]

            pe.wait_ge(S("early_in"), EARLY)
            pe.wait_ge(S("early_in"), EARLY)
            pe.transpose(B[4][:, 0:NVEC], VROW[0:NVEC, :], ident[0:NVEC, 0:NVEC]).then_inc(S("vec_ps"), 1)
            pe.wait_ge(S("vec"), 1)
            pe.wait_ge(S("normed"), nth("x"))
            turn_rows(cols(HN))
            pe.wait_ge(S("hT_dve"), 4)
            pe.wait_ge(S("hT_act"), 4)
            products("cq", HT)
            products("ckv", HT)
            for name in ("f", "q", "v", "og"):
                products(name, HT)
            pe.wait_ge(S("normed"), nth("lat"))
            for c in range(2):
                for t in range(TT):
                    pe.transpose(B[4][:, c * T + t * P:c * T + t * P + P], CQ[:, t, c * P:c * P + P], ident)
            for t in range(TT):
                mm = pe.transpose(B[5][:, t * P:t * P + P], CK[:, t, 0:P], ident)
            mm.then_inc(S("lat_ps"), 1)
            pe.wait_ge(S("latT"), 1)
            products("uq", CQT)
            products("ukv", CKT.unsqueeze(1))
            pe.wait_ge(S("silu_c"), 1)

            def modulation(i):
                wait_bank(i)
                wait_slot(pe, results[i][1])
                w = slot_view(results[i][1])
                for k in range(DK):
                    g = k % 4
                    mm = pe.matmul(bank_of(i)[32 * g:32 * g + 32, 0:256], CC[:, k, :], w[:, k, :],
                                   start=(k < 4), stop=(k >= 4))
                mm.then_inc(S("res_a"), 1)

            def modulation_sum(u):
                pe.wait_ge(S("emptied_act"), emptied[of["mod"][u]][1])
                row = MRW[:, u % 2, :]
                if u < 8:
                    for part in range(2):
                        mm = pe.matmul(B[7][:, 4 * u + 2 * part:4 * u + 2 * part + 2], row[:, part * P:part * P + P],
                                       const("pick2"), start=True, stop=True)
                else:
                    mm = pe.matmul(B[5 + (u - 8) // 2][:, (u % 2) * 256:(u % 2) * 256 + 256], const("row0"), row,
                                   start=True, stop=True)
                mm.then_inc(S("mod_sum"), 1)

            pending = None
            for i in sorted(of["gate"] + of["mod"]):
                if results[i][0] == "gate":
                    product(i, HT)
                else:
                    modulation(i)
                if pending is not None:
                    modulation_sum(pending)
                pending = of["mod"].index(i) if results[i][0] == "mod" else None
            modulation_sum(pending) if pending is not None else None
            pe.wait_ge(S("normed"), nth("ctx"))
            for i in sorted(of["gate"] + of["mod"])[-4:]:
                pe.wait_ge(S("emptied_" + emptied[i][0]), emptied[i][1])
            turn_rows(cols(HN), 0)
            pe.wait_ge(S("mod_in"), 1)
            pe.wait_ge(S("normed"), nth("qk"))
            pe.wait_ge(S("qk_pool"), 1)
            for h in range(MH):
                if h >= 4:
                    pe.wait_ge(S("qkT_even" if h % 2 == 0 else "qkT_odd"), h // 2 - 1)
                for s in range(2):
                    for t in range(TT):
                        mm = pe.transpose(B[4 + h % 4][0:QK, s * T + t * P:s * T + t * P + P],
                                          QKM[:, s, t, h * QK:h * QK + QK], ident)
                mm.then_inc(S("qkT_ps"), 1)
            pe.wait_ge(S("qkT_even"), 4)
            pe.wait_ge(S("qkT_odd"), 4)
            pe.wait_ge(S("cT_dve"), 8)

            spare = [(i, part) for i in of["kc"] + of["vc"] for part in range(2)]

            def context_product(n=1):
                for _ in range(n):
                    i, part = spare.pop(0)
                    product(i, HT, parts=(part,))

            def mla_scores(h):
                if h >= 2:
                    pe.wait_ge(S("mla_p"), 2 * (h - 1))
                for t in range(TT):
                    mm = pe.matmul(B[4 + h % 2][:, t * T:t * T + T], QKT[0:QK, h, t * P:t * P + P],
                                   QKT[0:QK, h, T:2 * T], start=True, stop=True)
                mm.then_inc(S("mla_s"), 1)

            mla_scores(0)
            for h in range(MH):
                if h + 1 < MH:
                    mla_scores(h + 1)
                if h % 2 == 1:
                    context_product()
                pe.wait_ge(S("mla_p"), 2 * h + 2)
                if h >= 2:
                    pe.wait_ge(S("mla_pt"), h - 1)
                for kt in range(TT):
                    for t in range(TT):
                        mm = pe.transpose(B[6 + h % 2][:, kt * T + t * P:kt * T + t * P + P],
                                          PR[:, h % 2, t, kt * P:kt * P + P], ident)
                mm.then_inc(S("mla_pT"), 1)
                pe.wait_ge(S("mla_pt"), h + 1)
                if h >= 2:
                    pe.wait_ge(S("mla_o"), h - 1)
                for t in range(TT):
                    for kt in range(TT):
                        mm = pe.matmul(B[h % 2][:, t * VD:t * VD + VD], PT[:, h % 2, kt, t * P:t * P + P],
                                       KV[:, kt, h * P + NOPE:h * P + P], start=(kt == 0), stop=(kt == TT - 1))
                mm.then_inc(S("mla_pv"), 1)
            context_product(4)
            for n, lv in enumerate(LEVELS):
                if n:
                    context_product()
                pe.wait_ge(S("gla_qk"), n + 1)
                if n == 0:
                    pe.wait_ge(S("mla_o"), MH)
                if n >= 3:
                    pe.wait_ge(S("gla_a"), n - 2)
                for st in range(TT):
                    bank = B[GLA_BANKS[n % 3] + st]
                    for h in range(GH):
                        tt = 1 - st if lv == 128 else st
                        q = QT if lv == "diag" else DEC[:, n % 2, 0].rearrange("p (h t) -> p h t", h=GH)
                        k = DEC[:, n % 2, 1].rearrange("p (h t) -> p h t", h=GH)
                        mm = pe.matmul(bank[:, h * P:h * P + P], k[:, h, st * P:st * P + P],
                                       q[:, h, tt * P:tt * P + P], start=True, stop=True)
                mm.then_inc(S("gla_s"), 1)
            context_product()
            pe.wait_ge(S("gla_a"), len(LEVELS))
            for tt in range(TT):
                for h in range(GH):
                    for st in range(TT):
                        sc = AD[:, st, h, :] if st == tt else AXX[:, st, h, :]
                        mm = pe.matmul(B[tt][:, h * P:h * P + P], sc, V[:, st, h * P:h * P + P],
                                       start=(st == 0), stop=(st == TT - 1))
            mm.then_inc(S("gla_o_ps"), 1)
            for c in range(GH):
                for t in range(TT):
                    mm = pe.transpose(B[4 + c // 2][:, (c % 2) * T + t * P:(c % 2) * T + t * P + P],
                                      OM[:, t, c * P:c * P + P], ident)
            mm.then_inc(S("omT_ps"), 1)
            pe.wait_ge(S("normed"), nth("o"))
            for c in range(GH):
                for t in range(TT):
                    mm = pe.transpose(B[6 + c // 2][:, (c % 2) * T + t * P:(c % 2) * T + t * P + P],
                                      OO[:, t, c, :], ident)
            mm.then_inc(S("ogT_ps"), 1)
            pe.wait_ge(S("omT"), 1)
            pe.wait_ge(S("gla_o"), 1)
            products("yb", OTM)
            pe.wait_ge(S("ogT"), 1)
            products("ya", OTG)
            pe.wait_ge(S("merged"), 4)
            products("out", GATE[:, 0:8, :])

            pe.wait_ge(S("p_in"), 16)
            for c in range(2):
                for t in range(TT):
                    mm = pe.transpose(B[4][:, c * T + t * P:c * T + t * P + P], PRAW[:, t, c * P:c * P + P], ident)
            mm.then_inc(S("pT_ps"), 1)
            pe.wait_ge(S("pT"), 1)
            products("pp", PTR)

            pe.wait_ge(S("normed"), nth("hm"))
            turn_rows(cols(HN))
            pe.wait_ge(S("rT_dve"), 4)
            pe.wait_ge(S("rT_act"), 4)
            pe.wait_ge(S("small_in"), SMALL)
            for t in range(TT):
                for k in range(DK):
                    mm = pe.matmul(B[4][:, t * 72:t * 72 + 72], HT[:, k, t * P:t * P + P], RW[:, k, :],
                                   start=(k == 0), stop=(k == DK - 1))
            mm.then_inc(S("logits_ps"), 1)
            pe.wait_ge(S("group"), 1)
            U, ONE = const("ustrict"), const("ones")[:, 0:P]
            pe.matmul(B[5][:, 0:8], U, GOH[:, 0, :], start=True, stop=True)
            pe.matmul(B[5][:, 8:16], ONE, GOH[:, 0, :], start=True, stop=False)
            pe.matmul(B[5][:, 8:16], U, GOH[:, 1, :], start=False, stop=True)
            pe.matmul(B[5][:, 16:24], ONE, GOH[:, 0, :], start=True, stop=False)
            pe.matmul(B[5][:, 16:24], ONE, GOH[:, 1, :], start=False, stop=True).then_inc(S("rank_ps"), 1)

            def slot_in(j, r):
                pe.wait_ge(S(f"arr_m{moe_slot(j)}"), r * slot_sum[moe_slot(j)] + slot_after[j])

            def moe_round(r, first=False):
                def at(n, k):
                    return r * n + k

                pe.wait_ge(S("sel"), at(1, 1))
                if not first:
                    pe.wait_ge(S("moe_x"), r)
                for k in range(DK):
                    for t in range(TT):
                        mm = pe.matmul(B[0][:, k * SLOT:k * SLOT + SLOT], HN[:, t, k * P:k * P + P], SEL[:, t, 0:SLOT],
                                       start=(t == 0), stop=(t == TT - 1))
                mm.then_inc(S("gath_ps"), 1)
                for t in range(TT):
                    mm = pe.matmul(B[1][:, 0:EPG], SEL[:, t, :], WT[:, t, :], start=(t == 0), stop=(t == TT - 1))
                for t in range(TT):
                    mm = pe.transpose(B[2][:, t * P:t * P + P], SEL[:, t, :], ident)
                mm.then_inc(S("sel_ps"), 1)
                pe.wait_ge(S("gath"), at(1, 1))

                def up(p):
                    bank = B[3 + p % 2]
                    if p >= 2:
                        pe.wait_ge(S("hid"), at(PAIRS, p - 1))
                    for half in range(2):
                        js = [moe_index[("up", 2 * p + e, half)] for e in range(2)]
                        for j in js:
                            slot_in(j, r)
                        for k in range(DK // 2):
                            kk = half * DK // 2 + k
                            for e in range(2):
                                w = ring[:, moe_slot(js[e]), :].rearrange("p (k n) -> p k n", k=DK // 2)
                                mm = pe.matmul(bank[e * SLOT:e * SLOT + SLOT, :], XG[:, kk, :], w[:, k, :],
                                               start=(kk == 0), stop=(kk == DK - 1))
                                if k == DK // 2 - 1:
                                    mm.then_inc(S("moe_used"), 1)

                def turn_hidden(p):
                    pe.wait_ge(S("hid"), at(PAIRS, p + 1))
                    for c in range(2):
                        mm = pe.transpose(B[6 + p % 2][:, c * P:c * P + P], HHR[:, p % 2, c * P:c * P + P], ident)
                    mm.then_inc(S("hht_ps"), 1)

                def down(p):
                    pe.wait_ge(S("hht"), at(PAIRS, p + 1))
                    for e in range(2):
                        j = moe_index[("down", 2 * p + e, 0)]
                        slot_in(j, r)
                        w = ring[:, moe_slot(j), :].rearrange("p (c n) -> p c n", c=2)
                        for c in range(2):
                            for half in range(2):
                                mm = pe.matmul(B[5][half * SLOT:half * SLOT + SLOT, :],
                                               HHT[:, p % 2, c, e * SLOT:e * SLOT + SLOT], w[:, c, half * 512:half * 512 + 512],
                                               start=(p == 0 and e == 0 and c == 0),
                                               stop=(p == PAIRS - 1 and e == 1 and c == 1))
                        mm.then_inc(S("moe_used"), 1)

                up(0)
                for p in range(PAIRS):
                    if p + 1 < PAIRS:
                        up(p + 1)
                    turn_hidden(p)
                    down(p)
                pe.wait_ge(S("yy"), at(1, 1))
                for t in range(TT):
                    for half in range(2):
                        rows = slice(half * SLOT, half * SLOT + SLOT)
                        mm = pe.matmul(B[2 * t + half][:, :], STR[rows, t * P:t * P + P], YY[rows, :], start=True, stop=True)
                mm.then_inc(S("scat_ps"), 1)

            for i in range(NRA - 4, NRA):
                pe.wait_ge(S("emptied_" + emptied[i][0]), emptied[i][1])
            moe_round(0, first=True)
            pe.wait_ge(S("table"), 1)
            rounds = pe.value_load(RT[0:1, 0:1], min_val=4, max_val=ROUNDS)
            with pe.Fori(1, rounds) as r:
                moe_round(r)

            pe.wait_ge(S("normed"), nth("ple"))
            turn_rows(cols(HN))
            pe.wait_ge(S("pleT_dve"), 4)
            pe.wait_ge(S("pleT_act"), 4)
            for i in of["ple"]:
                product(i, HT, first=True)

            pe.wait_ge(S("normed"), nth("two"))
            turn_rows(cols(HN))
            pe.wait_ge(S("twoT"), 8)
            for name in ("zb", "ga", "gb", "za", "b", "c", "xin"):
                products(name, HT)
            for name in ("q2", "k2"):
                for n, i in enumerate(of[name]):
                    product(i, HT)
                    m = n + (4 if name == "k2" else 0)
                    pe.wait_ge(S("emptied_act"), emptied[i][1])
                    if m >= 2:
                        pe.wait_ge(S("roped"), m - 1)
                    pe.matmul(B[4 + m % 2][:, :], const("rot"), RAW[:, m % 2, :], start=True, stop=True)\
                      .then_inc(S("rot_ps"), 1)
            products("v2", HT)
            pe.wait_ge(S("roped"), 8)
            for i in of["v2"]:
                pe.wait_ge(S("emptied_" + emptied[i][0]), emptied[i][1])

            N2 = H2 * TT

            def scores2(n):
                h, t = divmod(n, TT)
                c, p0 = h // 2, (h % 2) * HD
                if n >= 2:
                    pe.wait_ge(S("na_p"), n - 1)
                bank = B[4 + n % 2]
                pe.matmul(bank[:, 0:T], QT2[p0:p0 + HD, c, t * P:t * P + P], KT2[p0:p0 + HD, c, :], start=True, stop=False)
                pe.wait_ge(S("bm"), n + 1)
                pe.matmul(bank[:, 0:T], const("flip"), BM[:, n % 2, :], start=False, stop=True)
                pe.matmul(bank[:, T:2 * T], QT2[p0:p0 + HD, c, t * P:t * P + P], KC[p0:p0 + HD, c, :],
                          start=True, stop=True).then_inc(S("na_s"), 1)

            scores2(0)
            for n in range(N2):
                h, t = divmod(n, TT)
                if n + 1 < N2:
                    scores2(n + 1)
                pe.wait_ge(S("na_p"), n + 1)
                if n >= 2:
                    pe.wait_ge(S("na_pt"), n - 1)
                for kt in range(4):
                    mm = pe.transpose(B[6 + n % 2][:, kt * P:kt * P + P], PR2[:, n % 2, kt * P:kt * P + P], ident)
                mm.then_inc(S("na_pT"), 1)
                pe.wait_ge(S("na_pt"), n + 1)
                if n >= 2:
                    pe.wait_ge(S("na_o"), n - 1)
                for kt in range(4):
                    v = V2 if kt < 2 else VC
                    mm = pe.matmul(B[n % 2][:, 0:HD], PT2[:, n % 2, kt * P:kt * P + P],
                                   v[:, kt % 2, h * HD:h * HD + HD], start=(kt == 0), stop=(kt == 3))
                mm.then_inc(S("na_pv"), 1)
            pe.wait_ge(S("na_o"), N2)
            turn_rows(cols(HN))
            products("yconv", YA)
            pe.wait_ge(S("oT"), 8)
            products("yattn", HT)
            pe.wait_ge(S("merged2"), 4)
            products("wo", GA)

        @block.scalar
        def _(act):
            act.dma_start(CST[:], a["consts"]).then_inc(S("early_in"), 16)
            for name, (row, n) in VEC_ROWS.items():
                v = a[name]
                if name == "b_mod_2":
                    src = v[0, 0:2048].rearrange("(r p) -> r p", p=P)
                elif name == "conv_w_2":
                    src = v[0].rearrange("k (r p) -> (k r) p", p=P)
                elif name == "hg_lb":
                    src = v.rearrange("d j (r p) -> (d j r) p", p=P)
                elif name == "c_ctx_2":
                    src = v.rearrange("(r p) -> r p", p=P)
                else:
                    src = v[0].rearrange("(r p) -> r p", p=P)
                act.dma_start(VROW[row:row + n, :], src).then_inc(S("early_in"), 16)
            act.dma_start(POSI[:], a["positions"].rearrange("o (t p) -> p (o t)", p=P),
                          allow_slow_non_contiguous=True).then_inc(S("early_in"), 16)
            act.dma_start(QKN[:, 0, :], a["q_norm"][0].partition_broadcast(P)).then_inc(S("small_in"), 16)
            act.dma_start(QKN[:, 1, :], a["k_norm"][0].partition_broadcast(P)).then_inc(S("small_in"), 16)
            act.dma_start(ONB[:], a["hg_onorm"][0].partition_broadcast(P)).then_inc(S("small_in"), 16)
            act.dma_start(HT[:, 0:3, :].rearrange("p a b -> p (a b)"), a["masks"].rearrange("p a b -> p (a b)"))\
               .then_inc(S("masks_in"), 16)
            act.dma_start(RB[:, 0:8], a["b_rg"][0].partition_broadcast(P)).then_inc(S("small_in"), 16)
            act.dma_start(RB[:, 8:72], a["b_re"][0].partition_broadcast(P)).then_inc(S("small_in"), 16)
            act.dma_start(RW[:, :, 0:8], a["w_rg"][0].rearrange("(p k) n -> p k n", p=P)).then_inc(S("small_in"), 16)
            act.dma_start(RW[:, :, 8:72], a["w_re"][0].rearrange("(p k) n -> p k n", p=P)).then_inc(S("small_in"), 16)
            act.dma_start(LNM[:], a["ln_moe"][0].rearrange("(p k) -> p k", p=P)).then_inc(S("small_in"), 16)
            act.dma_start(PG[:], a["post_g_2"][0].partition_broadcast(P)).then_inc(S("small_in"), 16)
            act.dma_start(BGT[:], a["b_mod_2"][0, 2048:3072].partition_broadcast(P)).then_inc(S("small_in"), 16)

            def sumsq(src, tag):
                for t in range(TT):
                    ins = nc.scalar.activation(HN[:, t, :], src[:, t, :], ACT.Square, accum_out=ss[tag][:, t:t + 1])
                ins.then_inc(S("sumsq"), 1)

            def turned(tag, done, gain):
                for k in range(4, 8):
                    if k % 2 == 0:
                        act.wait_ge(S("turned"), 4 * nth(tag, TURNS) - 3 + k // 2)
                    nc.scalar.activation(HT[:, k, :], B[4 + k // 2][:, (k % 2) * T:(k % 2) * T + T], ACT.Copy,
                                         scale=gain(k)).then_inc(S(done), 1)

            act.wait_ge(S("x_in"), 16)
            sumsq(X, "x")
            act.wait_ge(S("ang"), 1)
            nc.scalar.activation(SN, RED, ACT.Sin)
            nc.scalar.activation(CS, KQ, ACT.Sin).then_inc(S("sincos"), 1)
            act.wait_ge(S("vec"), 1)
            turned("x", "hT_act", lambda k: vec("ln_mix", k))
            act.dma_start(HN[:], a["ctx_2"][0].rearrange("(t p) d -> p t d", p=P)).then_inc(S("ctx_in"), 16)
            act.wait_ge(S("cc"), 1)
            nc.scalar.activation(CSG, CC[:, :, 0:2], ACT.Sigmoid).then_inc(S("sig_c"), 1)
            act.wait_ge(S("lbd"), 2)
            nc.scalar.activation(LBF, LBF, ACT.Sigmoid)
            nc.scalar.activation(LBR, LBR, ACT.Sigmoid).then_inc(S("lb"), 1)
            for n, i in enumerate(of["f"]):
                wait_result(act, i)
                nc.scalar.activation(SF[:, 2 * n:2 * n + 2, :].rearrange("p a t -> p (a t)"), bank_of(i)[:, :],
                                     ACT.Sigmoid).then_inc(S("emptied_act"), 1)
            act.wait_ge(S("ctx_in"), 16)
            for t in range(TT):
                ins = nc.scalar.activation(CSQ[:, t, :], HN[:, t, :], ACT.Square, accum_out=ss["ctx"][:, t:t + 1])
            ins.then_inc(S("sumsq"), 1)
            for n, i in enumerate(of["q"]):
                wait_result(act, i)
                nc.scalar.activation(QT[:, 2 * n:2 * n + 2, :].rearrange("p a t -> p (a t)"), bank_of(i)[:, :],
                                     ACT.Sigmoid).then_inc(S("sig"), 1)
            for n, i in enumerate(of["v"]):
                wait_result(act, i)
                nc.scalar.activation(V[:, :, 256 * n:256 * n + 256], bank_of(i)[:, :].rearrange("p (t c) -> p t c", t=TT),
                                     ACT.Copy).then_inc(S("emptied_act"), 1)
            for n, i in enumerate(of["og"]):
                wait_result(act, i)
                nc.scalar.activation(OG[:, :, 256 * n:256 * n + 256], bank_of(i)[:, :].rearrange("p (t c) -> p t c", t=TT),
                                     ACT.Sigmoid).then_inc(S("sig"), 1)
            act.wait_ge(S("emptied_dve"), emptied[of["ckv"][0]][1])
            for t in range(TT):
                nc.scalar.activation(CQT[:, t, :], CQ[:, t, :], ACT.Square, accum_out=SSL[:, t:t + 1])
            for t in range(TT):
                ins = nc.scalar.activation(CKT[:, t * P:t * P + P], CK[:, t, 0:P], ACT.Square, accum_out=SSL[:, 2 + t:3 + t])
            ins.then_inc(S("sumsq"), 1)
            for n, i in enumerate(of["ukv"]):
                wait_result(act, i)
                nc.scalar.activation(KV[:, :, 256 * n:256 * n + 256], bank_of(i)[:, :].rearrange("p (t c) -> p t c", t=TT),
                                     ACT.Copy).then_inc(S("emptied_act"), 1)
            act.wait_ge(S("emptied_dve"), emptied[of["uq"][-1]][1])
            nc.scalar.activation(SQ[:, 0], QKM[:, 0].rearrange("p t (h d) -> p (t h) d", h=MH), ACT.Square)
            act.wait_ge(S("km"), 1)
            nc.scalar.activation(SQ[:, 1], QKM[:, 1].rearrange("p t (h d) -> p (t h) d", h=MH), ACT.Square)\
              .then_inc(S("sumsq"), 1)
            for i in sorted(of["gate"] + of["mod"]):
                wait_result(act, i)
                n = of[results[i][0]].index(i)
                if results[i][0] == "gate":
                    nc.scalar.activation(GATE[:, 2 * n:2 * n + 2, :].rearrange("p a t -> p (a t)"), bank_of(i)[:, :],
                                         ACT.Sigmoid).then_inc(S("emptied_act"), 1)
                else:
                    if n >= 2:
                        act.wait_ge(S("mod_sum"), n - 1)
                    nc.scalar.activation(MRW[:, n % 2, :], bank_of(i)[:, 0:256], ACT.Copy).then_inc(S("emptied_act"), 1)
            act.wait_ge(S("fgate"), 1)
            nc.scalar.activation(SF[:, :, :], SF[:, :, :], ACT.Ln).then_inc(S("logf"), 1)
            for h in range(0, MH, 2):
                act.wait_ge(S("qkT_ps"), h + 1)
                nc.scalar.activation(QKT[0:QK, h, :], B[4 + h % 4][0:QK, :], ACT.Copy).then_inc(S("qkT_even"), 1)
            scale = QK ** -0.5

            def context_keys(n):
                i = of["kc"][n]
                wait_result(act, i)
                nc.scalar.activation(HN[:, n // 2, (n % 2) * 512:(n % 2) * 512 + 512], bank_of(i)[:, :], ACT.Copy)\
                  .then_inc(S("emptied_act"), 1)

            def context_values(n):
                i = of["vc"][n]
                wait_result(act, i)
                nc.scalar.activation(VC[:, :, 256 * n:256 * n + 256], bank_of(i)[:, :].rearrange("p (t c) -> p t c", t=TT),
                                     ACT.Copy).then_inc(S("emptied_act"), 1)

            for h in range(MH):
                if h == 4:
                    context_keys(0)
                act.wait_ge(S("mla_nmax"), h + 1)
                if h >= 2:
                    act.wait_ge(S("mla_pT"), h - 1)
                for t in range(TT):
                    nc.scalar.activation(PR[:, h % 2, t, :], B[4 + h % 2][:, t * T:t * T + T], ACT.Exp, scale=scale,
                                         bias=NMX[:, h % 2, t:t + 1], accum_out=SUM[:, h % 2, t:t + 1])\
                      .then_inc(S("mla_p"), 1)
                act.wait_ge(S("mla_pT"), h + 1)
                if h >= 2:
                    act.wait_ge(S("mla_pv"), h - 1)
                nc.scalar.activation(PT[:, h % 2, :, :].rearrange("p a t -> p (a t)"), B[6 + h % 2][:, :], ACT.Copy)\
                  .then_inc(S("mla_pt"), 1)
            context_keys(1)
            for n, lv in enumerate(LEVELS[:-1]):
                act.wait_ge(S("gla_dec"), n + 1)
                nc.scalar.activation(DEC[:, n % 2, :, :], DEC[:, n % 2, :, :], ACT.Exp).then_inc(S("gla_exp"), 1)
                if n <= 1:
                    context_keys(n + 2)
                if n == 2:
                    act.wait_ge(S("cum"), 1)
                    act.wait_ge(S("emptied_act"), emptied[of["kc"][-1]][1])
                    act.dma_start(KC.rearrange("p a t -> p (a t)"), HN[:].rearrange("p a t -> p (a t)"))\
                       .then_inc(S("kc_in"), 16)
                if n in (3, 5, 6):
                    context_values({3: 0, 5: 1, 6: 2}[n])
            context_values(3)
            act.wait_ge(S("omT_ps"), 1)
            for c in range(2):
                ins = nc.scalar.activation(OTM[:, 2 * c:2 * c + 2, :].rearrange("p a t -> p (a t)"), B[4 + c][:, :], ACT.Copy)
            ins.then_inc(S("omT"), 1)
            act.wait_ge(S("gla_o"), 1)
            nc.scalar.activation(OSQ, OO.rearrange("p t h v -> p (t h) v"), ACT.Square).then_inc(S("sumsq"), 1)
            act.wait_ge(S("ogT_ps"), 1)
            for c in range(2):
                ins = nc.scalar.activation(OTG[:, 2 * c:2 * c + 2, :].rearrange("p a t -> p (a t)"), B[6 + c][:, :], ACT.Copy)
            ins.then_inc(S("ogT"), 1)

            act.wait_ge(S("normed"), nth("o"))
            act.dma_start(PRAW[:], a["p"][0, 0].rearrange("(t p) d -> p t d", p=P)).then_inc(S("p_in"), 16)
            act.wait_ge(S("kc_in"), 16)
            act.wait_ge(S("emptied_dve"), emptied[of["out"][-1]][1])
            sumsq(X, "hm")
            for n, i in enumerate(of["pp"]):
                wait_result(act, i)
                nc.scalar.activation(PP[:, :, 256 * n:256 * n + 256], bank_of(i)[:, :].rearrange("p (t c) -> p t c", t=TT),
                                     ACT.Copy).then_inc(S("emptied_act"), 1)
            act.wait_ge(S("small_in"), SMALL)
            turned("hm", "rT_act", lambda k: LNM[:, k:k + 1])
            act.wait_ge(S("gdiff"), 1)
            nc.scalar.activation(GEXP, GEXP, ACT.Exp).then_inc(S("gexp"), 1)
            act.wait_ge(S("ediff"), 1)
            nc.scalar.activation(E2W, DLT, ACT.Exp).then_inc(S("eexp"), 1)

            def moe_round(r):
                def at(n, k):
                    return r * n + k

                act.wait_ge(S("sel_ps"), at(1, 1))
                nc.scalar.activation(STR, B[2][:, 0:T], ACT.Copy).then_inc(S("str"), 1)

                def sigmoid(p):
                    act.wait_ge(S("moe_used"), at(NM, moe_index[("up", 2 * p + 1, 1)] + 1))
                    nc.scalar.activation(SGM[:, p % 2], B[3 + p % 2][:, 0:FE], ACT.Sigmoid).then_inc(S("moe_sig"), 1)

                sigmoid(0)
                for p in range(PAIRS):
                    if p + 1 < PAIRS:
                        sigmoid(p + 1)
                    act.wait_ge(S("hht_ps"), at(PAIRS, p + 1))
                    nc.scalar.activation(HHT[:, p % 2].rearrange("p c s -> p (c s)"), B[6 + p % 2][:, 0:2 * P], ACT.Copy)\
                      .then_inc(S("hht"), 1)
                act.wait_ge(S("moe_used"), at(NM, NM))
                nc.scalar.activation(YY, B[5][:, :], ACT.Copy).then_inc(S("yy"), 1)

            moe_round(0)
            act.wait_ge(S("table"), 1)
            rounds = act.value_load(RT[0:1, 0:1], min_val=4, max_val=ROUNDS)
            with act.Fori(1, rounds) as r:
                moe_round(r)

            act.wait_ge(S("moe_x"), rounds + 0)
            sumsq(X, "ple")
            turned("ple", "pleT_act", lambda k: vec("ln_ple", k))
            for n, i in enumerate(of["ple"]):
                wait_result(act, i)
                if n >= 2:
                    act.wait_ge(S("ple_x"), n - 1)
                nc.scalar.activation(SG[:, n % 2].rearrange("p t c -> p (t c)"), bank_of(i)[:, :], ACT.Sigmoid)\
                  .then_inc(S("emptied_act"), 1)
            act.wait_ge(S("ple_x"), 4)
            act.wait_ge(S("turned"), 4 * nth("ple", TURNS))
            sumsq(X, "two")
            for n, i in enumerate(of["zb"]):
                wait_result(act, i)
                nc.scalar.activation(ZB[:, :, 256 * n:256 * n + 256], bank_of(i)[:, :].rearrange("p (t c) -> p t c", t=TT),
                                     ACT.Sigmoid).then_inc(S("sig2"), 1)
            for name, dst in (("ga", GA), ("gb", GB)):
                for n, i in enumerate(of[name]):
                    wait_result(act, i)
                    nc.scalar.activation(dst[:, 2 * n:2 * n + 2, :].rearrange("p a t -> p (a t)"), bank_of(i)[:, :],
                                         ACT.Sigmoid).then_inc(S("emptied_act"), 1)
            for n, i in enumerate(of["za"]):
                wait_result(act, i)
                nc.scalar.activation(YA[:, 2 * n:2 * n + 2, :].rearrange("p a t -> p (a t)"), bank_of(i)[:, :],
                                     ACT.Sigmoid).then_inc(S("sig2"), 1)
            for n, i in enumerate(of["c"]):
                wait_result(act, i)
                nc.scalar.activation(UC[:, 2 * n:2 * n + 2, 1:T + 1], bank_of(i)[:, :].rearrange("p (a t) -> p a t", a=2),
                                     ACT.Copy).then_inc(S("emptied_act"), 1)
            for m, i in enumerate(of["q2"] + of["k2"]):
                wait_result(act, i)
                if m >= 2:
                    act.wait_ge(S("roped"), m - 1)
                nc.scalar.activation(RAW[:, m % 2, :], bank_of(i)[:, :], ACT.Copy).then_inc(S("emptied_act"), 1)
            act.wait_ge(S("conv"), 8)
            for n, i in enumerate(of["v2"]):
                wait_result(act, i)
                nc.scalar.activation(V2[:, :, 256 * n:256 * n + 256], bank_of(i)[:, :].rearrange("p (t c) -> p t c", t=TT),
                                     ACT.Copy).then_inc(S("emptied_act"), 1)
            act.wait_ge(S("roped"), 8)
            for n in range(H2 * TT):
                act.wait_ge(S("na_nmax"), n + 1)
                if n >= 2:
                    act.wait_ge(S("na_pT"), n - 1)
                nc.scalar.activation(PR2[:, n % 2, :], B[4 + n % 2][:, :], ACT.Exp, bias=NMX2[:, n % 2:n % 2 + 1],
                                     accum_out=SUM2[:, n % 2:n % 2 + 1]).then_inc(S("na_p"), 1)
                act.wait_ge(S("na_pT"), n + 1)
                if n >= 2:
                    act.wait_ge(S("na_pv"), n - 1)
                nc.scalar.activation(PT2[:, n % 2, :], B[6 + n % 2][:, :], ACT.Copy).then_inc(S("na_pt"), 1)
            for k in range(DK):
                if k % 2 == 0:
                    act.wait_ge(S("turned"), 4 * nth("o", TURNS) - 3 + k // 2)
                nc.scalar.activation(HT[:, k, :], B[4 + k // 2][:, (k % 2) * T:(k % 2) * T + T], ACT.Copy)\
                  .then_inc(S("oT"), 1)
            act.wait_ge(S("emptied_dve"), emptied[of["wo"][-1]][1])
            sumsq(YF, "y")

        M_TMP_K = area(M0, 4, TT, MH * 16)
        M_TMP_Q = area(M0 + 6720, 4, TT, MH * 16)

        def norm_rope(ve, link, s, tmp):
            x = QKM[:, s].rearrange("p t (h d) -> p (t h) d", h=MH)
            link(ve.tensor_tensor(x, x, over(RSH[:, 16 * s:16 * s + 16].unsqueeze(2), 16, QK), ALU.mult))
            link(ve.tensor_tensor(x, x, over(QKN[:, s:s + 1, :], 16, QK), ALU.mult))
            xr = QKM[:, s].rearrange("p t (h d) -> p t h d", h=MH)
            x1, x2 = xr[:, :, :, NOPE:NOPE + 16], xr[:, :, :, NOPE + 16:QK]
            tm = [tmp[:, j].rearrange("p t (h d) -> p t h d", h=MH) for j in range(4)]
            cs = over(CS.unsqueeze(2), TT, MH, 16)
            sn = over(SN.unsqueeze(2), TT, MH, 16)
            ve.tensor_tensor(tm[0], x1, cs, ALU.mult)
            ve.tensor_tensor(tm[1], x2, sn, ALU.mult)
            ve.tensor_tensor(tm[2], x2, cs, ALU.mult)
            link(ve.tensor_tensor(tm[3], x1, sn, ALU.mult))
            ve.tensor_tensor(x1, tm[0], tm[1], ALU.subtract)
            return ve.tensor_tensor(x2, tm[2], tm[3], ALU.add)

        @block.gpsimd
        def _(pool):
            def power(dst, src, n, tag):
                pool.wait_ge(S("mean_sq"), nth(tag))
                nc.gpsimd.tensor_tensor(dst, src, NHALF[:, 0:n], ALU.pow).then_inc(S("rms"), 1)

            nc.gpsimd.memset(NHALF, -0.5).then_inc(S("nhalf"), 1)
            pool.wait_ge(S("nhalf"), 1)
            power(rs["x"], ss["x"], 2, "x")
            power(rs["ctx"], ss["ctx"], 2, "ctx")
            power(RSL, SSL, 4, "lat")
            for t in range(TT):
                dst = QKM[:, 1, t].rearrange("p (h d) -> p h d", h=MH)
                if t == 0:
                    pool.wait_ge(S("emptied_act"), emptied[of["ukv"][-1]][1])
                    pool.wait_ge(S("emptied_dve"), emptied[of["ckv"][0]][1])
                nc.gpsimd.tensor_copy(dst[:, :, 0:NOPE], KV[:, t].rearrange("p (h d) -> p h d", h=MH)[:, :, 0:NOPE])
                ins = nc.gpsimd.tensor_copy(dst[:, :, NOPE:QK], over(CK[:, t, P:160].unsqueeze(1), MH, ROPE))
            ins.then_inc(S("km"), 1)
            power(RSH, SSH, 32, "qk")

            def chain(ins, name, n=[0]):
                n[0] += 1
                ins.then_inc(S(name), 1)
                pool.wait_ge(S(name), n[0])

            pool.wait_ge(S("km"), 1)
            pool.wait_ge(S("sumsq"), nth("qk"))
            pool.wait_ge(S("rms"), nth("qk"))
            pool.wait_ge(S("small_in"), SMALL)
            pool.wait_ge(S("sincos"), 1)
            norm_rope(nc.gpsimd, lambda ins: chain(ins, "pool_chain"), 1, M_TMP_K).then_inc(S("qk_pool"), 1)

            pool.wait_ge(S("mla_pv"), MH)
            pool.wait_ge(S("mla_o"), MH)
            pool.wait_ge(S("cum"), 1)
            for n, lv in enumerate(LEVELS[:-1]):
                if n >= 2:
                    pool.wait_ge(S("gla_s"), n - 1)
                dq, dk = DEC[:, n % 2, 0], DEC[:, n % 2, 1]
                fc = FC.rearrange("p h t -> p (h t)")
                bx = BX.rearrange("p h t -> p (h t)")
                if isinstance(lv, int):
                    m = lv

                    def halves(v):
                        v = v.rearrange("p (b two m) -> p b two m", two=2, m=m)
                        return v[:, :, 0, :], v[:, :, 1, :]

                    blocks = GH * T // (2 * m)
                    fl, fr = halves(fc)
                    bl, br = halves(bx)
                    qs = halves(dq)
                    ks = halves(dk)
                    f_edge = over(fl[:, :, m - 1:m], blocks, m)
                    b_edge = over(br[:, :, 0:1], blocks, m)
                    nc.gpsimd.tensor_tensor(qs[0], b_edge, bl, ALU.subtract)
                    nc.gpsimd.tensor_tensor(qs[1], fr, f_edge, ALU.subtract)
                    nc.gpsimd.tensor_tensor(ks[0], f_edge, fl, ALU.subtract)
                    nc.gpsimd.tensor_tensor(ks[1], br, b_edge, ALU.subtract).then_inc(S("gla_dec"), 1)
                else:
                    def blk(v):
                        return v.rearrange("p (b m) -> p b m", m=8)

                    if lv == "base_fwd":
                        ref = over(blk(fc)[:, :, 3:4], GH * T // 8, 8)
                        nc.gpsimd.tensor_tensor(blk(dq), blk(fc), ref, ALU.subtract)
                        nc.gpsimd.tensor_tensor(blk(dk), ref, blk(fc), ALU.subtract).then_inc(S("gla_dec"), 1)
                    else:
                        ref = over(blk(bx)[:, :, 4:5], GH * T // 8, 8)
                        nc.gpsimd.tensor_tensor(blk(dq), ref, blk(bx), ALU.subtract)
                        nc.gpsimd.tensor_tensor(blk(dk), blk(bx), ref, ALU.subtract).then_inc(S("gla_dec"), 1)
            power(RSO, SSO, 8, "o")
            power(rs["hm"], ss["hm"], 2, "hm")
            power(rs["ple"], ss["ple"], 2, "ple")
            power(rs["two"], ss["two"], 2, "two")
            pool.wait_ge(S("conv"), 8)

            def bias_dma(h):
                for t in range(TT):
                    for q in range(2):
                        at = (h * ROWS + 2 * t + q) * TOEP
                        src = bass.AP(a["toeplitz"].tensor, at, [[ROWS, GW], [1, T]])
                        pool.dma_start(BT[q * GW:q * GW + GW, h % 2, t, :], src).then_inc(S(f"bt{h % 2}"), 16)

            bias_dma(0)
            for h in range(H2):
                if h + 1 < H2:
                    bias_dma(h + 1)
                pool.wait_ge(S(f"bt{h % 2}"), 64 * (h // 2 + 1))
                for t in range(TT):
                    n = h * TT + t
                    if n >= 2:
                        pool.wait_ge(S("na_s"), n - 1)
                    nc.gpsimd.tensor_tensor(BM[:, n % 2, :].rearrange("p (r c) -> p c r", r=ROWS),
                                            BT[:, h % 2, t, :].rearrange("p (c r) -> p c r", r=ROWS),
                                            const("winmask").rearrange("p (c r) -> p c r", r=ROWS), ALU.add)\
                      .then_inc(S("bm"), 1)
                    pool.wait_ge(S("bm"), n + 1)
            power(rs["y"], ss["y"], 2, "y")

        @block.vector
        def _(dve):
            V_ = nc.vector
            links = [0]

            def link(ins):
                links[0] += 1
                ins.then_inc(S("dve_chain"), 1)
                dve.wait_ge(S("dve_chain"), links[0])

            def mean_sq(tag, n):
                v = ss[tag]
                dve.wait_ge(S("sumsq"), nth(tag))
                V_.tensor_scalar(v, v, 1.0 / n, EPS, ALU.mult, ALU.add).then_inc(S("mean_sq"), 1)

            def normalize(src, tag, dst=None):
                mean_sq(tag, D)
                dve.wait_ge(S("rms"), nth(tag))
                for t in range(TT):
                    o = HN[:, t, :] if dst is None else dst(t)
                    i_ = src[:, t, :] if dst is None else src[:, t, :].rearrange("p (q k) -> p k q", k=DK)
                    ins = V_.tensor_scalar(o, i_, rs[tag][:, t:t + 1], None, ALU.mult)
                ins.then_inc(S("normed"), 1)

            def turned(tag, done, gain, ks=range(4), bias=None, first_bank=4):
                for k in ks:
                    if k % 2 == 0:
                        dve.wait_ge(S("turned"), 4 * nth(tag, TURNS) - 3 + k // 2)
                    src = B[first_bank + k // 2][:, (k % 2) * T:(k % 2) * T + T]
                    if bias is None:
                        V_.tensor_scalar(HT[:, k, :], src, gain(k), None, ALU.mult).then_inc(S(done), 1)
                    else:
                        V_.tensor_scalar(HT[:, k, :], src, gain(k), bias(k), ALU.mult, ALU.add).then_inc(S(done), 1)

            def tiles(i):
                return bank_of(i)[:, :].rearrange("p (t c) -> p t c", t=TT)

            dve.wait_ge(S("early_in"), EARLY)
            dve.wait_ge(S("early_in"), EARLY)
            link(V_.tensor_copy(POSF, POSI[:]))
            for t in range(TT):
                ins = V_.tensor_scalar(ANG[:, t, :], const("invfreq"), POSF[:, t:t + 1], None, ALU.mult)
            link(ins)
            magic = 1.5 * 2 ** 23
            link(V_.tensor_scalar(KQ, ANG, 1.0 / (2 * np.pi), magic, ALU.mult, ALU.add))
            link(V_.tensor_scalar(KQ, KQ, magic, None, ALU.subtract))
            c1 = 6.28125
            c2 = float(np.float32(2 * np.pi - c1))
            c3 = float(2 * np.pi - c1 - np.float64(np.float32(c2)))
            link(V_.scalar_tensor_tensor(out=RED, in0=KQ, scalar=-c1, in1=ANG, op0=ALU.mult, op1=ALU.add))
            link(V_.scalar_tensor_tensor(out=RED, in0=KQ, scalar=-c2, in1=RED, op0=ALU.mult, op1=ALU.add))
            link(V_.scalar_tensor_tensor(out=RED, in0=KQ, scalar=-c3, in1=RED, op0=ALU.mult, op1=ALU.add))
            link(V_.tensor_scalar(RED, RED, float(np.float32(3.1415925)), -float(np.float32(3.1415925)), ALU.min, ALU.max))
            link(V_.tensor_scalar(KQ, RED, -1.0, None, ALU.mult))
            link(V_.tensor_tensor(KQ, KQ, RED, ALU.max))
            V_.tensor_scalar(KQ, KQ, -1.0, float(np.pi / 2), ALU.mult, ALU.add).then_inc(S("ang"), 1)

            dve.wait_ge(S("masks_in"), 16)
            V_.tensor_copy(MSK[:].rearrange("p a b -> p (a b)"), HT[:, 0:3, :].rearrange("p a b -> p (a b)"))
            dve.wait_ge(S("vec_ps"), 1)
            V_.tensor_copy(VEC[:], B[4][:, 0:NVEC]).then_inc(S("vec"), 1)
            normalize(X, "x")
            dve.wait_ge(S("vec"), 1)
            at = VEC_ROWS["hg_lb"][0]
            lbv = VEC[:, at:at + 16].rearrange("p (d j r) -> p d j r", d=2, j=2)
            l0, l1 = lbv[:, :, 0, :], lbv[:, :, 1, :]
            V_.tensor_tensor(LBF.rearrange("p (d r) -> p d r", d=2), l0, l1, ALU.subtract).then_inc(S("lbd"), 1)
            V_.tensor_tensor(LBR.rearrange("p (d r) -> p d r", d=2), l1, l0, ALU.subtract).then_inc(S("lbd"), 1)
            link(V_.memset(CC, 0.0))
            V_.tensor_copy(CC[:, :, 0], vec("c_2", 0, 8))
            V_.tensor_copy(CC[:, :, 1], vec("c_ctx_2", 0, 8)).then_inc(S("cc"), 1)
            turned("x", "hT_dve", lambda k: vec("ln_mix", k))
            i = of["cq"][0]
            wait_result(dve, i)
            V_.tensor_copy(CQ[:, :, :], tiles(i)).then_inc(S("emptied_dve"), 1)
            i = of["ckv"][0]
            wait_result(dve, i)
            V_.tensor_copy(CK[:, :, :], tiles(i)[:, :, 0:160]).then_inc(S("emptied_dve"), 1)

            def silu_result(dst, i, sem, n):
                wait_result(dve, i)
                dve.wait_ge(S(sem), n)
                V_.tensor_tensor(dst, dst, bank_of(i)[:, :] if len(dst.shape) == 2 else tiles(i), ALU.mult)\
                  .then_inc(S("emptied_dve"), 1)

            for n, i in enumerate(of["q"]):
                silu_result(QT[:, 2 * n:2 * n + 2, :].rearrange("p a t -> p (a t)"), i, "sig", n + 1)
            mean_sq("ctx", D)
            dve.wait_ge(S("rms"), nth("ctx"))
            for t in range(TT):
                ins = V_.tensor_scalar(HN[:, t, :], HN[:, t, :], rs["ctx"][:, t:t + 1], None, ALU.mult)
            ins.then_inc(S("normed"), 1)
            dve.wait_ge(S("sig_c"), 1)
            dve.wait_ge(S("cc"), 1)
            V_.tensor_tensor(CC[:, :, 0:2], CC[:, :, 0:2], CSG, ALU.mult).then_inc(S("silu_c"), 1)
            dve.wait_ge(S("lb"), 1)
            dve.wait_ge(S("emptied_act"), emptied[of["f"][-1]][1])
            for c in range(8):
                ins = V_.tensor_scalar(SF[:, c, :], SF[:, c, :], LBR[:, c:c + 1], LBF[:, c:c + 1], ALU.mult, ALU.add)
            link(ins)
            link(V_.tensor_scalar(KF[:, :, :], SF[:, :, :], -1.0, 1.0, ALU.mult, ALU.add))
            V_.tensor_scalar(SF[:, :, :], SF[:, :, :], F_FLOOR, None, ALU.max).then_inc(S("fgate"), 1)
            for n, i in enumerate(of["og"]):
                silu_result(OG[:, :, 256 * n:256 * n + 256], i, "sig", n + 3)
            dve.wait_ge(S("sumsq"), nth("lat"))
            V_.tensor_scalar(SSL[:, 0:2], SSL[:, 0:2], 1.0 / QR, EPS, ALU.mult, ALU.add)
            V_.tensor_scalar(SSL[:, 2:4], SSL[:, 2:4], 1.0 / KVR, EPS, ALU.mult, ALU.add).then_inc(S("mean_sq"), 1)
            dve.wait_ge(S("rms"), nth("lat"))
            for t in range(TT):
                V_.tensor_scalar(CQ[:, t, :], CQ[:, t, :], RSL[:, t:t + 1], None, ALU.mult)
                ins = V_.tensor_scalar(CK[:, t, 0:P], CK[:, t, 0:P], RSL[:, 2 + t:3 + t], None, ALU.mult)
            ins.then_inc(S("normed"), 1)
            dve.wait_ge(S("lat_ps"), 1)
            for c in range(2):
                V_.tensor_scalar(CQT[:, c, :], B[4][:, c * T:c * T + T], vec("mla_qa_norm", c), None, ALU.mult)
            V_.tensor_scalar(CKT, B[5][:, 0:T], vec("mla_kva_norm"), None, ALU.mult).then_inc(S("latT"), 1)
            for n, i in enumerate(of["uq"]):
                wait_result(dve, i)
                V_.tensor_copy(QKM[:, 0, :, 256 * n:256 * n + 256], tiles(i)).then_inc(S("emptied_dve"), 1)
            dve.wait_ge(S("sumsq"), nth("qk"))
            link(V_.tensor_reduce(SSH, SQ.rearrange("p s a d -> p (s a) d"), AX_X, ALU.add))
            V_.tensor_scalar(SSH, SSH, 1.0 / QK, EPS, ALU.mult, ALU.add).then_inc(S("mean_sq"), 1)
            dve.wait_ge(S("rms"), nth("qk"))
            dve.wait_ge(S("small_in"), SMALL)
            dve.wait_ge(S("sincos"), 1)
            norm_rope(V_, link, 0, M_TMP_Q).then_inc(S("normed"), 1)
            dve.wait_ge(S("normed"), nth("qk"))
            dve.wait_ge(S("mod_sum"), 12)
            V_.tensor_tensor(MODT, B[7][:, 0:32].rearrange("p (a b) -> p a b", a=16),
                             over(vec("b_mod_2", 0, 16).unsqueeze(2), 16, 2), ALU.add)
            for u in range(2):
                bs = BGT[:, 512 * u:512 * u + 512]
                ins = V_.tensor_tensor(bs, bs, B[5 + u][:, :], ALU.add)
            ins.then_inc(S("mod_in"), 1)
            dve.wait_ge(S("mod_in"), 1)
            for s in range(2):
                ins = V_.tensor_scalar(ACOL[:, s, :], MODT[:, 8:16, s], 1.0, None, ALU.add)
            link(ins)
            for s in range(2):
                ins = V_.tensor_tensor(ACOL[:, s, :], ACOL[:, s, :], vec("pre_g_2", 0, 8), ALU.mult)
            link(ins)
            link(V_.tensor_tensor(PG[:], PG[:], BGT, ALU.mult))
            turned("ctx", "cT_dve", lambda k: ACOL[:, 1, k:k + 1], range(DK), lambda k: MODT[:, k, 1:2], 0)
            for h in range(1, MH, 2):
                dve.wait_ge(S("qkT_ps"), h + 1)
                V_.tensor_copy(QKT[0:QK, h, :], B[4 + h % 4][0:QK, :]).then_inc(S("qkT_odd"), 1)
            scale = QK ** -0.5

            def mla_max(h):
                dve.wait_ge(S("mla_s"), h + 1)
                link(V_.tensor_reduce(MX[:, h % 2, :], B[4 + h % 2][:, :].rearrange("p (t k) -> p t k", t=TT), AX_X, ALU.max))
                if h >= 2:
                    dve.wait_ge(S("mla_p"), 2 * (h - 1))
                V_.tensor_scalar(NMX[:, h % 2, :], MX[:, h % 2, :], -scale, None, ALU.mult).then_inc(S("mla_nmax"), 1)

            mla_max(0)
            for h in range(MH):
                if h + 1 < MH:
                    mla_max(h + 1)
                dve.wait_ge(S("mla_p"), 2 * h + 2)
                link(V_.reciprocal(RSM[:, h % 2, :], SUM[:, h % 2, :]))
                dve.wait_ge(S("mla_pv"), h + 1)
                V_.tensor_tensor(OM[:, :, h * VD:h * VD + VD], B[h % 2][:, 0:TT * VD].rearrange("p (t v) -> p t v", t=TT),
                                 over(RSM[:, h % 2, :].unsqueeze(2), TT, VD), ALU.mult).then_inc(S("mla_o"), 1)
            dve.wait_ge(S("logf"), 1)
            for h in range(GH):
                V_.memset(BX[:, h, 0:1], 0.0)
                V_.tensor_tensor_scan(FC[:, h, :], const("ones"), SF[:, h, :], 0.0, ALU.mult, ALU.add)
                ins = V_.tensor_tensor_scan(BX[:, h, 1:T], const("ones")[:, 0:T - 1], SF[:, GH + h, 0:T - 1], 0.0,
                                            ALU.mult, ALU.add)
            ins.then_inc(S("cum"), 1)
            kfl = KF[:, 0:GH, :].rearrange("p h t -> p (h t)")
            kbl = KF[:, GH:2 * GH, :].rearrange("p h t -> p (h t)")
            qfl = QT.rearrange("p h t -> p (h t)")

            def gla_operands(n):
                lv = LEVELS[n]
                dq, dk = DEC[:, n % 2, 0], DEC[:, n % 2, 1]
                if lv == "diag":
                    dve.wait_ge(S("gla_s"), n - 1)
                    V_.tensor_tensor(dk, kfl, kbl, ALU.add).then_inc(S("gla_qk"), 1)
                    return
                dve.wait_ge(S("gla_exp"), n + 1)
                V_.tensor_tensor(dq, dq, qfl, ALU.mult)
                if isinstance(lv, int):
                    def halves(v):
                        v = v.rearrange("p (b two m) -> p b two m", two=2, m=lv)
                        return v[:, :, 0, :], v[:, :, 1, :]
                    (dl, dr), (kl, _), (_, kr) = halves(dk), halves(kfl), halves(kbl)
                    V_.tensor_tensor(dl, dl, kl, ALU.mult)
                    ins = V_.tensor_tensor(dr, dr, kr, ALU.mult)
                else:
                    ins = V_.tensor_tensor(dk, dk, kfl if lv == "base_fwd" else kbl, ALU.mult)
                ins.then_inc(S("gla_qk"), 1)

            def gla_scores(n):
                lv = LEVELS[n]
                dve.wait_ge(S("gla_s"), n + 1)
                if n:
                    dve.wait_ge(S("gla_a"), n)
                for st in range(TT):
                    bank = B[GLA_BANKS[n % 3] + st][:, :].rearrange("p (h t) -> p h t", h=GH)
                    if lv == 128:
                        ins = V_.tensor_copy(AXX[:, st], bank)
                    elif lv == 64:
                        ins = V_.tensor_copy(AD[:, st], bank)
                    else:
                        ins = V_.copy_predicated(AD[:, st], over(MSK[:, MASK_OF[lv]:MASK_OF[lv] + 1, :], GH, P), bank)
                ins.then_inc(S("gla_a"), 1)

            gla_operands(0)
            for n in range(len(LEVELS)):
                if n + 1 < len(LEVELS):
                    gla_operands(n + 1)
                gla_scores(n)
            dve.wait_ge(S("gla_o_ps"), 1)
            for tt in range(TT):
                ins = V_.tensor_copy(OO[:, tt], B[tt][:, :].rearrange("p (h v) -> p h v", h=GH))
            ins.then_inc(S("gla_o"), 1)
            dve.wait_ge(S("sumsq"), nth("o"))
            link(V_.tensor_reduce(SSO, OSQ, AX_X, ALU.add))
            V_.tensor_scalar(SSO, SSO, 1.0 / GK, EPS, ALU.mult, ALU.add).then_inc(S("mean_sq"), 1)
            dve.wait_ge(S("rms"), nth("o"))
            dve.wait_ge(S("small_in"), SMALL)
            oo = OO.rearrange("p t h v -> p (t h) v")
            link(V_.tensor_tensor(oo, oo, over(RSO.unsqueeze(2), 8, GK), ALU.mult))
            link(V_.tensor_tensor(oo, oo, over(ONB[:].unsqueeze(1), 8, GK), ALU.mult))
            oo2 = OO.rearrange("p t h v -> p (t h v)")
            V_.tensor_tensor(oo2, oo2, OG.rearrange("p t c -> p (t c)"), ALU.mult).then_inc(S("normed"), 1)
            def pair(base, n):
                return GATE[:, base + 2 * n:base + 2 * n + 2, :].rearrange("p a t -> p (a t)")
            dve.wait_ge(S("emptied_act"), emptied[of["gate"][-1]][1])
            for n, i in enumerate(of["yb"]):
                wait_result(dve, i)
                V_.tensor_tensor(pair(8, n), pair(8, n), bank_of(i)[:, :], ALU.mult).then_inc(S("emptied_dve"), 1)
            for n, i in enumerate(of["ya"]):
                wait_result(dve, i)
                V_.tensor_tensor(pair(0, n), pair(0, n), bank_of(i)[:, :], ALU.mult).then_inc(S("emptied_dve"), 1)
                dve.wait_ge(S("emptied_dve"), emptied[i][1])
                V_.tensor_tensor(pair(0, n), pair(0, n), pair(8, n), ALU.add).then_inc(S("merged"), 1)
            for n, i in enumerate(of["out"]):
                wait_result(dve, i)
                xs = X[:, :, 256 * n:256 * n + 256]
                V_.tensor_tensor(xs, xs, tiles(i), ALU.add).then_inc(S("emptied_dve"), 1)
            dve.wait_ge(S("pT_ps"), 1)
            V_.tensor_copy(PTR.rearrange("p a t -> p (a t)"), B[4][:, :]).then_inc(S("pT"), 1)

            normalize(X, "hm", lambda t: HN[:, t, :].rearrange("p (k q) -> p k q", k=DK))
            dve.wait_ge(S("small_in"), SMALL)
            turned("hm", "rT_dve", lambda k: LNM[:, k:k + 1])
            dve.wait_ge(S("logits_ps"), 1)
            dve.wait_ge(S("small_in"), SMALL)
            link(V_.tensor_tensor(LGT, B[4][:, 0:144].rearrange("p (t c) -> p t c", t=TT), over(RB[:].unsqueeze(1), TT, 72),
                                  ALU.add))
            g = LGT[:, :, 0:8]
            rev = over(const("rev8").unsqueeze(1), TT, 8)

            def first_max(v, mx, onehot):
                link(V_.tensor_reduce(mx, v, AX_X, ALU.max))
                link(V_.tensor_tensor(VAL, v, over(mx.unsqueeze(2), TT, 8), ALU.is_equal))
                link(V_.tensor_tensor(VAL, VAL, rev, ALU.mult))
                link(V_.tensor_reduce(VMX, VAL, AX_X, ALU.max))
                return V_.tensor_tensor(onehot, VAL, over(VMX.unsqueeze(2), TT, 8), ALU.is_equal)

            first_max(g, GMX, GOH).then_inc(S("group"), 1)
            V_.tensor_tensor(GEXP, g, over(GMX.unsqueeze(2), TT, 8), ALU.subtract).then_inc(S("gdiff"), 1)
            dve.wait_ge(S("group"), 1)
            for t in range(TT):
                link(V_.tensor_tensor(GEX, LGT[:, t, 8:72].rearrange("p (g e) -> p g e", g=NG),
                                      over(GOH[:, t, :].unsqueeze(2), NG, EPG), ALU.mult))
                link(V_.tensor_reduce(EL[:, t, :], GEX.rearrange("p g e -> p e g"), AX_X, ALU.add))
            link(first_max(EL, M1, O1))
            link(V_.scalar_tensor_tensor(out=EL2, in0=O1, scalar=-1e30, in1=EL, op0=ALU.mult, op1=ALU.add))
            link(first_max(EL2, M2, O2))
            V_.tensor_tensor(DLT, M2, M1, ALU.subtract).then_inc(S("ediff"), 1)
            dve.wait_ge(S("gexp"), 1)
            link(V_.tensor_reduce(GSM, GEXP, AX_X, ALU.add))
            link(V_.reciprocal(PGR, GSM))
            dve.wait_ge(S("eexp"), 1)
            link(V_.tensor_scalar(DEN, E2W, 1.0, None, ALU.add))
            link(V_.reciprocal(W1, DEN))
            link(V_.tensor_tensor(W1, W1, PGR, ALU.mult))
            link(V_.tensor_tensor(W2, W1, E2W, ALU.mult))
            link(V_.tensor_tensor(O1, O1, over(W1.unsqueeze(2), TT, 8), ALU.mult))
            link(V_.tensor_tensor(O2, O2, over(W2.unsqueeze(2), TT, 8), ALU.mult))
            V_.tensor_tensor(WT, O1, O2, ALU.add)
            dve.wait_ge(S("rank_ps"), 1)
            V_.tensor_copy(RK, B[5][:, 0:16].rearrange("p (t g) -> p t g", t=TT))
            link(V_.tensor_copy(CNT, B[5][:, 16:24]))
            link(V_.tensor_scalar(NR, CNT, 0.5, None, ALU.is_gt))
            for lot in range(1, T // SLOT):
                link(V_.scalar_tensor_tensor(out=NR, in0=CNT, scalar=SLOT * lot + 0.5, in1=NR, op0=ALU.is_gt, op1=ALU.add))
            link(V_.tensor_scalar(NR[:, 0:1], NR[:, 0:1], 1.0, None, ALU.max))
            link(V_.tensor_tensor_scan(ENDS, const("ones")[:, 0:8], NR, 0.0, ALU.mult, ALU.add))
            link(V_.tensor_tensor(STA, ENDS, NR, ALU.subtract))
            link(V_.scalar_tensor_tensor(out=RK, in0=over(STA.unsqueeze(1), TT, 8), scalar=float(SLOT), in1=RK,
                                         op0=ALU.mult, op1=ALU.add))
            link(V_.tensor_tensor(RK, RK, GOH, ALU.mult))
            link(V_.tensor_reduce(POS, RK, AX_X, ALU.add))
            link(V_.tensor_tensor(TAB, over(ENDS.unsqueeze(1), ROUNDS, 8), over(const("round_id").unsqueeze(2), ROUNDS, 8),
                                  ALU.is_le))
            link(V_.tensor_reduce(TABR, TAB, AX_X, ALU.add))
            link(V_.tensor_scalar(TABR, TABR, float(NG - 1), None, ALU.min))
            V_.tensor_copy(RT[:, 1:1 + ROUNDS], TABR)
            V_.tensor_scalar(RT[:, 14:15], ENDS[:, 7:8], float(NM), float(-RING), ALU.mult, ALU.add)
            V_.tensor_copy(RT[:, 0:1], ENDS[:, 7:8]).then_inc(S("table"), 1)
            dve.wait_ge(S("table"), 1)

            def select():
                for t in range(TT):
                    ins = V_.tensor_scalar(SEL[:, t, :], const("iota_slot"), POS[:, t:t + 1], None, ALU.is_equal)
                ins.then_inc(S("sel"), 1)

            def moe_round(r):
                def at(n, k):
                    return r * n + k

                dve.wait_ge(S("sel"), at(1, 1))
                V_.tensor_scalar(POS, POS, float(SLOT), None, ALU.subtract).then_inc(S("pos_next"), 1)
                dve.wait_ge(S("gath_ps"), at(1, 1))
                V_.tensor_tensor(XG, B[0][:, :].rearrange("p (k s) -> p k s", k=DK), over(LNM[:].unsqueeze(2), DK, SLOT),
                                 ALU.mult).then_inc(S("gath"), 1)
                dve.wait_ge(S("sel_ps"), at(1, 1))
                for e in range(2):
                    rows = slice(e * SLOT, e * SLOT + SLOT)
                    ins = V_.tensor_copy(WPR[rows, :], B[1][rows, 0:EPG].rearrange("p (q e) -> p q e", e=2)[:, :, e])
                ins.then_inc(S("wpr"), 1)
                dve.wait_ge(S("wpr"), at(1, 1))
                for p in range(PAIRS):
                    bank = B[3 + p % 2]
                    dve.wait_ge(S("moe_sig"), at(PAIRS, p + 1))
                    V_.tensor_tensor(SGM[:, p % 2], SGM[:, p % 2], bank[:, 0:FE], ALU.mult).then_inc(S("moe_silu"), 1)
                    dve.wait_ge(S("moe_silu"), at(PAIRS, p + 1))
                    V_.scalar_tensor_tensor(out=HHR[:, p % 2], in0=bank[:, FE:2 * FE], scalar=WPR[:, p:p + 1],
                                            in1=SGM[:, p % 2], op0=ALU.mult, op1=ALU.mult).then_inc(S("hid"), 1)
                    if p == 0:
                        dve.wait_ge(S("str"), at(1, 1))
                        dve.wait_ge(S("pos_next"), at(1, 1))
                        select()
                dve.wait_ge(S("scat_ps"), at(1, 1))
                for t in range(TT):
                    for half in range(2):
                        xs = X[:, t, half * 512:half * 512 + 512]
                        ins = V_.tensor_tensor(xs, xs, B[2 * t + half][:, :], ALU.add)
                ins.then_inc(S("moe_x"), 1)
                dve.wait_ge(S("moe_x"), at(1, 1))

            select()
            moe_round(0)
            rounds = dve.value_load(RT[0:1, 0:1], min_val=4, max_val=ROUNDS)
            with dve.Fori(1, rounds) as r:
                moe_round(r)

            normalize(X, "ple")
            turned("ple", "pleT_dve", lambda k: vec("ln_ple", k))
            for n, i in enumerate(of["ple"]):
                dve.wait_ge(S("emptied_act"), emptied[i][1])
                link(V_.tensor_tensor(SG[:, n % 2], SG[:, n % 2], PP[:, :, 256 * n:256 * n + 256], ALU.mult))
                xs = X[:, :, 256 * n:256 * n + 256]
                V_.tensor_tensor(xs, xs, SG[:, n % 2], ALU.add).then_inc(S("ple_x"), 1)
            normalize(X, "two")
            turned("two", "twoT", lambda k: ACOL[:, 0, k:k + 1], range(DK), lambda k: MODT[:, k, 0:1])
            for n, i in enumerate(of["zb"]):
                silu_result(ZB[:, :, 256 * n:256 * n + 256], i, "sig2", n + 1)
            V_.memset(UC[:, :, 0:1], 0.0)
            V_.memset(UC[:, :, T + 1:T + 2], 0.0)

            def two(tile, n):
                return tile[:, 2 * n:2 * n + 2, :].rearrange("p a t -> p (a t)")

            for n, i in enumerate(of["za"]):
                silu_result(two(YA, n), i, "sig2", n + 5)
            for n, i in enumerate(of["b"]):
                wait_result(dve, i)
                dve.wait_ge(S("emptied_dve"), emptied[of["za"][n]][1])
                V_.tensor_tensor(two(YA, n), two(YA, n), bank_of(i)[:, :], ALU.mult).then_inc(S("emptied_dve"), 1)
            for n, i in enumerate(of["xin"]):
                wait_result(dve, i)
                dve.wait_ge(S("emptied_act"), emptied[of["c"][n]][1])
                u = UC[:, 2 * n:2 * n + 2, 1:T + 1]
                V_.tensor_tensor(u, u, bank_of(i)[:, :].rearrange("p (a t) -> p a t", a=2), ALU.mult)\
                  .then_inc(S("emptied_dve"), 1)
            dve.wait_ge(S("emptied_dve"), emptied[of["xin"][-1]][1])

            def conv_chunk(k):
                cv = V2[:, k % 2, 0:T]
                link(V_.tensor_scalar(cv, UC[:, k, 0:T], vec("conv_w_2", k), vec("conv_b_2", k), ALU.mult, ALU.add))
                link(V_.scalar_tensor_tensor(out=cv, in0=UC[:, k, 1:T + 1], scalar=vec("conv_w_2", 8 + k), in1=cv,
                                             op0=ALU.mult, op1=ALU.add))
                link(V_.scalar_tensor_tensor(out=cv, in0=UC[:, k, 2:T + 2], scalar=vec("conv_w_2", 16 + k), in1=cv,
                                             op0=ALU.mult, op1=ALU.add))
                return V_.tensor_tensor(YA[:, k, :], YA[:, k, :], cv, ALU.mult)

            for m in range(8):
                conv_chunk(m).then_inc(S("conv"), 1)
                s = 1.0 if m >= 4 else HD ** -0.5
                dst = two(QT2 if m < 4 else KT2, m % 4)
                i = (of["q2"] + of["k2"])[m]
                dve.wait_ge(S("rot_ps"), m + 1)
                d3 = dst.rearrange("p (a t) -> p a t", a=2)
                V_.tensor_tensor(d3, B[4 + m % 2][:, :].rearrange("p (a t) -> p a t", a=2),
                                 over(const("sinT").unsqueeze(1), 2, T), ALU.mult)
                raw = RAW[:, m % 2, :].rearrange("p (a t) -> p a t", a=2)
                link(V_.tensor_tensor(RTM[:, m % 2, :].rearrange("p (a t) -> p a t", a=2), raw,
                                      over(const("cosT").unsqueeze(1), 2, T), ALU.mult))
                if m >= 4:
                    V_.tensor_tensor(dst, dst, RTM[:, m % 2, :], ALU.add).then_inc(S("roped"), 1)
                else:
                    link(V_.tensor_tensor(dst, dst, RTM[:, m % 2, :], ALU.add))
                    V_.tensor_scalar(dst, dst, s, None, ALU.mult).then_inc(S("roped"), 1)

            def na_max(n):
                dve.wait_ge(S("na_s"), n + 1)
                bank = B[4 + n % 2]
                link(V_.tensor_reduce(MX2[:, n % 2:n % 2 + 1], bank[:, :], AX_X, ALU.max))
                if n >= 2:
                    dve.wait_ge(S("na_p"), n - 1)
                V_.tensor_scalar(NMX2[:, n % 2:n % 2 + 1], MX2[:, n % 2:n % 2 + 1], -1.0, None, ALU.mult)\
                  .then_inc(S("na_nmax"), 1)

            na_max(0)
            for n in range(H2 * TT):
                h, t = divmod(n, TT)
                if n + 1 < H2 * TT:
                    na_max(n + 1)
                dve.wait_ge(S("na_p"), n + 1)
                link(V_.reciprocal(RSM2[:, n % 2:n % 2 + 1], SUM2[:, n % 2:n % 2 + 1]))
                dve.wait_ge(S("na_pv"), n + 1)
                V_.scalar_tensor_tensor(out=HN[:, t, h * HD:h * HD + HD], in0=B[n % 2][:, 0:HD],
                                        scalar=RSM2[:, n % 2:n % 2 + 1], in1=ZB[:, t, h * HD:h * HD + HD],
                                        op0=ALU.mult, op1=ALU.mult).then_inc(S("na_o"), 1)
            for n, i in enumerate(of["yconv"]):
                wait_result(dve, i)
                V_.tensor_tensor(two(GA, n), two(GA, n), bank_of(i)[:, :], ALU.mult).then_inc(S("emptied_dve"), 1)
            for n, i in enumerate(of["yattn"]):
                wait_result(dve, i)
                V_.tensor_tensor(two(GB, n), two(GB, n), bank_of(i)[:, :], ALU.mult).then_inc(S("emptied_dve"), 1)
                dve.wait_ge(S("emptied_dve"), emptied[i][1])
                V_.tensor_tensor(two(GA, n), two(GA, n), two(GB, n), ALU.add).then_inc(S("merged2"), 1)
            for n, i in enumerate(of["wo"]):
                wait_result(dve, i)
                V_.tensor_copy(YF[:, :, 256 * n:256 * n + 256], tiles(i)).then_inc(S("emptied_dve"), 1)
            mean_sq("y", D)
            dve.wait_ge(S("rms"), nth("y"))
            for t in range(TT):
                link(V_.scalar_tensor_tensor(out=YF[:, t, :], in0=YF[:, t, :], scalar=rs["y"][:, t:t + 1], in1=PG[:],
                                             op0=ALU.mult, op1=ALU.mult))
                V_.tensor_tensor(HN[:, t, :], YF[:, t, :], X[:, t, :], ALU.add).then_inc(S("final"), 1)


_NAMES = ["x", "p", "positions", "ln_mix", "w_in", "hg_lb", "hg_onorm", "w_oA", "mla_qa_norm", "mla_kva_norm", "w_uq",
          "w_ukv", "q_norm", "k_norm", "w_oB", "w_out", "ln_moe", "w_rg", "b_rg", "w_re", "b_re", "w1", "w3", "w2",
          "ln_ple", "w_ple_gate", "w_ple_proj", "c_2", "ctx_2", "c_ctx_2", "w_mod_2", "b_mod_2", "pre_g_2", "post_g_2",
          "w_in_2", "conv_w_2", "conv_b_2", "w_out_conv_2", "w_out_attn_2", "w_o_2"]


def kernel(**inputs):
    import concourse.bacc as bacc
    from concourse.bass_utils import run_bass_kernel_spmd

    nc = bacc.Bacc("TRN2", target_bir_lowering=False, num_devices=1)
    arrays = {n: np.ascontiguousarray(inputs[n]) for n in _NAMES}
    rpb = np.asarray(inputs["rpb_2"])[0]
    table = np.zeros((H2, ROWS, 2 * GW - 1, ROWS), rpb.dtype)
    for qr in range(ROWS):
        table[:, qr, GW - WIN:GW + WIN - 1, :] = rpb[:, 7 - qr:7 - qr + ROWS, :].transpose(0, 2, 1)
    arrays["toeplitz"] = table.reshape(-1)
    arrays["consts"], arrays["masks"] = constants()
    a, maps = {}, {}
    for n, v in arrays.items():
        maps["in_" + n] = v
        a[n] = nc.dram_tensor("in_" + n, v.shape, mybir.dt.from_np(v.dtype), kind="ExternalInput").ap()
    out = nc.dram_tensor("out", (1, T, D), F32, kind="ExternalOutput").ap()
    build(nc, a, out)
    r = run_bass_kernel_spmd(nc, [maps], core_ids=[0])
    return r.results[0]["out"]
```

```python
from contextlib import ExitStack

import numpy as np

import concourse.bass as bass
from concourse import mybir

F32 = mybir.dt.float32
I32 = mybir.dt.int32
U8 = mybir.dt.uint8
ALU = mybir.AluOpType
ACT = mybir.ActivationFunctionType
AX_X = mybir.AxisListType.X

P = 128
T = 256
TT = T // P
D = 1024
DK = D // P
EPS = 1e-6

GH, GK = 4, 128
F_FLOOR = float(np.exp(-20.0))
MH, NOPE, ROPE, VD = 8, 64, 32, 64
QK = NOPE + ROPE
QR, KVR = 256, 128
NG, EPG = 8, 8
FE = 256
SLOT = 64
ROUNDS = (T - NG) // SLOT + NG
COL_Q, COL_FF, COL_FB, COL_V, COL_OG = 0, 512, 1024, 1536, 2048
COL_CQ, COL_CKV, COL_GA, COL_GB = 2560, 2816, 2976, 4000

H2, HD = 16, 64
GW, ROWS, WIN = 64, 4, 16
C_B, C_C, C_X, C_ZA, C_Q, C_K, C_V, C_ZB, C_GA, C_GB = [1024 * i for i in range(10)]
TOEP = (2 * GW - 1) * ROWS

RING = 8
LEVELS = [128, 64, 32, 16, 8, "base_fwd", "base_bwd", "diag"]
GLA_BANKS = (0, 4, 6)
MASK_OF = {32: 0, 16: 1, 8: 2, "base_fwd": 3, "base_bwd": 4, "diag": 5}

VEC_ROWS, _at = {}, 0
for _name, _n in (("pre_g_2", 8), ("b_mod_2", 16), ("conv_w_2", 24), ("conv_b_2", 8), ("c_2", 8), ("c_ctx_2", 8),
                  ("ln_mix", 8), ("ln_ple", 8), ("mla_qa_norm", 2), ("mla_kva_norm", 1), ("hg_lb", 16)):
    VEC_ROWS[_name] = (_at, _n)
    _at += _n
NVEC = _at

CONST_COLS, _at = {}, 0
for _name, _n in (("ident", 128), ("ustrict", 128), ("ones", 256), ("rot", 128), ("cosT", 256), ("sinT", 256),
                  ("winmask", 256), ("flip", 128), ("invfreq", 16), ("iota_slot", 128), ("rev8", 8), ("pick2", 2), ("row0", 128), ("round_id", ROUNDS)):
    CONST_COLS[_name] = (_at, _n)
    _at += _n
NCONST = _at


def constants():
    c = np.zeros((P, NCONST), np.float32)

    def put(name, value):
        a, n = CONST_COLS[name]
        c[:, a:a + n] = value

    i = np.arange(P)
    put("ident", np.eye(P))
    put("ustrict", i[:, None] < i[None, :])
    put("ones", 1.0)
    rot = np.zeros((P, P))
    for r in range(P):
        if (r % 32) < 16:
            rot[r + 16, r] = -1.0
        else:
            rot[r - 16, r] = 1.0
    put("rot", rot)
    half = HD // 2
    inv = 10000.0 ** (-np.arange(0, half, 2, dtype=np.float32) / np.float32(half))
    t = np.arange(T)
    d = np.arange(P) % HD
    where = np.where(d[:, None] < 32, (t // GW)[None, :], (t % GW)[None, :]).astype(np.float32)
    ang = where * inv.astype(np.float32)[d % 16][:, None]
    put("cosT", np.cos(ang.astype(np.float64)))
    put("sinT", np.sin(ang.astype(np.float64)))
    qc = GW - 1 - i % GW
    put("flip", (i[:, None] // GW == i[None, :] // GW) & (i[:, None] % GW == GW - 1 - i[None, :] % GW))
    start = np.clip(qc - WIN // 2, 0, GW - WIN)
    kc = np.arange(T) // ROWS
    inside = (kc[None, :] >= start[:, None]) & (kc[None, :] < start[:, None] + WIN)
    put("winmask", np.where(inside, 0.0, -1e30))
    put("invfreq", 10000.0 ** (-np.arange(16, dtype=np.float32) / np.float32(16)))
    put("iota_slot", np.arange(P) % SLOT)
    put("rev8", 8 - np.arange(8))
    put("pick2", i[:, None] % 32 == np.arange(2)[None, :])
    put("row0", (i % 32 == 0)[:, None])
    put("round_id", np.arange(ROUNDS))
    m = np.zeros((P, 6, P), np.float32)
    s, t2 = i[:, None], i[None, :]
    m[:, 0] = s // 64 == t2 // 64
    m[:, 1] = s // 32 == t2 // 32
    m[:, 2] = s // 16 == t2 // 16
    m[:, 3] = s // 8 == t2 // 8
    m[:, 4] = (s // 8 == t2 // 8) & (s > t2)
    m[:, 5] = s == t2
    return c, m


def build(nc, a, out):
    with ExitStack() as ctx:
        sems = {}

        def S(name):
            if name not in sems:
                sems[name] = ctx.enter_context(nc.semaphore(name))
            return sems[name]

        def sb(name, shape, dt=F32):
            return ctx.enter_context(nc.sbuf_tensor(name, shape, dt))

        ring = sb("ring", [P, RING, 2048])
        X = sb("X", [P, TT, D])
        HN = sb("HN", [P, TT, D])
        HT = sb("HT", [P, DK, T])
        CST = sb("CST", [P, NCONST])
        MSK = sb("MSK", [P, 6, P], U8)
        VROW = sb("VROW", [P, P])
        VEC = sb("VEC", [P, NVEC])
        QKN = sb("QKN", [P, 2, QK])
        ONB = sb("ONB", [P, GK])
        RB = sb("RB", [P, 72])
        RW = sb("RW", [P, DK, 72])
        LNM = sb("LNM", [P, DK])
        PG = sb("PG", [P, D])
        POSI = sb("POSI", [P, TT], I32)
        SM = sb("SM", [P, 1200])
        RT = sb("RT", [P, 16], I32)
        sm_at = [0]

        def small(*shape):
            n = int(np.prod(shape))
            v = SM[:, sm_at[0]:sm_at[0] + n]
            sm_at[0] += n
            if len(shape) == 2:
                v = v.rearrange("p (a b) -> p a b", a=shape[0])
            if len(shape) == 3:
                v = v.rearrange("p (a b c) -> p a b c", a=shape[0], b=shape[1])
            return v

        AR = sb("AR", [P, 25152])

        def area(at, *shape):
            n = int(np.prod(shape))
            assert at + n <= 25152, (at, shape)
            v = AR[:, at:at + n]
            if len(shape) == 2:
                v = v.rearrange("p (a b) -> p a b", a=shape[0])
            if len(shape) == 3:
                v = v.rearrange("p (a b c) -> p a b c", a=shape[0], b=shape[1])
            if len(shape) == 4:
                v = v.rearrange("p (a b c d) -> p a b c d", a=shape[0], b=shape[1], c=shape[2])
            return v

        def const(name):
            at, n = CONST_COLS[name]
            return CST[:, at:at + n]

        def vec(name, k=0, n=1):
            at = VEC_ROWS[name][0] + k
            return VEC[:, at:at + n]

        def over(ap, *shape):
            return ap.to_broadcast([P] + list(shape))

        ident = const("ident")
        QT = area(0, GH, T)
        SF = area(1024, 2 * GH, T)
        KF = area(3072, 2 * GH, T)
        V = area(5120, TT, 512)
        OG = area(6144, TT, 512)
        GATE = area(7168, 16, T)
        OM = area(11264, TT, 512)
        MSF = area(7168, 6 * P)
        M0 = 12288
        CQ = area(M0, TT, QR)
        CK = area(M0 + 512, TT, 160)
        CQT = area(M0 + 832, 2, T)
        CKT = area(M0 + 1344, T)
        KV = area(M0 + 1600, TT, D)
        QKM = area(M0 + 3648, 2, TT, MH * QK)
        QKT = area(M0 + 6720, MH, 512)
        SQ = area(M0 + 6720, 2, TT * MH, QK)
        PR = area(M0 + 10816, 2, TT, T)
        PT = area(M0 + 11840, 2, TT, T)
        FC = area(M0, GH, T)
        BX = area(M0 + 1024, GH, T)
        DEC = area(M0 + 2048, 2, 2, GH * T)
        AD = area(M0 + 6144, 2, GH, P)
        AXX = area(M0 + 7168, 2, GH, P)
        OO = area(M0 + 8192, TT, GH, GK)
        OSQ = area(M0, TT * GH, GK)
        OTG = area(M0 + 2048, GH, T)
        OTM = area(M0 + 3072, GH, T)
        KC = area(1024, DK, T)
        VC = area(M0 + 10816, TT, D)
        PP = area(3072, TT, D)
        PRAW = area(5120, TT, T)
        PTR = area(5632, 2, T)
        CSQ = area(M0 + 6720, TT, D)
        BGT = area(M0 + 10816, D)
        MRW = area(M0 + 11840, 2, 256)
        E0 = 6144
        SEL = area(E0, TT, P)
        XG = area(E0 + 256, DK, SLOT)
        STR = area(E0 + 768, T)
        SGM = area(E0 + 1024, 2, FE)
        HHR = area(E0 + 1536, 2, FE)
        HHT = area(E0 + 2048, 2, 2, P)
        YY = area(E0 + 2560, 512)
        LGT = area(E0 + 3072, TT, 72)
        GEX = area(E0 + 3216, NG, EPG)
        SG = area(E0, 2, TT, T)
        E0 = 3072
        GA = area(E0, DK, T)
        GB = area(E0 + 2048, DK, T)
        ZB = area(E0 + 4096, DK, T)
        YA = area(E0 + 6144, DK, T)
        UC = area(E0 + 8192, DK, T + 2)
        BT = area(E0 + 8192, 2, TT, T)
        BM = area(E0 + 9216, 3, T)
        QT2 = area(E0 + 10256, DK, T)
        KT2 = area(E0 + 12304, DK, T)
        V2 = area(E0 + 14352, TT, D)
        RAW = area(E0 + 16400, 2, 512)
        RTM = area(E0 + 17424, 2, 512)
        PR2 = area(E0 + 16400, 3, 512)
        PT2 = [HN[:].rearrange("p t d -> p (t d)").rearrange("p (h k q) -> p h k q", h=2, k=4),
               area(E0 + 17936, 2, 4, T)]
        YF = area(E0 + 10256, TT, D)

        MODT = small(16, 2)
        CC = small(DK, 32)
        CSG = small(DK, 2)
        ACOL = small(2, DK)
        LBF = small(8)
        LBR = small(8)
        NHALF = small(32)
        ss = {n: small(2) for n in ("x", "hm", "ctx", "ple", "two", "y")}
        rs = {n: small(2) for n in ss}
        SSL, RSL = small(4), small(4)
        SS2, SSY = small(TT, 4), small(TT, 4)
        SSH, RSH = small(32), small(32)
        SSO, RSO = small(8), small(8)
        ANG, CS, SN = small(TT, 16), small(TT, 16), small(TT, 16)
        POSF, KQ, RED = small(2), small(TT, 16), small(TT, 16)
        MX, NMX, SUM, RSM = small(2, 2), small(2, 2), small(2, 2), small(2, 2)
        MX2, NMX2, SUM2, RSM2 = small(2), small(2), small(2), small(2)
        GMX, GEXP, GSM, PGR = small(2), small(TT, 8), small(2), small(2)
        VAL, VMX, GOH = small(TT, 8), small(2), small(TT, 8)
        EL, EL2, M1, M2, O1, O2 = small(TT, 8), small(TT, 8), small(2), small(2), small(TT, 8), small(TT, 8)
        DLT, E2W, DEN, W1, W2 = small(2), small(2), small(2), small(2), small(2)
        WT = small(TT, 8)
        WPR = small(EPG // 2)
        CNT, NR, ENDS, STA = small(8), small(8), small(8), small(8)
        RK, POS = small(TT, 8), small(2)
        TAB = small(ROUNDS, 8)
        TABR = small(ROUNDS)

        B = [ctx.enter_context(nc.psum_tensor(f"bank{i}", [P, 512], F32)) for i in range(8)]

        def wcols(w, c0, n, k=DK):
            return w[0].rearrange("(k p) n -> p k n", p=P)[:, :, c0:c0 + n], k, n

        w_in, w_in2 = a["w_in"], a["w_in_2"]
        fills = []
        results = []

        def fill(src, name, feature=True, ncols=256):
            fills.append(src)
            k, n = src[1], src[2]
            for c0 in range(0, n, ncols):
                results.append((name, len(fills) - 1, c0, feature, min(ncols, n - c0)))

        fill(wcols(w_in, COL_CQ, 256), name="cq", feature=False)
        fill(wcols(w_in, COL_CKV, 160), name="ckv", feature=False)
        for c in range(2):
            fill(wcols(w_in, COL_FF + 256 * c, 256), name="f")
        for c in range(2):
            fill(wcols(w_in, COL_FB + 256 * c, 256), name="f")
        fill(wcols(a["w_uq"], 0, 768, 2), name="uq", feature=False)
        fill(wcols(a["w_ukv"], 0, 1024, 1), name="ukv", feature=False)
        for c in range(6):
            name, col = (("q", COL_Q), ("v", COL_V), ("og", COL_OG))[c // 2]
            fill(wcols(w_in, col + 256 * (c % 2), 256), name=name, feature=(name == "q"))
            for m in (2 * c, 2 * c + 1):
                fill(wcols(a["w_mod_2"], 256 * m, 256), name="mod")
        for c in range(8):
            fill(wcols(w_in, COL_GA + 256 * c, 256), name="gate")
        for c in range(4):
            fill(wcols(w_in2, C_K + 256 * c, 256), name="kc")
        for c in range(4):
            fill(wcols(w_in2, C_V + 256 * c, 256), name="vc", feature=False)
        for c in range(2):
            fill(wcols(a["w_oB"], 512 * c, 512, 4), name="yb")
        for c in range(2):
            fill(wcols(a["w_oA"], 512 * c, 512, 4), name="ya")
        for c in range(4):
            fill(wcols(a["w_out"], 256 * c, 256), name="out", feature=False)
        fill(wcols(a["w_ple_proj"], 0, 1024, 2), name="pp", feature=False)
        NA = len(fills)
        NRA = len(results)
        for c in range(4):
            fill(wcols(a["w_ple_gate"], 256 * c, 256), name="ple", feature=False)
        for name, col, feature in (("zb", C_ZB, True), ("ga", C_GA, True), ("gb", C_GB, True), ("za", C_ZA, True),
                                   ("b", C_B, True), ("c", C_C, True), ("xin", C_X, True), ("q2", C_Q, True),
                                   ("k2", C_K, True), ("v2", C_V, False)):
            for c in range(4):
                fill(wcols(w_in2, col + 256 * c, 256), name=name, feature=feature)
        for c in range(4):
            fill(wcols(a["w_out_conv_2"], 256 * c, 256), name="yconv")
        for c in range(4):
            fill(wcols(a["w_out_attn_2"], 256 * c, 256), name="yattn")
        for c in range(4):
            fill(wcols(a["w_o_2"], 256 * c, 256), name="wo", feature=False)
        NC_ = len(fills) - NA
        last_result = {f: i for i, (_, f, _, _, _) in enumerate(results)}
        of = {}
        for i, r in enumerate(results):
            of.setdefault(r[0], []).append(i)

        EMPTIER = {"cq": "dve", "ckv": "dve", "f": "act", "q": "dve", "v": "act", "og": "dve", "uq": "dve",
                   "ukv": "act", "gate": "act", "yb": "dve", "ya": "dve", "out": "dve", "mod": "act",
                   "kc": "act", "vc": "act", "pp": "act", "ple": "act", "zb": "dve", "ga": "act", "gb": "act",
                   "za": "dve", "b": "dve", "c": "act", "xin": "dve", "q2": "act", "k2": "act", "v2": "act",
                   "yconv": "dve", "yattn": "dve", "wo": "dve"}
        emptied, _n = {}, {"dve": 0, "act": 0}
        for i, r in enumerate(results):
            e = EMPTIER[r[0]]
            _n[e] += 1
            emptied[i] = (e, _n[e])

        def ready_sem(i):
            return ("res_a", i + 1) if i < NRA else ("res_c", i - NRA + 1)

        def wait_result(eng, i):
            n, v = ready_sem(i)
            eng.wait_ge(S(n), v)

        bank_no = [2 + n % 2 if r[0] in ("gate", "kc", "vc") else n % 4 for n, r in enumerate(results)]

        def bank_of(i):
            return B[bank_no[i]]

        def bank_before(i):
            return max((j for j in range(i) if bank_no[j] == bank_no[i]), default=None)

        PAIRS = EPG // 2

        def ups(p):
            return [("up", 2 * p + e, half) for half in range(2) for e in range(2)]

        def downs(p):
            return [("down", 2 * p + e, 0) for e in range(2)]

        moe_order = ups(0) + ups(1) + downs(0) + ups(2) + downs(1) + ups(3) + downs(2) + downs(3)
        moe_index = {key: j for j, key in enumerate(moe_order)}
        NM = len(moe_order)
        C_BASE = NA % RING

        MRING, EXTRA = 12, (12, 13)
        beside = area(M0 - 2048, MRING - RING + len(EXTRA), 2048)

        def moe_slot(j):
            return j % MRING

        def expert_slot(j, extra):
            if extra:
                return beside[:, MRING - RING + EXTRA.index(j), :]
            m = moe_slot(j)
            return beside[:, m, :] if m < MRING - RING else ring[:, (C_BASE + m - (MRING - RING)) % RING, :]

        slot_sum, slot_after = {}, []
        for _j, _key in enumerate(moe_order):
            _s = moe_slot(_j)
            slot_sum[_s] = slot_sum.get(_s, 0) + (32 if _key[0] == "up" else 16)
            slot_after.append(slot_sum[_s])

        missing = {moe_slot(j): 32 for j in EXTRA}

        def c_slot(f):
            return (C_BASE + f - NA) % RING

        def slot_of(f):
            return f % RING if f < NA else c_slot(f)

        def slot_view(f):
            _, k, n = fills[f]
            return ring[:, slot_of(f), 0:k * n].rearrange("p (k n) -> p k n", k=k)

        EARLY, SMALL = 16 * 12, 16 * 11
        NORMS = ["x", "lat", "ctx", "qk", "o", "hm", "ple", "two", "y"]
        NORMED = [n for n in NORMS if n not in ("ple", "y")]
        TURNS = ["x", "ctx", "hm", "ple", "two"]

        def nth(tag, seq=NORMS):
            return seq.index(tag) + 1

        block = ctx.enter_context(nc.Block())

        @block.sync
        def _(sp):
            sp.dma_start(X[:], a["x"][0].rearrange("(t p) d -> p t d", p=P)).then_inc(S("x_in"), 16)

            sp.dma_start(CST[:], a["consts"]).then_inc(S("early_in"), 16)
            for name, (row, n) in VEC_ROWS.items():
                v = a[name]
                if name == "b_mod_2":
                    src = v[0, 0:2048].rearrange("(r p) -> r p", p=P)
                elif name == "conv_w_2":
                    src = v[0].rearrange("k (r p) -> (k r) p", p=P)
                elif name == "hg_lb":
                    src = v.rearrange("d j (r p) -> (d j r) p", p=P)
                elif name == "c_ctx_2":
                    src = v.rearrange("(r p) -> r p", p=P)
                else:
                    src = v[0].rearrange("(r p) -> r p", p=P)
                sp.dma_start(VROW[row:row + n, :], src).then_inc(S("early_in"), 16)
            sp.wait_ge(S("early_in"), EARLY)

            def stream_a():
                for f in range(NA):
                    if f >= RING:
                        sp.wait_ge(S("res_a"), last_result[f - RING] + 1)
                    sp.dma_start(slot_view(f), fills[f][0]).then_inc(S(f"arr_a{slot_of(f)}"), 16)

            stream_a()

            def expert_dma(j, g, extra=False):
                kind, e, half = moe_order[j]
                dst = expert_slot(j, extra)
                arrived = S("arr_extra") if extra else S(f"arr_m{moe_slot(j)}")
                if kind == "down":
                    src = a["w2"][0, bass.ds(g * EPG + e, 1), :, :].rearrange("o (c p) n -> p (o c) n", p=P)
                    sp.dma_start(dst.rearrange("p (c n) -> p c n", c=2), src).then_inc(arrived, 16)
                else:
                    for w, name in enumerate(("w1", "w3")):
                        src = a[name][0, bass.ds(g * EPG + e, 1), :, :].rearrange("o (p k) n -> p (o k) n", p=P)
                        sp.dma_start(dst.rearrange("p (k n) -> p k n", k=DK // 2)[:, :, w * FE:w * FE + FE],
                                     src[:, half * DK // 2:(half + 1) * DK // 2, :]).then_inc(arrived, 16)

            for j in (4, 5, 6, 0, 1, 2, 3, 7, 8, 9, 10, 12, 13, 11):
                if j in EXTRA or j < MRING - RING:
                    sp.wait_ge(S("merged"), 4)
                else:
                    sp.wait_ge(S("res_a"), last_result[NA - MRING + j] + 1)
                expert_dma(j, 0, extra=j in EXTRA)
            for j in range(MRING + len(EXTRA), NM):
                sp.wait_ge(S("moe_used"), j - MRING + 1)
                expert_dma(j, 0)
            sp.wait_ge(S("table"), 1)
            rounds = sp.value_load(RT[0:1, 0:1], min_val=4, max_val=ROUNDS)
            with sp.Fori(0, rounds - 1) as r:
                g = sp.value_load(RT[0:1, bass.ds(r + 2, 1)], min_val=0, max_val=NG - 1)
                for j in range(NM):
                    sp.wait_ge(S("moe_used"), r * NM + (NM + j - MRING + 1))
                    expert_dma(j, g)

            used = sp.value_load(RT[0:1, 14:15], min_val=4 * NM - RING, max_val=ROUNDS * NM)
            for f in range(NA, NA + NC_):
                if f - NA < RING:
                    sp.wait_ge(S("moe_used"), used + (f - NA + 1))
                else:
                    sp.wait_ge(S("res_c"), last_result[f - RING] - NRA + 1)
                sp.dma_start(slot_view(f), fills[f][0]).then_inc(S(f"arr_c{slot_of(f)}"), 16)
            for t in range(TT):
                sp.wait_ge(S("final"), t + 1)
                sp.dma_start(out[0, t * P:t * P + P, :], HN[:, t, :]).then_inc(S("stored"), 16)
            sp.wait_ge(S("stored"), 16 * TT)

        def wait_slot(pe, f):
            if f < NA:
                pe.wait_ge(S(f"arr_a{slot_of(f)}"), 16 * (f // RING + 1))
            else:
                pe.wait_ge(S(f"arr_c{slot_of(f)}"), 16 * ((f - NA) // RING + 1))

        @block.tensor
        def _(pe):
            def wait_bank(i):
                if bank_before(i) is not None:
                    e, n = emptied[bank_before(i)]
                    pe.wait_ge(S("emptied_" + e), n)

            def product(i, act, first=None, parts=(0, 1)):
                name, f, c0, feature, n = results[i]
                if first is None and 0 in parts:
                    wait_bank(i)
                if c0 == 0 and 0 in parts:
                    wait_slot(pe, f)
                w, bank = slot_view(f), bank_of(i)
                k_n = fills[f][1]
                for part in parts:
                    for k in range(k_n):
                        if feature:
                            mm = pe.matmul(bank[:, part * T:part * T + T], w[:, k, c0 + part * P:c0 + part * P + P],
                                           act[:, k, :], start=(k == 0), stop=(k == k_n - 1))
                        else:
                            mm = pe.matmul(bank[:, part * 256:part * 256 + n], act[:, k, part * P:part * P + P],
                                           w[:, k, c0:c0 + n], start=(k == 0), stop=(k == k_n - 1))
                if 1 in parts:
                    mm.then_inc(S(ready_sem(i)[0]), 1)

            def products(name, act):
                for i in of[name]:
                    product(i, act)

            def turn_rows(src, first_bank=4):
                for k in range(DK):
                    for t in range(TT):
                        mm = pe.transpose(B[first_bank + k // 2][:, (k % 2) * T + t * P:(k % 2) * T + t * P + P], src(k, t), ident)
                    if k % 2 == 1:
                        mm.then_inc(S("turned"), 1)

            def cols(tile):
                return lambda k, t: tile[:, t, k * P:k * P + P]

            pe.wait_ge(S("early_in"), EARLY)
            pe.wait_ge(S("early_in"), EARLY)
            pe.transpose(B[0][:, 0:NVEC], VROW[0:NVEC, :], ident[0:NVEC, 0:NVEC]).then_inc(S("vec_ps"), 1)
            pe.wait_ge(S("normed"), nth("x", NORMED))
            turn_rows(cols(HN))
            pe.wait_ge(S("hT_dve"), 4)
            pe.wait_ge(S("hT_act"), 4)
            products("cq", HT)
            products("ckv", HT)
            products("f", HT)
            pe.wait_ge(S("normed"), nth("lat", NORMED))
            for c in range(2):
                for t in range(TT):
                    pe.transpose(B[4][:, c * T + t * P:c * T + t * P + P], CQ[:, t, c * P:c * P + P], ident)
            for t in range(TT):
                mm = pe.transpose(B[5][:, t * P:t * P + P], CK[:, t, 0:P], ident)
            mm.then_inc(S("lat_ps"), 1)
            pe.wait_ge(S("latT"), 1)
            products("uq", CQT)
            products("ukv", CKT.unsqueeze(1))
            pe.wait_ge(S("silu_c"), 1)

            def modulation(i):
                wait_bank(i)
                wait_slot(pe, results[i][1])
                w = slot_view(results[i][1])
                for k in range(DK):
                    g = k % 4
                    mm = pe.matmul(bank_of(i)[32 * g:32 * g + 32, 0:256], CC[:, k, :], w[:, k, :],
                                   start=(k < 4), stop=(k >= 4))
                mm.then_inc(S("res_a"), 1)

            def modulation_sum(u):
                pe.wait_ge(S("emptied_act"), emptied[of["mod"][u]][1])
                row = MRW[:, u % 2, :]
                if u < 8:
                    for part in range(2):
                        mm = pe.matmul(B[7][:, 4 * u + 2 * part:4 * u + 2 * part + 2], row[:, part * P:part * P + P],
                                       const("pick2"), start=True, stop=True)
                else:
                    mm = pe.matmul(B[5 + (u - 8) // 2][:, (u % 2) * 256:(u % 2) * 256 + 256], const("row0"), row,
                                   start=True, stop=True)
                mm.then_inc(S("mod_sum"), 1)

            pending = None
            for i in range(of["q"][0], of["gate"][0]):
                if results[i][0] == "mod":
                    modulation(i)
                else:
                    product(i, HT)
                if pending is not None:
                    modulation_sum(pending)
                pending = of["mod"].index(i) if results[i][0] == "mod" else None
            modulation_sum(pending)
            pe.wait_ge(S("mod_in"), 1)
            pe.wait_ge(S("normed"), nth("qk", NORMED))
            pe.wait_ge(S("qk_pool"), 1)
            for h in range(MH):
                if h >= 4:
                    pe.wait_ge(S("qkT_even" if h % 2 == 0 else "qkT_odd"), h // 2 - 1)
                for s in range(2):
                    for t in range(TT):
                        mm = pe.transpose(B[4 + h % 4][0:QK, s * T + t * P:s * T + t * P + P],
                                          QKM[:, s, t, h * QK:h * QK + QK], ident)
                mm.then_inc(S("qkT_ps"), 1)
            pe.wait_ge(S("qkT_even"), 4)
            pe.wait_ge(S("qkT_odd"), 4)
            def mla_scores(h):
                if h >= 2:
                    pe.wait_ge(S("mla_p"), 2 * (h - 1))
                for t in range(TT):
                    mm = pe.matmul(B[4 + h % 2][:, t * T:t * T + T], QKT[0:QK, h, t * P:t * P + P],
                                   QKT[0:QK, h, T:2 * T], start=True, stop=True)
                mm.then_inc(S("mla_s"), 1)

            def mla_turn(h):
                pe.wait_ge(S("mla_p"), 2 * h + 2)
                if h >= 2:
                    pe.wait_ge(S("mla_pt"), h - 1)
                for kt in range(TT):
                    for t in range(TT):
                        mm = pe.transpose(B[6 + h % 2][:, kt * T + t * P:kt * T + t * P + P],
                                          PR[:, h % 2, t, kt * P:kt * P + P], ident)
                mm.then_inc(S("mla_pT"), 1)

            def mla_values(h):
                pe.wait_ge(S("mla_pt"), h + 1)
                if h >= 2:
                    pe.wait_ge(S("mla_o"), h - 1)
                for t in range(TT):
                    for kt in range(TT):
                        mm = pe.matmul(B[h % 2][:, t * VD:t * VD + VD], PT[:, h % 2, kt, t * P:t * P + P],
                                       KV[:, kt, h * P + NOPE:h * P + P], start=(kt == 0), stop=(kt == TT - 1))
                mm.then_inc(S("mla_pv"), 1)

            for i in range(of["gate"][0] - 4, of["gate"][0]):
                pe.wait_ge(S("emptied_" + emptied[i][0]), emptied[i][1])
            mla_scores(0)
            for h in range(MH):
                if h + 1 < MH:
                    mla_scores(h + 1)
                mla_turn(h)
                product(of["gate"][h], HT)
                mla_values(h)
            pe.wait_ge(S("normed"), nth("ctx", NORMED))
            turn_rows(cols(HN))
            pe.wait_ge(S("cT_dve"), 8)
            spare = [(i, part) for i in of["kc"] + of["vc"] for part in range(2)]

            def context_product(n=1):
                for _ in range(n):
                    i, part = spare.pop(0)
                    product(i, HT, parts=(part,))

            context_product(4)
            for n, lv in enumerate(LEVELS):
                context_product((0, 2, 2, 2, 2, 1, 1, 1)[n])
                pe.wait_ge(S("gla_qk"), n + 1)
                if n == 0:
                    pe.wait_ge(S("mla_o"), MH)
                if n >= 3:
                    pe.wait_ge(S("gla_a"), n - 2)
                for st in range(TT):
                    bank = B[GLA_BANKS[n % 3] + st]
                    for h in range(GH):
                        tt = 1 - st if lv == 128 else st
                        q = QT if lv == "diag" else DEC[:, n % 2, 0].rearrange("p (h t) -> p h t", h=GH)
                        k = DEC[:, n % 2, 1].rearrange("p (h t) -> p h t", h=GH)
                        mm = pe.matmul(bank[:, h * P:h * P + P], k[:, h, st * P:st * P + P],
                                       q[:, h, tt * P:tt * P + P], start=True, stop=True)
                mm.then_inc(S("gla_s"), 1)
            context_product()
            pe.wait_ge(S("gla_a"), len(LEVELS))
            for tt in range(TT):
                for h in range(GH):
                    for st in range(TT):
                        sc = AD[:, st, h, :] if st == tt else AXX[:, st, h, :]
                        mm = pe.matmul(B[tt][:, h * P:h * P + P], sc, V[:, st, h * P:h * P + P],
                                       start=(st == 0), stop=(st == TT - 1))
            mm.then_inc(S("gla_o_ps"), 1)
            for c in range(GH):
                for t in range(TT):
                    mm = pe.transpose(B[4 + c // 2][:, (c % 2) * T + t * P:(c % 2) * T + t * P + P],
                                      OM[:, t, c * P:c * P + P], ident)
            mm.then_inc(S("omT_ps"), 1)
            pe.wait_ge(S("omT"), 1)
            pe.wait_ge(S("gla_o"), 1)
            products("yb", OTM)
            pe.wait_ge(S("normed"), nth("o", NORMED))
            for c in range(GH):
                for t in range(TT):
                    mm = pe.transpose(B[6 + c // 2][:, (c % 2) * T + t * P:(c % 2) * T + t * P + P],
                                      OO[:, t, c, :], ident)
            mm.then_inc(S("ogT_ps"), 1)
            pe.wait_ge(S("ogT"), 1)
            products("ya", OTG)
            pe.wait_ge(S("merged"), 4)
            products("out", GATE[:, 0:8, :])

            pe.wait_ge(S("emptied_dve"), emptied[of["out"][-1]][1])
            turn_rows(lambda k, t: X[:, t, :].rearrange("p (q k) -> p k q", k=DK)[:, k, :])
            pe.wait_ge(S("rT_dve"), 4)
            pe.wait_ge(S("rT_act"), 4)
            pe.wait_ge(S("small_in"), SMALL)
            for t in range(TT):
                for k in range(DK):
                    mm = pe.matmul(B[4][:, t * 72:t * 72 + 72], HT[:, k, t * P:t * P + P], RW[:, k, :],
                                   start=(k == 0), stop=(k == DK - 1))
            mm.then_inc(S("logits_ps"), 1)
            pe.wait_ge(S("p_in"), 16)
            for c in range(2):
                for t in range(TT):
                    mm = pe.transpose(B[6][:, c * T + t * P:c * T + t * P + P], PRAW[:, t, c * P:c * P + P], ident)
            mm.then_inc(S("pT_ps"), 1)
            pe.wait_ge(S("group"), 1)
            U, ONE = const("ustrict"), const("ones")[:, 0:P]
            pe.matmul(B[5][:, 0:8], U, GOH[:, 0, :], start=True, stop=True)
            pe.matmul(B[5][:, 8:16], ONE, GOH[:, 0, :], start=True, stop=False)
            pe.matmul(B[5][:, 8:16], U, GOH[:, 1, :], start=False, stop=True)
            pe.matmul(B[5][:, 16:24], ONE, GOH[:, 0, :], start=True, stop=False)
            pe.matmul(B[5][:, 16:24], ONE, GOH[:, 1, :], start=False, stop=True).then_inc(S("rank_ps"), 1)
            pe.wait_ge(S("pT"), 1)
            products("pp", PTR)

            def slot_in(j, r):
                n = moe_slot(j)
                if isinstance(r, int):
                    if j in EXTRA:
                        pe.wait_ge(S("arr_extra"), 32 * len(EXTRA))
                    else:
                        pe.wait_ge(S(f"arr_m{n}"), slot_after[j])
                else:
                    pe.wait_ge(S(f"arr_m{n}"), r * slot_sum[n] + (slot_after[j] - missing.get(n, 0)))

            def expert_weights(j, r, k):
                return expert_slot(j, isinstance(r, int) and j in EXTRA).rearrange("p (k n) -> p k n", k=k)

            def moe_round(r, first=False):
                def at(n, k):
                    return r * n + k

                pe.wait_ge(S("sel"), at(1, 1))
                if not first:
                    pe.wait_ge(S("moe_x"), r)
                for k in range(DK):
                    for t in range(TT):
                        mm = pe.matmul(B[0][:, k * SLOT:k * SLOT + SLOT], HN[:, t, k * P:k * P + P], SEL[:, t, 0:SLOT],
                                       start=(t == 0), stop=(t == TT - 1))
                mm.then_inc(S("gath_ps"), 1)
                for t in range(TT):
                    mm = pe.matmul(B[1][:, 0:EPG], SEL[:, t, :], WT[:, t, :], start=(t == 0), stop=(t == TT - 1))
                for t in range(TT):
                    mm = pe.transpose(B[2][:, t * P:t * P + P], SEL[:, t, :], ident)
                mm.then_inc(S("sel_ps"), 1)
                pe.wait_ge(S("gath"), at(1, 1))

                def up(p):
                    bank = B[3 + p % 2]
                    if p >= 2:
                        pe.wait_ge(S("hid"), at(PAIRS, p - 1))
                    for half in range(2):
                        js = [moe_index[("up", 2 * p + e, half)] for e in range(2)]
                        for j in js:
                            slot_in(j, r)
                        for k in range(DK // 2):
                            kk = half * DK // 2 + k
                            for e in range(2):
                                w = expert_weights(js[e], r, DK // 2)
                                mm = pe.matmul(bank[e * SLOT:e * SLOT + SLOT, :], XG[:, kk, :], w[:, k, :],
                                               start=(kk == 0), stop=(kk == DK - 1))
                                if k == DK // 2 - 1:
                                    mm.then_inc(S("moe_used"), 1)

                def turn_hidden(p):
                    pe.wait_ge(S("hid"), at(PAIRS, p + 1))
                    for c in range(2):
                        mm = pe.transpose(B[6 + p % 2][:, c * P:c * P + P], HHR[:, p % 2, c * P:c * P + P], ident)
                    mm.then_inc(S("hht_ps"), 1)

                def down(p):
                    pe.wait_ge(S("hht"), at(PAIRS, p + 1))
                    for e in range(2):
                        j = moe_index[("down", 2 * p + e, 0)]
                        slot_in(j, r)
                        w = expert_weights(j, r, 2)
                        for c in range(2):
                            for half in range(2):
                                mm = pe.matmul(B[5][half * SLOT:half * SLOT + SLOT, :],
                                               HHT[:, p % 2, c, e * SLOT:e * SLOT + SLOT], w[:, c, half * 512:half * 512 + 512],
                                               start=(p == 0 and e == 0 and c == 0),
                                               stop=(p == PAIRS - 1 and e == 1 and c == 1))
                        mm.then_inc(S("moe_used"), 1)

                up(0)
                for p in range(PAIRS):
                    if p + 1 < PAIRS:
                        up(p + 1)
                    turn_hidden(p)
                    down(p)
                pe.wait_ge(S("yy"), at(1, 1))
                for t in range(TT):
                    for half in range(2):
                        rows = slice(half * SLOT, half * SLOT + SLOT)
                        mm = pe.matmul(B[2 * t + half][:, :], STR[rows, t * P:t * P + P], YY[rows, :], start=True, stop=True)
                mm.then_inc(S("scat_ps"), 1)

            for i in range(NRA - 4, NRA):
                pe.wait_ge(S("emptied_" + emptied[i][0]), emptied[i][1])
            pe.wait_ge(S("normed"), nth("hm", NORMED))
            moe_round(0, first=True)
            pe.wait_ge(S("table"), 1)
            rounds = pe.value_load(RT[0:1, 0:1], min_val=4, max_val=ROUNDS)
            with pe.Fori(1, rounds) as r:
                moe_round(r)

            pe.wait_ge(S("moe_x"), rounds + 0)
            turn_rows(cols(X))
            pe.wait_ge(S("pleT_dve"), 4)
            pe.wait_ge(S("pleT_act"), 4)
            for i in of["ple"]:
                product(i, HT, first=True)

            pe.wait_ge(S("normed"), nth("two", NORMED))
            turn_rows(cols(HN))
            pe.wait_ge(S("twoT"), 8)
            for name in ("zb", "ga", "gb", "za", "b", "c", "xin"):
                products(name, HT)
            def rotate(m):
                i = (of["q2"] + of["k2"])[m]
                pe.wait_ge(S("emptied_act"), emptied[i][1])
                if m >= 2:
                    pe.wait_ge(S("roped"), m - 1)
                pe.matmul(B[4 + m % 2][:, :], const("rot"), RAW[:, m % 2, :], start=True, stop=True)\
                  .then_inc(S("rot_ps"), 1)

            for m, i in enumerate(of["q2"] + of["k2"]):
                product(i, HT)
                if m:
                    rotate(m - 1)
            product(of["v2"][0], HT)
            rotate(7)
            for i in of["v2"][1:]:
                product(i, HT)
            pe.wait_ge(S("roped"), 8)
            for i in of["v2"]:
                pe.wait_ge(S("emptied_" + emptied[i][0]), emptied[i][1])

            products("yconv", YA)
            for i in of["yconv"]:
                pe.wait_ge(S("emptied_" + emptied[i][0]), emptied[i][1])

            def scores2(n):
                h, t = divmod(n, TT)
                c, p0 = h // 2, (h % 2) * HD
                if n >= 3:
                    pe.wait_ge(S("na_p"), n - 2)
                bank = B[2 + n % 3]
                pe.matmul(bank[:, 0:T], QT2[p0:p0 + HD, c, t * P:t * P + P], KT2[p0:p0 + HD, c, :], start=True, stop=False)
                pe.wait_ge(S("bm"), n + 1)
                pe.matmul(bank[:, 0:T], const("flip"), BM[:, n % 3, :], start=False, stop=True)
                pe.matmul(bank[:, T:2 * T], QT2[p0:p0 + HD, c, t * P:t * P + P], KC[p0:p0 + HD, c, :],
                          start=True, stop=True).then_inc(S("na_s"), 1)

            def values2(c):
                pe.wait_ge(S("na_pt"), 4 * c + 4)
                if c >= 2:
                    pe.wait_ge(S("na_o"), c - 1)
                for kt in range(4):
                    v = V2 if kt < 2 else VC
                    for e in range(2):
                        h = 2 * c + e
                        mm = pe.matmul(B[c % 2][e * HD:e * HD + HD, 0:T], v[:, kt % 2, h * HD:h * HD + HD],
                                       PT2[c % 2][:, e, kt, :], start=(kt == 0), stop=(kt == 3))
                mm.then_inc(S("na_pv"), 1)

            N2 = H2 * TT
            scores2(0)
            scores2(1)
            for n in range(N2):
                if n + 2 < N2:
                    scores2(n + 2)
                if n % 4 == 1 and n > 4:
                    values2(n // 4 - 1)
                pe.wait_ge(S("na_pn"), n + 1)
                if n >= 2:
                    pe.wait_ge(S("na_pt"), n - 1)
                for kt in range(4):
                    mm = pe.transpose(B[5 + n % 2][:, kt * P:kt * P + P], PR2[:, n % 3, kt * P:kt * P + P], ident)
                mm.then_inc(S("na_pT"), 1)
            values2(H2 // 2 - 1)
            pe.wait_ge(S("na_o"), H2 // 2)
            products("yattn", HT)
            pe.wait_ge(S("merged2"), 4)
            products("wo", GA)

        @block.scalar
        def _(act):
            def sumsq(src, tag):
                for t in range(TT):
                    ins = nc.scalar.activation(HN[:, t, :], src[:, t, :], ACT.Square, accum_out=ss[tag][:, t:t + 1])
                ins.then_inc(S("sumsq"), 1)

            def turned(tag, done, gain):
                for k in range(4, 8):
                    if k % 2 == 0:
                        act.wait_ge(S("turned"), 4 * nth(tag, TURNS) - 3 + k // 2)
                    nc.scalar.activation(HT[:, k, :], B[4 + k // 2][:, (k % 2) * T:(k % 2) * T + T], ACT.Copy,
                                         scale=gain(k)).then_inc(S(done), 1)

            act.wait_ge(S("x_in"), 16)
            sumsq(X, "x")
            act.dma_start(QKN[:, 0, :], a["q_norm"][0].partition_broadcast(P)).then_inc(S("small_in"), 16)
            act.dma_start(QKN[:, 1, :], a["k_norm"][0].partition_broadcast(P)).then_inc(S("small_in"), 16)
            act.dma_start(ONB[:], a["hg_onorm"][0].partition_broadcast(P)).then_inc(S("small_in"), 16)
            act.dma_start(POSI[:], a["positions"].rearrange("o (t p) -> p (o t)", p=P),
                          allow_slow_non_contiguous=True).then_inc(S("small_in"), 16)
            act.dma_start(MSF, a["masks"].rearrange("p a b -> p (a b)"))\
               .then_inc(S("masks_in"), 16)
            act.dma_start(RB[:, 0:8], a["b_rg"][0].partition_broadcast(P)).then_inc(S("small_in"), 16)
            act.dma_start(RB[:, 8:72], a["b_re"][0].partition_broadcast(P)).then_inc(S("small_in"), 16)
            act.dma_start(RW[:, :, 0:8], a["w_rg"][0].rearrange("(p k) n -> p k n", p=P)).then_inc(S("small_in"), 16)
            act.dma_start(RW[:, :, 8:72], a["w_re"][0].rearrange("(p k) n -> p k n", p=P)).then_inc(S("small_in"), 16)
            act.dma_start(LNM[:], a["ln_moe"][0].rearrange("(p k) -> p k", p=P)).then_inc(S("small_in"), 16)
            act.dma_start(PG[:], a["post_g_2"][0].partition_broadcast(P)).then_inc(S("small_in"), 16)
            act.dma_start(BGT[:], a["b_mod_2"][0, 2048:3072].partition_broadcast(P)).then_inc(S("small_in"), 16)
            act.wait_ge(S("vec"), 1)
            turned("x", "hT_act", lambda k: vec("ln_mix", k))
            act.dma_start(HN[:], a["ctx_2"][0].rearrange("(t p) d -> p t d", p=P)).then_inc(S("ctx_in"), 16)
            act.wait_ge(S("cc"), 1)
            nc.scalar.activation(CSG, CC[:, :, 0:2], ACT.Sigmoid).then_inc(S("sig_c"), 1)
            act.wait_ge(S("emptied_dve"), emptied[of["ckv"][0]][1])
            for t in range(TT):
                nc.scalar.activation(CQT[:, t, :], CQ[:, t, :], ACT.Square, accum_out=SSL[:, t:t + 1])
            for t in range(TT):
                ins = nc.scalar.activation(CKT[:, t * P:t * P + P], CK[:, t, 0:P], ACT.Square, accum_out=SSL[:, 2 + t:3 + t])
            ins.then_inc(S("sumsq"), 1)
            act.wait_ge(S("lbd"), 2)
            nc.scalar.activation(LBF, LBF, ACT.Sigmoid)
            nc.scalar.activation(LBR, LBR, ACT.Sigmoid).then_inc(S("lb"), 1)
            act.wait_ge(S("ang"), 1)
            nc.scalar.activation(SN, RED, ACT.Sin)
            nc.scalar.activation(CS, KQ, ACT.Sin).then_inc(S("sincos"), 1)
            for n, i in enumerate(of["f"]):
                wait_result(act, i)
                nc.scalar.activation(SF[:, 2 * n:2 * n + 2, :].rearrange("p a t -> p (a t)"), bank_of(i)[:, :],
                                     ACT.Sigmoid).then_inc(S("emptied_act"), 1)
            act.wait_ge(S("ctx_in"), 16)
            for t in range(TT):
                ins = nc.scalar.activation(CSQ[:, t, :], HN[:, t, :], ACT.Square, accum_out=ss["ctx"][:, t:t + 1])
            ins.then_inc(S("sumsq"), 1)
            for n, i in enumerate(of["ukv"]):
                wait_result(act, i)
                nc.scalar.activation(KV[:, :, 256 * n:256 * n + 256], bank_of(i)[:, :].rearrange("p (t c) -> p t c", t=TT),
                                     ACT.Copy).then_inc(S("emptied_act"), 1)
            for i in range(of["q"][0], of["gate"][0]):
                wait_result(act, i)
                name = results[i][0]
                n = of[name].index(i)
                if name == "q":
                    nc.scalar.activation(QT[:, 2 * n:2 * n + 2, :].rearrange("p a t -> p (a t)"), bank_of(i)[:, :],
                                         ACT.Sigmoid).then_inc(S("sig"), 1)
                elif name == "v":
                    nc.scalar.activation(V[:, :, 256 * n:256 * n + 256], bank_of(i)[:, :].rearrange("p (t c) -> p t c", t=TT),
                                         ACT.Copy).then_inc(S("emptied_act"), 1)
                elif name == "og":
                    nc.scalar.activation(OG[:, :, 256 * n:256 * n + 256], bank_of(i)[:, :].rearrange("p (t c) -> p t c", t=TT),
                                         ACT.Sigmoid).then_inc(S("sig"), 1)
                else:
                    if n >= 2:
                        act.wait_ge(S("mod_sum"), n - 1)
                    nc.scalar.activation(MRW[:, n % 2, :], bank_of(i)[:, 0:256], ACT.Copy).then_inc(S("emptied_act"), 1)
                if i == of["mod"][3]:
                    act.wait_ge(S("sumsq"), nth("ctx"))
                    act.wait_ge(S("emptied_dve"), emptied[of["uq"][-1]][1])
                    nc.scalar.activation(SQ[:, 0], QKM[:, 0].rearrange("p t (h d) -> p (t h) d", h=MH), ACT.Square)
                    act.wait_ge(S("km"), 1)
                    nc.scalar.activation(SQ[:, 1], QKM[:, 1].rearrange("p t (h d) -> p (t h) d", h=MH), ACT.Square)\
                      .then_inc(S("sumsq"), 1)
            act.wait_ge(S("fgate"), 1)
            nc.scalar.activation(SF[:, :, :], SF[:, :, :], ACT.Ln).then_inc(S("logf"), 1)
            for h in range(0, MH, 2):
                act.wait_ge(S("qkT_ps"), h + 1)
                nc.scalar.activation(QKT[0:QK, h, :], B[4 + h % 4][0:QK, :], ACT.Copy).then_inc(S("qkT_even"), 1)
            scale = QK ** -0.5

            def context_keys(n):
                i = of["kc"][n]
                wait_result(act, i)
                nc.scalar.activation(HN[:, n // 2, (n % 2) * 512:(n % 2) * 512 + 512], bank_of(i)[:, :], ACT.Copy)\
                  .then_inc(S("emptied_act"), 1)

            def context_values(n):
                i = of["vc"][n]
                wait_result(act, i)
                nc.scalar.activation(VC[:, :, 256 * n:256 * n + 256], bank_of(i)[:, :].rearrange("p (t c) -> p t c", t=TT),
                                     ACT.Copy).then_inc(S("emptied_act"), 1)

            def mla_exp(h):
                act.wait_ge(S("mla_nmax"), h + 1)
                if h >= 2:
                    act.wait_ge(S("mla_pT"), h - 1)
                for t in range(TT):
                    nc.scalar.activation(PR[:, h % 2, t, :], B[4 + h % 2][:, t * T:t * T + T], ACT.Exp, scale=scale,
                                         bias=NMX[:, h % 2, t:t + 1], accum_out=SUM[:, h % 2, t:t + 1])\
                      .then_inc(S("mla_p"), 1)

            act.wait_ge(S("masks"), 1)
            mla_exp(0)
            for h in range(MH):
                act.wait_ge(S("mla_pT"), h + 1)
                if h >= 2:
                    act.wait_ge(S("mla_pv"), h - 1)
                nc.scalar.activation(PT[:, h % 2, :, :].rearrange("p a t -> p (a t)"), B[6 + h % 2][:, :], ACT.Copy)\
                  .then_inc(S("mla_pt"), 1)
                if h + 1 < MH:
                    mla_exp(h + 1)
                i = of["gate"][h]
                wait_result(act, i)
                nc.scalar.activation(GATE[:, 2 * h:2 * h + 2, :].rearrange("p a t -> p (a t)"), bank_of(i)[:, :],
                                     ACT.Sigmoid).then_inc(S("emptied_act"), 1)
            for n, lv in enumerate(LEVELS[:-1]):
                act.wait_ge(S("gla_dec"), n + 1)
                nc.scalar.activation(DEC[:, n % 2, :, :], DEC[:, n % 2, :, :], ACT.Exp).then_inc(S("gla_exp"), 1)
                if n < 4:
                    context_keys(n)
                else:
                    context_values(n - 4)
            act.wait_ge(S("cum"), 1)
            act.wait_ge(S("emptied_act"), emptied[of["kc"][-1]][1])
            act.dma_start(KC.rearrange("p a t -> p (a t)"), HN[:].rearrange("p a t -> p (a t)")).then_inc(S("kc_in"), 16)
            context_values(3)
            act.wait_ge(S("omT_ps"), 1)
            for c in range(2):
                ins = nc.scalar.activation(OTM[:, 2 * c:2 * c + 2, :].rearrange("p a t -> p (a t)"), B[4 + c][:, :], ACT.Copy)
            ins.then_inc(S("omT"), 1)
            act.wait_ge(S("gla_o"), 1)
            nc.scalar.activation(OSQ, OO.rearrange("p t h v -> p (t h) v"), ACT.Square).then_inc(S("sumsq"), 1)
            act.wait_ge(S("ogT_ps"), 1)
            for c in range(2):
                ins = nc.scalar.activation(OTG[:, 2 * c:2 * c + 2, :].rearrange("p a t -> p (a t)"), B[6 + c][:, :], ACT.Copy)
            ins.then_inc(S("ogT"), 1)

            act.wait_ge(S("normed"), nth("o", NORMED))
            act.dma_start(PRAW[:], a["p"][0, 0].rearrange("(t p) d -> p t d", p=P)).then_inc(S("p_in"), 16)
            act.wait_ge(S("kc_in"), 16)
            act.wait_ge(S("emptied_dve"), emptied[of["out"][-1]][1])
            sumsq(X, "hm")
            act.wait_ge(S("small_in"), SMALL)
            turned("hm", "rT_act", lambda k: LNM[:, k:k + 1])
            act.wait_ge(S("pT_ps"), 1)
            nc.scalar.activation(PTR.rearrange("p a t -> p (a t)"), B[6][:, :], ACT.Copy).then_inc(S("pT"), 1)

            def embedding(n):
                i = of["pp"][n]
                wait_result(act, i)
                nc.scalar.activation(PP[:, :, 256 * n:256 * n + 256], bank_of(i)[:, :].rearrange("p (t c) -> p t c", t=TT),
                                     ACT.Copy).then_inc(S("emptied_act"), 1)

            act.wait_ge(S("gdiff"), 1)
            nc.scalar.activation(GEXP, GEXP, ACT.Exp).then_inc(S("gexp"), 1)
            embedding(0)
            act.wait_ge(S("ediff"), 1)
            nc.scalar.activation(E2W, DLT, ACT.Exp).then_inc(S("eexp"), 1)
            for n in range(1, 4):
                embedding(n)

            def moe_round(r):
                def at(n, k):
                    return r * n + k

                act.wait_ge(S("sel_ps"), at(1, 1))
                nc.scalar.activation(STR, B[2][:, 0:T], ACT.Copy).then_inc(S("str"), 1)

                def sigmoid(p):
                    act.wait_ge(S("moe_used"), at(NM, moe_index[("up", 2 * p + 1, 1)] + 1))
                    nc.scalar.activation(SGM[:, p % 2], B[3 + p % 2][:, 0:FE], ACT.Sigmoid).then_inc(S("moe_sig"), 1)

                sigmoid(0)
                for p in range(PAIRS):
                    if p + 1 < PAIRS:
                        sigmoid(p + 1)
                    act.wait_ge(S("hht_ps"), at(PAIRS, p + 1))
                    nc.scalar.activation(HHT[:, p % 2].rearrange("p c s -> p (c s)"), B[6 + p % 2][:, 0:2 * P], ACT.Copy)\
                      .then_inc(S("hht"), 1)
                act.wait_ge(S("moe_used"), at(NM, NM))
                nc.scalar.activation(YY, B[5][:, :], ACT.Copy).then_inc(S("yy"), 1)

            moe_round(0)
            act.wait_ge(S("table"), 1)
            rounds = act.value_load(RT[0:1, 0:1], min_val=4, max_val=ROUNDS)
            with act.Fori(1, rounds) as r:
                moe_round(r)

            act.wait_ge(S("moe_x"), rounds + 0)
            sumsq(X, "ple")
            turned("ple", "pleT_act", lambda k: vec("ln_ple", k))

            def square_two(n):
                act.wait_ge(S("ple_x"), n + 1)
                for t in range(TT):
                    ins = nc.scalar.activation(HN[:, t, 256 * n:256 * n + 256], X[:, t, 256 * n:256 * n + 256], ACT.Square,
                                               accum_out=SS2[:, t, n:n + 1])
                return ins

            act.wait_ge(S("sumsq"), nth("ple"))
            for n, i in enumerate(of["ple"]):
                wait_result(act, i)
                if n >= 2:
                    act.wait_ge(S("ple_x"), n - 1)
                if n == 0:
                    act.wait_ge(S("rms"), nth("ple"))
                for t in range(TT):
                    ins = nc.scalar.activation(SG[:, n % 2, t, :], bank_of(i)[:, t * 256:t * 256 + 256], ACT.Sigmoid,
                                               scale=rs["ple"][:, t:t + 1])
                ins.then_inc(S("emptied_act"), 1)
                if n >= 1:
                    square_two(n - 1)
            square_two(3).then_inc(S("sumsq"), 1)
            for n, i in enumerate(of["zb"]):
                wait_result(act, i)
                nc.scalar.activation(ZB[:, 2 * n:2 * n + 2, :].rearrange("p a t -> p (a t)"), bank_of(i)[:, :],
                                     ACT.Sigmoid).then_inc(S("sig2"), 1)
            for name, dst in (("ga", GA), ("gb", GB)):
                for n, i in enumerate(of[name]):
                    wait_result(act, i)
                    nc.scalar.activation(dst[:, 2 * n:2 * n + 2, :].rearrange("p a t -> p (a t)"), bank_of(i)[:, :],
                                         ACT.Sigmoid).then_inc(S("emptied_act"), 1)
            for n, i in enumerate(of["za"]):
                wait_result(act, i)
                nc.scalar.activation(YA[:, 2 * n:2 * n + 2, :].rearrange("p a t -> p (a t)"), bank_of(i)[:, :],
                                     ACT.Sigmoid).then_inc(S("sig2"), 1)
            for n, i in enumerate(of["c"]):
                wait_result(act, i)
                nc.scalar.activation(UC[:, 2 * n:2 * n + 2, 1:T + 1], bank_of(i)[:, :].rearrange("p (a t) -> p a t", a=2),
                                     ACT.Copy).then_inc(S("emptied_act"), 1)
            for m, i in enumerate(of["q2"] + of["k2"]):
                wait_result(act, i)
                if m >= 2:
                    act.wait_ge(S("roped"), m - 1)
                nc.scalar.activation(RAW[:, m % 2, :], bank_of(i)[:, :], ACT.Copy).then_inc(S("emptied_act"), 1)
            act.wait_ge(S("conv"), 8)
            for n, i in enumerate(of["v2"]):
                wait_result(act, i)
                nc.scalar.activation(V2[:, :, 256 * n:256 * n + 256], bank_of(i)[:, :].rearrange("p (t c) -> p t c", t=TT),
                                     ACT.Copy).then_inc(S("emptied_act"), 1)
            act.wait_ge(S("roped"), 8)

            def exp2(n):
                act.wait_ge(S("na_nmax"), n + 1)
                if n >= 3:
                    act.wait_ge(S("na_pT"), n - 2)
                nc.scalar.activation(PR2[:, n % 3, :], B[2 + n % 3][:, :], ACT.Exp, bias=NMX2[:, n % 2:n % 2 + 1],
                                     accum_out=SUM2[:, n % 2:n % 2 + 1]).then_inc(S("na_p"), 1)

            exp2(0)
            for n in range(H2 * TT):
                h, t = divmod(n, TT)
                if n + 1 < H2 * TT:
                    exp2(n + 1)
                act.wait_ge(S("na_pT"), n + 1)
                if n >= 8 and n % 4 == 0:
                    act.wait_ge(S("na_pv"), n // 4 - 1)
                nc.scalar.activation(PT2[(h // 2) % 2][:, h % 2, :, t * P:t * P + P],
                                     B[5 + n % 2][:, :].rearrange("p (k q) -> p k q", k=4), ACT.Copy).then_inc(S("na_pt"), 1)
            for n, i in enumerate(of["wo"]):
                act.wait_ge(S("emptied_dve"), emptied[i][1])
                for t in range(TT):
                    ins = nc.scalar.activation(HN[:, t, 256 * n:256 * n + 256], bank_of(i)[:, t * 256:t * 256 + 256], ACT.Square,
                                               accum_out=SSY[:, t, n:n + 1])
            ins.then_inc(S("sumsq"), 1)

        M_TMP_K = area(M0, 4, TT, MH * 16)
        M_TMP_Q = area(M0 + 6720, 4, TT, MH * 16)

        def norm_rope(ve, link, s, tmp):
            x = QKM[:, s].rearrange("p t (h d) -> p (t h) d", h=MH)
            link(ve.tensor_tensor(x, x, over(RSH[:, 16 * s:16 * s + 16].unsqueeze(2), 16, QK), ALU.mult))
            link(ve.tensor_tensor(x, x, over(QKN[:, s:s + 1, :], 16, QK), ALU.mult))
            xr = QKM[:, s].rearrange("p t (h d) -> p t h d", h=MH)
            x1, x2 = xr[:, :, :, NOPE:NOPE + 16], xr[:, :, :, NOPE + 16:QK]
            tm = [tmp[:, j].rearrange("p t (h d) -> p t h d", h=MH) for j in range(4)]
            cs = over(CS.unsqueeze(2), TT, MH, 16)
            sn = over(SN.unsqueeze(2), TT, MH, 16)
            ve.tensor_tensor(tm[0], x1, cs, ALU.mult)
            ve.tensor_tensor(tm[1], x2, sn, ALU.mult)
            ve.tensor_tensor(tm[2], x2, cs, ALU.mult)
            link(ve.tensor_tensor(tm[3], x1, sn, ALU.mult))
            ve.tensor_tensor(x1, tm[0], tm[1], ALU.subtract)
            return ve.tensor_tensor(x2, tm[2], tm[3], ALU.add)

        @block.gpsimd
        def _(pool):
            def power(dst, src, n, tag):
                pool.wait_ge(S("mean_sq"), nth(tag))
                nc.gpsimd.tensor_tensor(dst, src, NHALF[:, 0:n], ALU.pow).then_inc(S("rms"), 1)

            nc.gpsimd.memset(NHALF, -0.5).then_inc(S("nhalf"), 1)
            pool.wait_ge(S("nhalf"), 1)
            power(rs["x"], ss["x"], 2, "x")
            power(RSL, SSL, 4, "lat")
            power(rs["ctx"], ss["ctx"], 2, "ctx")
            for t in range(TT):
                dst = QKM[:, 1, t].rearrange("p (h d) -> p h d", h=MH)
                if t == 0:
                    pool.wait_ge(S("emptied_act"), emptied[of["ukv"][-1]][1])
                    pool.wait_ge(S("emptied_dve"), emptied[of["ckv"][0]][1])
                nc.gpsimd.tensor_copy(dst[:, :, 0:NOPE], KV[:, t].rearrange("p (h d) -> p h d", h=MH)[:, :, 0:NOPE])
                ins = nc.gpsimd.tensor_copy(dst[:, :, NOPE:QK], over(CK[:, t, P:160].unsqueeze(1), MH, ROPE))
            ins.then_inc(S("km"), 1)
            power(RSH, SSH, 32, "qk")

            def chain(ins, name, n=[0]):
                n[0] += 1
                ins.then_inc(S(name), 1)
                pool.wait_ge(S(name), n[0])

            pool.wait_ge(S("km"), 1)
            pool.wait_ge(S("sumsq"), nth("qk"))
            pool.wait_ge(S("rms"), nth("qk"))
            pool.wait_ge(S("small_in"), SMALL)
            pool.wait_ge(S("sincos"), 1)
            norm_rope(nc.gpsimd, lambda ins: chain(ins, "pool_chain"), 1, M_TMP_K).then_inc(S("qk_pool"), 1)

            pool.wait_ge(S("mla_pv"), MH)
            pool.wait_ge(S("mla_o"), MH)
            pool.wait_ge(S("cum"), 1)
            for n, lv in enumerate(LEVELS[:-1]):
                if n >= 2:
                    pool.wait_ge(S("gla_s"), n - 1)
                dq, dk = DEC[:, n % 2, 0], DEC[:, n % 2, 1]
                fc = FC.rearrange("p h t -> p (h t)")
                bx = BX.rearrange("p h t -> p (h t)")
                if isinstance(lv, int):
                    m = lv

                    def halves(v):
                        v = v.rearrange("p (b two m) -> p b two m", two=2, m=m)
                        return v[:, :, 0, :], v[:, :, 1, :]

                    blocks = GH * T // (2 * m)
                    fl, fr = halves(fc)
                    bl, br = halves(bx)
                    qs = halves(dq)
                    ks = halves(dk)
                    f_edge = over(fl[:, :, m - 1:m], blocks, m)
                    b_edge = over(br[:, :, 0:1], blocks, m)
                    nc.gpsimd.tensor_tensor(qs[0], b_edge, bl, ALU.subtract)
                    nc.gpsimd.tensor_tensor(qs[1], fr, f_edge, ALU.subtract)
                    nc.gpsimd.tensor_tensor(ks[0], f_edge, fl, ALU.subtract)
                    nc.gpsimd.tensor_tensor(ks[1], br, b_edge, ALU.subtract).then_inc(S("gla_dec"), 1)
                else:
                    def blk(v):
                        return v.rearrange("p (b m) -> p b m", m=8)

                    if lv == "base_fwd":
                        ref = over(blk(fc)[:, :, 3:4], GH * T // 8, 8)
                        nc.gpsimd.tensor_tensor(blk(dq), blk(fc), ref, ALU.subtract)
                        nc.gpsimd.tensor_tensor(blk(dk), ref, blk(fc), ALU.subtract).then_inc(S("gla_dec"), 1)
                    else:
                        ref = over(blk(bx)[:, :, 4:5], GH * T // 8, 8)
                        nc.gpsimd.tensor_tensor(blk(dq), ref, blk(bx), ALU.subtract)
                        nc.gpsimd.tensor_tensor(blk(dk), blk(bx), ref, ALU.subtract).then_inc(S("gla_dec"), 1)
            power(RSO, SSO, 8, "o")
            power(rs["hm"], ss["hm"], 2, "hm")
            pool.wait_ge(S("rms"), nth("hm"))
            for t in range(TT):
                ins = nc.gpsimd.tensor_tensor(HN[:, t, :].rearrange("p (k q) -> p k q", k=DK),
                                              X[:, t, :].rearrange("p (q k) -> p k q", k=DK),
                                              over(rs["hm"][:, t:t + 1].unsqueeze(2), DK, P), ALU.mult)
            ins.then_inc(S("normed"), 1)
            power(rs["ple"], ss["ple"], 2, "ple")
            power(rs["two"], ss["two"], 2, "two")
            pool.wait_ge(S("conv"), 8)

            def bias_dma(h):
                for t in range(TT):
                    src = bass.AP(a["toeplitz"].tensor, (h * ROWS + 2 * t) * TOEP, [[TOEP, 2], [ROWS, GW], [1, T]])
                    pool.dma_start(BT[:, h % 2, t, :], src).then_inc(S(f"bt{h % 2}"), 16)

            bias_dma(0)
            for h in range(H2):
                if h + 1 < H2:
                    bias_dma(h + 1)
                pool.wait_ge(S(f"bt{h % 2}"), 32 * (h // 2 + 1))
                for t in range(TT):
                    n = h * TT + t
                    if n >= 3:
                        pool.wait_ge(S("na_s"), n - 2)
                    nc.gpsimd.tensor_tensor(BM[:, n % 3, :].rearrange("p (r c) -> p c r", r=ROWS),
                                            BT[:, h % 2, t, :].rearrange("p (c r) -> p c r", r=ROWS),
                                            const("winmask").rearrange("p (c r) -> p c r", r=ROWS), ALU.add)\
                      .then_inc(S("bm"), 1)
                    pool.wait_ge(S("bm"), n + 1)
            power(rs["y"], ss["y"], 2, "y")

        @block.vector
        def _(dve):
            V_ = nc.vector
            links = [0]

            def link(ins):
                links[0] += 1
                ins.then_inc(S("dve_chain"), 1)
                dve.wait_ge(S("dve_chain"), links[0])

            def mean_sq(tag, n):
                v = ss[tag]
                dve.wait_ge(S("sumsq"), nth(tag))
                V_.tensor_scalar(v, v, 1.0 / n, EPS, ALU.mult, ALU.add).then_inc(S("mean_sq"), 1)

            def normalize(src, tag, dst=None):
                mean_sq(tag, D)
                dve.wait_ge(S("rms"), nth(tag))
                for t in range(TT):
                    o = HN[:, t, :] if dst is None else dst(t)
                    i_ = src[:, t, :] if dst is None else src[:, t, :].rearrange("p (q k) -> p k q", k=DK)
                    ins = V_.tensor_scalar(o, i_, rs[tag][:, t:t + 1], None, ALU.mult)
                ins.then_inc(S("normed"), 1)

            def turned(tag, done, gain, ks=range(4), bias=None, first_bank=4):
                for k in ks:
                    if k % 2 == 0:
                        dve.wait_ge(S("turned"), 4 * nth(tag, TURNS) - 3 + k // 2)
                    src = B[first_bank + k // 2][:, (k % 2) * T:(k % 2) * T + T]
                    if bias is None:
                        V_.tensor_scalar(HT[:, k, :], src, gain(k), None, ALU.mult).then_inc(S(done), 1)
                    else:
                        V_.tensor_scalar(HT[:, k, :], src, gain(k), bias(k), ALU.mult, ALU.add).then_inc(S(done), 1)

            def tiles(i):
                return bank_of(i)[:, :].rearrange("p (t c) -> p t c", t=TT)

            normalize(X, "x")
            dve.wait_ge(S("vec_ps"), 1)
            V_.tensor_copy(VEC[:], B[0][:, 0:NVEC]).then_inc(S("vec"), 1)
            dve.wait_ge(S("vec"), 1)
            at = VEC_ROWS["hg_lb"][0]
            lbv = VEC[:, at:at + 16].rearrange("p (d j r) -> p d j r", d=2, j=2)
            l0, l1 = lbv[:, :, 0, :], lbv[:, :, 1, :]
            V_.tensor_tensor(LBF.rearrange("p (d r) -> p d r", d=2), l0, l1, ALU.subtract).then_inc(S("lbd"), 1)
            V_.tensor_tensor(LBR.rearrange("p (d r) -> p d r", d=2), l1, l0, ALU.subtract).then_inc(S("lbd"), 1)
            link(V_.memset(CC, 0.0))
            V_.tensor_copy(CC[:, :, 0], vec("c_2", 0, 8))
            V_.tensor_copy(CC[:, :, 1], vec("c_ctx_2", 0, 8)).then_inc(S("cc"), 1)
            turned("x", "hT_dve", lambda k: vec("ln_mix", k))
            dve.wait_ge(S("masks_in"), 16)
            V_.tensor_copy(MSK[:].rearrange("p a b -> p (a b)"), MSF).then_inc(S("masks"), 1)
            dve.wait_ge(S("small_in"), SMALL)
            dve.wait_ge(S("small_in"), SMALL)
            link(V_.tensor_copy(POSF, POSI[:]))
            for t in range(TT):
                ins = V_.tensor_scalar(ANG[:, t, :], const("invfreq"), POSF[:, t:t + 1], None, ALU.mult)
            link(ins)
            magic = 1.5 * 2 ** 23
            link(V_.tensor_scalar(KQ, ANG, 1.0 / (2 * np.pi), magic, ALU.mult, ALU.add))
            link(V_.tensor_scalar(KQ, KQ, magic, None, ALU.subtract))
            c1 = 6.28125
            c2 = float(np.float32(2 * np.pi - c1))
            c3 = float(2 * np.pi - c1 - np.float64(np.float32(c2)))
            link(V_.scalar_tensor_tensor(out=RED, in0=KQ, scalar=-c1, in1=ANG, op0=ALU.mult, op1=ALU.add))
            link(V_.scalar_tensor_tensor(out=RED, in0=KQ, scalar=-c2, in1=RED, op0=ALU.mult, op1=ALU.add))
            link(V_.scalar_tensor_tensor(out=RED, in0=KQ, scalar=-c3, in1=RED, op0=ALU.mult, op1=ALU.add))
            link(V_.tensor_scalar(RED, RED, float(np.float32(3.1415925)), -float(np.float32(3.1415925)), ALU.min, ALU.max))
            link(V_.tensor_scalar(KQ, RED, -1.0, None, ALU.mult))
            link(V_.tensor_tensor(KQ, KQ, RED, ALU.max))
            V_.tensor_scalar(KQ, KQ, -1.0, float(np.pi / 2), ALU.mult, ALU.add).then_inc(S("ang"), 1)

            i = of["cq"][0]
            wait_result(dve, i)
            V_.tensor_copy(CQ[:, :, :], tiles(i)).then_inc(S("emptied_dve"), 1)
            i = of["ckv"][0]
            wait_result(dve, i)
            V_.tensor_copy(CK[:, :, :], tiles(i)[:, :, 0:160]).then_inc(S("emptied_dve"), 1)

            dve.wait_ge(S("sumsq"), nth("lat"))
            V_.tensor_scalar(SSL[:, 0:2], SSL[:, 0:2], 1.0 / QR, EPS, ALU.mult, ALU.add)
            V_.tensor_scalar(SSL[:, 2:4], SSL[:, 2:4], 1.0 / KVR, EPS, ALU.mult, ALU.add).then_inc(S("mean_sq"), 1)
            dve.wait_ge(S("rms"), nth("lat"))
            for t in range(TT):
                V_.tensor_scalar(CQ[:, t, :], CQ[:, t, :], RSL[:, t:t + 1], None, ALU.mult)
                ins = V_.tensor_scalar(CK[:, t, 0:P], CK[:, t, 0:P], RSL[:, 2 + t:3 + t], None, ALU.mult)
            ins.then_inc(S("normed"), 1)
            def silu_result(dst, i, sem, n):
                wait_result(dve, i)
                dve.wait_ge(S(sem), n)
                V_.tensor_tensor(dst, dst, bank_of(i)[:, :] if len(dst.shape) == 2 else tiles(i), ALU.mult)\
                  .then_inc(S("emptied_dve"), 1)

            dve.wait_ge(S("sig_c"), 1)
            dve.wait_ge(S("cc"), 1)
            V_.tensor_tensor(CC[:, :, 0:2], CC[:, :, 0:2], CSG, ALU.mult).then_inc(S("silu_c"), 1)
            dve.wait_ge(S("lat_ps"), 1)
            for c in range(2):
                V_.tensor_scalar(CQT[:, c, :], B[4][:, c * T:c * T + T], vec("mla_qa_norm", c), None, ALU.mult)
            V_.tensor_scalar(CKT, B[5][:, 0:T], vec("mla_kva_norm"), None, ALU.mult).then_inc(S("latT"), 1)
            for n, i in enumerate(of["uq"]):
                wait_result(dve, i)
                V_.tensor_copy(QKM[:, 0, :, 256 * n:256 * n + 256], tiles(i)).then_inc(S("emptied_dve"), 1)
            for n, i in enumerate(of["q"]):
                silu_result(QT[:, 2 * n:2 * n + 2, :].rearrange("p a t -> p (a t)"), i, "sig", n + 1)
            mean_sq("ctx", D)
            dve.wait_ge(S("rms"), nth("ctx"))
            for t in range(TT):
                ins = V_.tensor_scalar(HN[:, t, :], HN[:, t, :], rs["ctx"][:, t:t + 1], None, ALU.mult)
            ins.then_inc(S("normed"), 1)
            dve.wait_ge(S("lb"), 1)
            dve.wait_ge(S("emptied_act"), emptied[of["f"][-1]][1])
            for c in range(8):
                ins = V_.tensor_scalar(SF[:, c, :], SF[:, c, :], LBR[:, c:c + 1], LBF[:, c:c + 1], ALU.mult, ALU.add)
            link(ins)
            link(V_.tensor_scalar(KF[:, :, :], SF[:, :, :], -1.0, 1.0, ALU.mult, ALU.add))
            V_.tensor_scalar(SF[:, :, :], SF[:, :, :], F_FLOOR, None, ALU.max).then_inc(S("fgate"), 1)
            dve.wait_ge(S("sumsq"), nth("qk"))
            link(V_.tensor_reduce(SSH, SQ.rearrange("p s a d -> p (s a) d"), AX_X, ALU.add))
            V_.tensor_scalar(SSH, SSH, 1.0 / QK, EPS, ALU.mult, ALU.add).then_inc(S("mean_sq"), 1)
            dve.wait_ge(S("rms"), nth("qk"))
            dve.wait_ge(S("small_in"), SMALL)
            dve.wait_ge(S("sincos"), 1)
            norm_rope(V_, link, 0, M_TMP_Q).then_inc(S("normed"), 1)
            dve.wait_ge(S("normed"), nth("qk", NORMED))
            for n, i in enumerate(of["og"]):
                silu_result(OG[:, :, 256 * n:256 * n + 256], i, "sig", n + 3)
            dve.wait_ge(S("mod_sum"), 12)
            V_.tensor_tensor(MODT, B[7][:, 0:32].rearrange("p (a b) -> p a b", a=16),
                             over(vec("b_mod_2", 0, 16).unsqueeze(2), 16, 2), ALU.add)
            for u in range(2):
                bs = BGT[:, 512 * u:512 * u + 512]
                ins = V_.tensor_tensor(bs, bs, B[5 + u][:, :], ALU.add)
            ins.then_inc(S("mod_in"), 1)
            dve.wait_ge(S("mod_in"), 1)
            for s in range(2):
                ins = V_.tensor_scalar(ACOL[:, s, :], MODT[:, 8:16, s], 1.0, None, ALU.add)
            link(ins)
            for s in range(2):
                ins = V_.tensor_tensor(ACOL[:, s, :], ACOL[:, s, :], vec("pre_g_2", 0, 8), ALU.mult)
            link(ins)
            link(V_.tensor_tensor(PG[:], PG[:], BGT, ALU.mult))
            for h in range(1, MH, 2):
                dve.wait_ge(S("qkT_ps"), h + 1)
                V_.tensor_copy(QKT[0:QK, h, :], B[4 + h % 4][0:QK, :]).then_inc(S("qkT_odd"), 1)
            scale = QK ** -0.5

            def mla_max(h):
                dve.wait_ge(S("mla_s"), h + 1)
                link(V_.tensor_reduce(MX[:, h % 2, :], B[4 + h % 2][:, :].rearrange("p (t k) -> p t k", t=TT), AX_X, ALU.max))
                if h >= 2:
                    dve.wait_ge(S("mla_p"), 2 * (h - 1))
                V_.tensor_scalar(NMX[:, h % 2, :], MX[:, h % 2, :], -scale, None, ALU.mult).then_inc(S("mla_nmax"), 1)

            mla_max(0)
            for h in range(MH):
                if h + 1 < MH:
                    mla_max(h + 1)
                dve.wait_ge(S("mla_p"), 2 * h + 2)
                link(V_.reciprocal(RSM[:, h % 2, :], SUM[:, h % 2, :]))
                dve.wait_ge(S("mla_pv"), h + 1)
                V_.tensor_tensor(OM[:, :, h * VD:h * VD + VD], B[h % 2][:, 0:TT * VD].rearrange("p (t v) -> p t v", t=TT),
                                 over(RSM[:, h % 2, :].unsqueeze(2), TT, VD), ALU.mult).then_inc(S("mla_o"), 1)
            turned("ctx", "cT_dve", lambda k: ACOL[:, 1, k:k + 1], range(DK), lambda k: MODT[:, k, 1:2])
            dve.wait_ge(S("logf"), 1)
            for h in range(GH):
                V_.memset(BX[:, h, 0:1], 0.0)
                V_.tensor_tensor_scan(FC[:, h, :], const("ones"), SF[:, h, :], 0.0, ALU.mult, ALU.add)
                ins = V_.tensor_tensor_scan(BX[:, h, 1:T], const("ones")[:, 0:T - 1], SF[:, GH + h, 0:T - 1], 0.0,
                                            ALU.mult, ALU.add)
            ins.then_inc(S("cum"), 1)
            kfl = KF[:, 0:GH, :].rearrange("p h t -> p (h t)")
            kbl = KF[:, GH:2 * GH, :].rearrange("p h t -> p (h t)")
            qfl = QT.rearrange("p h t -> p (h t)")

            def gla_operands(n):
                lv = LEVELS[n]
                dq, dk = DEC[:, n % 2, 0], DEC[:, n % 2, 1]
                if lv == "diag":
                    dve.wait_ge(S("gla_s"), n - 1)
                    V_.tensor_tensor(dk, kfl, kbl, ALU.add).then_inc(S("gla_qk"), 1)
                    return
                dve.wait_ge(S("gla_exp"), n + 1)
                V_.tensor_tensor(dq, dq, qfl, ALU.mult)
                if isinstance(lv, int):
                    def halves(v):
                        v = v.rearrange("p (b two m) -> p b two m", two=2, m=lv)
                        return v[:, :, 0, :], v[:, :, 1, :]
                    (dl, dr), (kl, _), (_, kr) = halves(dk), halves(kfl), halves(kbl)
                    V_.tensor_tensor(dl, dl, kl, ALU.mult)
                    ins = V_.tensor_tensor(dr, dr, kr, ALU.mult)
                else:
                    ins = V_.tensor_tensor(dk, dk, kfl if lv == "base_fwd" else kbl, ALU.mult)
                ins.then_inc(S("gla_qk"), 1)

            def gla_scores(n):
                lv = LEVELS[n]
                dve.wait_ge(S("gla_s"), n + 1)
                if n:
                    dve.wait_ge(S("gla_a"), n)
                for st in range(TT):
                    bank = B[GLA_BANKS[n % 3] + st][:, :].rearrange("p (h t) -> p h t", h=GH)
                    if lv == 128:
                        ins = V_.tensor_copy(AXX[:, st], bank)
                    elif lv == 64:
                        ins = V_.tensor_copy(AD[:, st], bank)
                    else:
                        ins = V_.copy_predicated(AD[:, st], over(MSK[:, MASK_OF[lv]:MASK_OF[lv] + 1, :], GH, P), bank)
                ins.then_inc(S("gla_a"), 1)

            gla_operands(0)
            for n in range(len(LEVELS)):
                if n + 1 < len(LEVELS):
                    gla_operands(n + 1)
                gla_scores(n)
            dve.wait_ge(S("gla_o_ps"), 1)
            for tt in range(TT):
                ins = V_.tensor_copy(OO[:, tt], B[tt][:, :].rearrange("p (h v) -> p h v", h=GH))
            ins.then_inc(S("gla_o"), 1)
            dve.wait_ge(S("sumsq"), nth("o"))
            link(V_.tensor_reduce(SSO, OSQ, AX_X, ALU.add))
            V_.tensor_scalar(SSO, SSO, 1.0 / GK, EPS, ALU.mult, ALU.add).then_inc(S("mean_sq"), 1)
            dve.wait_ge(S("rms"), nth("o"))
            dve.wait_ge(S("small_in"), SMALL)
            oo = OO.rearrange("p t h v -> p (t h) v")
            link(V_.tensor_tensor(oo, oo, over(RSO.unsqueeze(2), 8, GK), ALU.mult))
            link(V_.tensor_tensor(oo, oo, over(ONB[:].unsqueeze(1), 8, GK), ALU.mult))
            oo2 = OO.rearrange("p t h v -> p (t h v)")
            V_.tensor_tensor(oo2, oo2, OG.rearrange("p t c -> p (t c)"), ALU.mult).then_inc(S("normed"), 1)
            def pair(base, n):
                return GATE[:, base + 2 * n:base + 2 * n + 2, :].rearrange("p a t -> p (a t)")
            dve.wait_ge(S("emptied_act"), emptied[of["gate"][-1]][1])
            for n, i in enumerate(of["yb"]):
                wait_result(dve, i)
                V_.tensor_tensor(pair(8, n), pair(8, n), bank_of(i)[:, :], ALU.mult).then_inc(S("emptied_dve"), 1)
            for n, i in enumerate(of["ya"]):
                wait_result(dve, i)
                V_.tensor_tensor(pair(0, n), pair(0, n), bank_of(i)[:, :], ALU.mult).then_inc(S("emptied_dve"), 1)
                dve.wait_ge(S("emptied_dve"), emptied[i][1])
                V_.tensor_tensor(pair(0, n), pair(0, n), pair(8, n), ALU.add).then_inc(S("merged"), 1)
            for n, i in enumerate(of["out"]):
                wait_result(dve, i)
                xs = X[:, :, 256 * n:256 * n + 256]
                V_.tensor_tensor(xs, xs, tiles(i), ALU.add).then_inc(S("emptied_dve"), 1)
            mean_sq("hm", D)
            dve.wait_ge(S("small_in"), SMALL)
            turned("hm", "rT_dve", lambda k: LNM[:, k:k + 1])
            dve.wait_ge(S("logits_ps"), 1)
            dve.wait_ge(S("small_in"), SMALL)
            dve.wait_ge(S("rms"), nth("hm"))
            for t in range(TT):
                ins = V_.scalar_tensor_tensor(out=LGT[:, t, :], in0=B[4][:, 72 * t:72 * t + 72], scalar=rs["hm"][:, t:t + 1],
                                              in1=RB[:], op0=ALU.mult, op1=ALU.add)
            link(ins)
            g = LGT[:, :, 0:8]
            rev = over(const("rev8").unsqueeze(1), TT, 8)

            def first_max(v, mx, onehot):
                link(V_.tensor_reduce(mx, v, AX_X, ALU.max))
                link(V_.tensor_tensor(VAL, v, over(mx.unsqueeze(2), TT, 8), ALU.is_equal))
                link(V_.tensor_tensor(VAL, VAL, rev, ALU.mult))
                link(V_.tensor_reduce(VMX, VAL, AX_X, ALU.max))
                return V_.tensor_tensor(onehot, VAL, over(VMX.unsqueeze(2), TT, 8), ALU.is_equal)

            first_max(g, GMX, GOH).then_inc(S("group"), 1)
            V_.tensor_tensor(GEXP, g, over(GMX.unsqueeze(2), TT, 8), ALU.subtract).then_inc(S("gdiff"), 1)
            dve.wait_ge(S("group"), 1)
            for t in range(TT):
                link(V_.tensor_tensor(GEX, LGT[:, t, 8:72].rearrange("p (g e) -> p g e", g=NG),
                                      over(GOH[:, t, :].unsqueeze(2), NG, EPG), ALU.mult))
                link(V_.tensor_reduce(EL[:, t, :], GEX.rearrange("p g e -> p e g"), AX_X, ALU.add))
            link(first_max(EL, M1, O1))
            link(V_.scalar_tensor_tensor(out=EL2, in0=O1, scalar=-1e30, in1=EL, op0=ALU.mult, op1=ALU.add))
            link(first_max(EL2, M2, O2))
            V_.tensor_tensor(DLT, M2, M1, ALU.subtract).then_inc(S("ediff"), 1)
            dve.wait_ge(S("gexp"), 1)
            link(V_.tensor_reduce(GSM, GEXP, AX_X, ALU.add))
            link(V_.reciprocal(PGR, GSM))
            dve.wait_ge(S("eexp"), 1)
            link(V_.tensor_scalar(DEN, E2W, 1.0, None, ALU.add))
            link(V_.reciprocal(W1, DEN))
            link(V_.tensor_tensor(W1, W1, PGR, ALU.mult))
            link(V_.tensor_tensor(W2, W1, E2W, ALU.mult))
            link(V_.tensor_tensor(O1, O1, over(W1.unsqueeze(2), TT, 8), ALU.mult))
            link(V_.tensor_tensor(O2, O2, over(W2.unsqueeze(2), TT, 8), ALU.mult))
            V_.tensor_tensor(WT, O1, O2, ALU.add)
            dve.wait_ge(S("rank_ps"), 1)
            V_.tensor_copy(RK, B[5][:, 0:16].rearrange("p (t g) -> p t g", t=TT))
            link(V_.tensor_copy(CNT, B[5][:, 16:24]))
            link(V_.tensor_scalar(NR, CNT, 0.5, None, ALU.is_gt))
            for lot in range(1, T // SLOT):
                link(V_.scalar_tensor_tensor(out=NR, in0=CNT, scalar=SLOT * lot + 0.5, in1=NR, op0=ALU.is_gt, op1=ALU.add))
            link(V_.tensor_scalar(NR[:, 0:1], NR[:, 0:1], 1.0, None, ALU.max))
            link(V_.tensor_tensor_scan(ENDS, const("ones")[:, 0:8], NR, 0.0, ALU.mult, ALU.add))
            link(V_.tensor_tensor(STA, ENDS, NR, ALU.subtract))
            link(V_.scalar_tensor_tensor(out=RK, in0=over(STA.unsqueeze(1), TT, 8), scalar=float(SLOT), in1=RK,
                                         op0=ALU.mult, op1=ALU.add))
            link(V_.tensor_tensor(RK, RK, GOH, ALU.mult))
            link(V_.tensor_reduce(POS, RK, AX_X, ALU.add))
            link(V_.tensor_tensor(TAB, over(ENDS.unsqueeze(1), ROUNDS, 8), over(const("round_id").unsqueeze(2), ROUNDS, 8),
                                  ALU.is_le))
            link(V_.tensor_reduce(TABR, TAB, AX_X, ALU.add))
            link(V_.tensor_scalar(TABR, TABR, float(NG - 1), None, ALU.min))
            V_.tensor_copy(RT[:, 1:1 + ROUNDS], TABR)
            V_.tensor_scalar(RT[:, 14:15], ENDS[:, 7:8], float(NM), float(-RING), ALU.mult, ALU.add)
            V_.tensor_copy(RT[:, 0:1], ENDS[:, 7:8]).then_inc(S("table"), 1)
            dve.wait_ge(S("table"), 1)

            def select():
                for t in range(TT):
                    ins = V_.tensor_scalar(SEL[:, t, :], const("iota_slot"), POS[:, t:t + 1], None, ALU.is_equal)
                ins.then_inc(S("sel"), 1)

            def moe_round(r):
                def at(n, k):
                    return r * n + k

                dve.wait_ge(S("sel"), at(1, 1))
                V_.tensor_scalar(POS, POS, float(SLOT), None, ALU.subtract).then_inc(S("pos_next"), 1)
                dve.wait_ge(S("gath_ps"), at(1, 1))
                V_.tensor_tensor(XG, B[0][:, :].rearrange("p (k s) -> p k s", k=DK), over(LNM[:].unsqueeze(2), DK, SLOT),
                                 ALU.mult).then_inc(S("gath"), 1)
                dve.wait_ge(S("sel_ps"), at(1, 1))
                for e in range(2):
                    rows = slice(e * SLOT, e * SLOT + SLOT)
                    ins = V_.tensor_copy(WPR[rows, :], B[1][rows, 0:EPG].rearrange("p (q e) -> p q e", e=2)[:, :, e])
                ins.then_inc(S("wpr"), 1)
                dve.wait_ge(S("wpr"), at(1, 1))
                for p in range(PAIRS):
                    bank = B[3 + p % 2]
                    dve.wait_ge(S("moe_sig"), at(PAIRS, p + 1))
                    V_.tensor_tensor(SGM[:, p % 2], SGM[:, p % 2], bank[:, 0:FE], ALU.mult).then_inc(S("moe_silu"), 1)
                    dve.wait_ge(S("moe_silu"), at(PAIRS, p + 1))
                    V_.scalar_tensor_tensor(out=HHR[:, p % 2], in0=bank[:, FE:2 * FE], scalar=WPR[:, p:p + 1],
                                            in1=SGM[:, p % 2], op0=ALU.mult, op1=ALU.mult).then_inc(S("hid"), 1)
                    if p == 0:
                        dve.wait_ge(S("str"), at(1, 1))
                        dve.wait_ge(S("pos_next"), at(1, 1))
                        select()
                dve.wait_ge(S("scat_ps"), at(1, 1))
                for t in range(TT):
                    for half in range(2):
                        xs = X[:, t, half * 512:half * 512 + 512]
                        ins = V_.tensor_tensor(xs, xs, B[2 * t + half][:, :], ALU.add)
                ins.then_inc(S("moe_x"), 1)
                dve.wait_ge(S("moe_x"), at(1, 1))

            select()
            moe_round(0)
            rounds = dve.value_load(RT[0:1, 0:1], min_val=4, max_val=ROUNDS)
            with dve.Fori(1, rounds) as r:
                moe_round(r)

            mean_sq("ple", D)
            turned("ple", "pleT_dve", lambda k: vec("ln_ple", k))
            for n, i in enumerate(of["ple"]):
                dve.wait_ge(S("emptied_act"), emptied[i][1])
                link(V_.tensor_tensor(SG[:, n % 2], SG[:, n % 2], PP[:, :, 256 * n:256 * n + 256], ALU.mult))
                xs = X[:, :, 256 * n:256 * n + 256]
                V_.tensor_tensor(xs, xs, SG[:, n % 2], ALU.add).then_inc(S("ple_x"), 1)
            dve.wait_ge(S("sumsq"), nth("two"))
            link(V_.tensor_reduce(ss["two"], SS2, AX_X, ALU.add))
            normalize(X, "two")
            turned("two", "twoT", lambda k: ACOL[:, 0, k:k + 1], range(DK), lambda k: MODT[:, k, 0:1])
            for n, i in enumerate(of["zb"]):
                silu_result(ZB[:, 2 * n:2 * n + 2, :].rearrange("p a t -> p (a t)"), i, "sig2", n + 1)
            V_.memset(UC[:, :, 0:1], 0.0)
            V_.memset(UC[:, :, T + 1:T + 2], 0.0)

            def two(tile, n):
                return tile[:, 2 * n:2 * n + 2, :].rearrange("p a t -> p (a t)")

            for n, i in enumerate(of["za"]):
                silu_result(two(YA, n), i, "sig2", n + 5)
            for n, i in enumerate(of["b"]):
                wait_result(dve, i)
                dve.wait_ge(S("emptied_dve"), emptied[of["za"][n]][1])
                V_.tensor_tensor(two(YA, n), two(YA, n), bank_of(i)[:, :], ALU.mult).then_inc(S("emptied_dve"), 1)
            for n, i in enumerate(of["xin"]):
                wait_result(dve, i)
                dve.wait_ge(S("emptied_act"), emptied[of["c"][n]][1])
                u = UC[:, 2 * n:2 * n + 2, 1:T + 1]
                V_.tensor_tensor(u, u, bank_of(i)[:, :].rearrange("p (a t) -> p a t", a=2), ALU.mult)\
                  .then_inc(S("emptied_dve"), 1)
            dve.wait_ge(S("emptied_dve"), emptied[of["xin"][-1]][1])

            def conv_chunk(k):
                cv = V2[:, k % 2, 0:T]
                link(V_.tensor_scalar(cv, UC[:, k, 0:T], vec("conv_w_2", k), vec("conv_b_2", k), ALU.mult, ALU.add))
                link(V_.scalar_tensor_tensor(out=cv, in0=UC[:, k, 1:T + 1], scalar=vec("conv_w_2", 8 + k), in1=cv,
                                             op0=ALU.mult, op1=ALU.add))
                link(V_.scalar_tensor_tensor(out=cv, in0=UC[:, k, 2:T + 2], scalar=vec("conv_w_2", 16 + k), in1=cv,
                                             op0=ALU.mult, op1=ALU.add))
                return V_.tensor_tensor(YA[:, k, :], YA[:, k, :], cv, ALU.mult)

            for m in range(8):
                conv_chunk(m).then_inc(S("conv"), 1)
                s = 1.0 if m >= 4 else HD ** -0.5
                dst = two(QT2 if m < 4 else KT2, m % 4)
                i = (of["q2"] + of["k2"])[m]
                dve.wait_ge(S("rot_ps"), m + 1)
                d3 = dst.rearrange("p (a t) -> p a t", a=2)
                V_.tensor_tensor(d3, B[4 + m % 2][:, :].rearrange("p (a t) -> p a t", a=2),
                                 over(const("sinT").unsqueeze(1), 2, T), ALU.mult)
                raw = RAW[:, m % 2, :].rearrange("p (a t) -> p a t", a=2)
                link(V_.tensor_tensor(RTM[:, m % 2, :].rearrange("p (a t) -> p a t", a=2), raw,
                                      over(const("cosT").unsqueeze(1), 2, T), ALU.mult))
                if m >= 4:
                    V_.tensor_tensor(dst, dst, RTM[:, m % 2, :], ALU.add).then_inc(S("roped"), 1)
                else:
                    link(V_.tensor_tensor(dst, dst, RTM[:, m % 2, :], ALU.add))
                    V_.tensor_scalar(dst, dst, s, None, ALU.mult).then_inc(S("roped"), 1)

            for n, i in enumerate(of["yconv"]):
                wait_result(dve, i)
                V_.tensor_tensor(two(GA, n), two(GA, n), bank_of(i)[:, :], ALU.mult).then_inc(S("emptied_dve"), 1)

            def na_max(n):
                dve.wait_ge(S("na_s"), n + 1)
                link(V_.tensor_reduce(MX2[:, n % 2:n % 2 + 1], B[2 + n % 3][:, :], AX_X, ALU.max))
                V_.tensor_scalar(NMX2[:, n % 2:n % 2 + 1], MX2[:, n % 2:n % 2 + 1], -1.0, None, ALU.mult)\
                  .then_inc(S("na_nmax"), 1)

            def na_out(c):
                dve.wait_ge(S("na_pv"), c + 1)
                V_.tensor_tensor(HT[:, c, :], B[c % 2][:, 0:T], ZB[:, c, :], ALU.mult).then_inc(S("na_o"), 1)

            na_max(0)
            na_max(1)
            for n in range(H2 * TT):
                dve.wait_ge(S("na_p"), n + 1)
                link(V_.reciprocal(RSM2[:, n % 2:n % 2 + 1], SUM2[:, n % 2:n % 2 + 1]))
                V_.tensor_scalar(PR2[:, n % 3, :], PR2[:, n % 3, :], RSM2[:, n % 2:n % 2 + 1], None, ALU.mult)\
                  .then_inc(S("na_pn"), 1)
                if n + 2 < H2 * TT:
                    na_max(n + 2)
                if n % 4 == 1 and n > 4:
                    na_out(n // 4 - 1)
            na_out(H2 // 2 - 1)
            for n, i in enumerate(of["yattn"]):
                wait_result(dve, i)
                V_.tensor_tensor(two(GB, n), two(GB, n), bank_of(i)[:, :], ALU.mult).then_inc(S("emptied_dve"), 1)
                dve.wait_ge(S("emptied_dve"), emptied[i][1])
                V_.tensor_tensor(two(GA, n), two(GA, n), two(GB, n), ALU.add).then_inc(S("merged2"), 1)
            for n, i in enumerate(of["wo"]):
                wait_result(dve, i)
                V_.tensor_tensor(YF[:, :, 256 * n:256 * n + 256], tiles(i),
                                 over(PG[:, 256 * n:256 * n + 256].unsqueeze(1), TT, 256), ALU.mult)\
                  .then_inc(S("emptied_dve"), 1)
            dve.wait_ge(S("sumsq"), nth("y"))
            link(V_.tensor_reduce(ss["y"], SSY, AX_X, ALU.add))
            mean_sq("y", D)
            dve.wait_ge(S("emptied_dve"), emptied[of["wo"][-1]][1])
            dve.wait_ge(S("rms"), nth("y"))
            for t in range(TT):
                V_.scalar_tensor_tensor(out=HN[:, t, :], in0=YF[:, t, :], scalar=rs["y"][:, t:t + 1], in1=X[:, t, :],
                                        op0=ALU.mult, op1=ALU.add).then_inc(S("final"), 1)


_NAMES = ["x", "p", "positions", "ln_mix", "w_in", "hg_lb", "hg_onorm", "w_oA", "mla_qa_norm", "mla_kva_norm", "w_uq",
          "w_ukv", "q_norm", "k_norm", "w_oB", "w_out", "ln_moe", "w_rg", "b_rg", "w_re", "b_re", "w1", "w3", "w2",
          "ln_ple", "w_ple_gate", "w_ple_proj", "c_2", "ctx_2", "c_ctx_2", "w_mod_2", "b_mod_2", "pre_g_2", "post_g_2",
          "w_in_2", "conv_w_2", "conv_b_2", "w_out_conv_2", "w_out_attn_2", "w_o_2"]


def kernel(**inputs):
    import concourse.bacc as bacc
    from concourse.bass_utils import run_bass_kernel_spmd

    nc = bacc.Bacc("TRN2", target_bir_lowering=False, num_devices=1)
    arrays = {n: np.ascontiguousarray(inputs[n]) for n in _NAMES}
    rpb = np.asarray(inputs["rpb_2"])[0]
    table = np.zeros((H2, ROWS, 2 * GW - 1, ROWS), rpb.dtype)
    for qr in range(ROWS):
        table[:, qr, GW - WIN:GW + WIN - 1, :] = rpb[:, 7 - qr:7 - qr + ROWS, :].transpose(0, 2, 1)
    arrays["toeplitz"] = table.reshape(-1)
    arrays["consts"], arrays["masks"] = constants()
    a, maps = {}, {}
    for n, v in arrays.items():
        maps["in_" + n] = v
        a[n] = nc.dram_tensor("in_" + n, v.shape, mybir.dt.from_np(v.dtype), kind="ExternalInput").ap()
    out = nc.dram_tensor("out", (1, T, D), F32, kind="ExternalOutput").ap()
    build(nc, a, out)
    r = run_bass_kernel_spmd(nc, [maps], core_ids=[0])
    return r.results[0]["out"]
```
